# Optimizing a Trainium2 kernel written in Bass

```python
import math
import jax, jax.numpy as jnp
from jax import lax
import numpy as np

D_MODEL = 1024
BATCH = 1
SEQ = 128
DEPTH = 2
DEC_BATCH = 1
DEC_SEQ = 256
PAST_LEN = 128

GRID_W = 64
N_MIXERS = 2
N_DIFF = (DEPTH + 1) // 2
N_MLA = DEPTH // 2
N_MOD = 9
D_FF = 2816
DIFF_HEADS = 8
DIFF_HD = 64
DIFF_VD = 2 * DIFF_HD
MLA_HEADS = 16
MLA_NOPE = 64
MLA_ROPE = 32
MLA_QK = MLA_NOPE + MLA_ROPE
MLA_VD = 64
Q_RANK = 768
KV_RANK = 256
ROPE_THETA = 10000.0
EPS = 1e-6
Q_BLOCK = 128
DIFF_SCALE = DIFF_HD ** -0.5
MLA_SCALE = MLA_QK ** -0.5

kernel_name = "diffmla_macaron_adaln_prefix_step"

def rms_norm(x, g):
    x32 = x.astype(jnp.float32)
    y = x32 * lax.rsqrt(jnp.mean(x32 * x32, axis=-1, keepdims=True) + EPS)
    return y.astype(x.dtype) * g

def grid_positions(n_tokens):
    rows = n_tokens // GRID_W
    row = jnp.repeat(jnp.arange(rows, dtype=jnp.int32), GRID_W)
    col = jnp.tile(jnp.arange(GRID_W, dtype=jnp.int32), rows)
    return row, col

def _rope_half(x, pos):
    n = x.shape[-1]
    freqs = ROPE_THETA ** (-jnp.arange(0, n, 2, dtype=jnp.float32) / n)
    ang = pos.astype(jnp.float32)[:, None] * freqs[None, :]
    shape = (1, pos.shape[0]) + (1,) * (x.ndim - 3) + (n // 2,)
    cos = jnp.cos(ang).reshape(shape).astype(x.dtype)
    sin = jnp.sin(ang).reshape(shape).astype(x.dtype)
    x1, x2 = x[..., : n // 2], x[..., n // 2:]
    return jnp.concatenate([x1 * cos - x2 * sin, x2 * cos + x1 * sin], axis=-1)

def rope_2d(x, row, col):
    r = x.shape[-1] // 2
    return jnp.concatenate([_rope_half(x[..., :r], row), _rope_half(x[..., r:], col)], axis=-1)

def rope_tail(x, row, col):
    return jnp.concatenate([x[..., :MLA_NOPE], rope_2d(x[..., MLA_NOPE:], row, col)], axis=-1)

def sweep_query_blocks(fn, *qs):
    B, L = qs[0].shape[:2]
    nb = L // Q_BLOCK
    blocks = tuple(jnp.moveaxis(q.reshape((B, nb, Q_BLOCK) + q.shape[2:]), 1, 0) for q in qs)
    out = lax.map(lambda qb: fn(*qb), blocks)
    return jnp.moveaxis(out, 0, 1).reshape((B, L) + out.shape[3:])

def softmax_f32(s, scale):
    return jax.nn.softmax(s.astype(jnp.float32) * scale, axis=-1)

def diff_attention(q, k, v, lam, scale):
    k1, k2 = k[..., 0, :], k[..., 1, :]

    def block(qb):
        a1 = softmax_f32(jnp.einsum('bqhd,bkhd->bhqk', qb[..., 0, :], k1), scale)
        a2 = softmax_f32(jnp.einsum('bqhd,bkhd->bhqk', qb[..., 1, :], k2), scale)
        a = a1 - lam * a2
        return jnp.einsum('bhqk,bkhv->bqhv', a.astype(v.dtype), v)

    return sweep_query_blocks(block, q)

def mha(q, k, v, scale):
    def block(qb):
        a = softmax_f32(jnp.einsum('bqhd,bkhd->bhqk', qb, k), scale)
        return jnp.einsum('bhqk,bkhv->bqhv', a.astype(v.dtype), v)

    return sweep_query_blocks(block, q)

def diff_qkv(h, w_qkv, q_g, k_g):
    B, L, _ = h.shape
    q, k, v = jnp.split(h @ w_qkv, 3, axis=-1)
    q = rms_norm(q.reshape(B, L, DIFF_HEADS, 2, DIFF_HD), q_g)
    k = rms_norm(k.reshape(B, L, DIFF_HEADS, 2, DIFF_HD), k_g)
    v = v.reshape(B, L, DIFF_HEADS, DIFF_VD)
    return q, k, v

def lambda_value(lam_p, layer_idx):
    lam_init = 0.8 - 0.6 * math.exp(-0.3 * layer_idx)
    lp = lam_p.astype(jnp.float32)
    lam = jnp.exp(jnp.sum(lp[0] * lp[1])) - jnp.exp(jnp.sum(lp[2] * lp[3])) + lam_init
    return lam, lam_init

def diff_out(o, lam_init, subln_g, w_o):
    B, L = o.shape[:2]
    o = rms_norm(o, subln_g) * (1.0 - lam_init)
    return o.reshape(B, L, DIFF_HEADS * DIFF_VD) @ w_o

def mla_down(h, w_down, qa_g, kva_g):
    cq, ckv, kpe = jnp.split(h @ w_down, [Q_RANK, Q_RANK + KV_RANK], axis=-1)
    return rms_norm(cq, qa_g), rms_norm(ckv, kva_g), kpe

def mla_queries(cq, w_q_up, q_g):
    B, L = cq.shape[:2]
    return rms_norm((cq @ w_q_up).reshape(B, L, MLA_HEADS, MLA_QK), q_g)

def mla_keys_values(ckv, kpe, w_kv_up, k_g):
    B, L = ckv.shape[:2]
    kv = (ckv @ w_kv_up).reshape(B, L, MLA_HEADS, MLA_NOPE + MLA_VD)
    k_nope, v = kv[..., :MLA_NOPE], kv[..., MLA_NOPE:]
    k_pe = jnp.broadcast_to(kpe[:, :, None, :], (B, L, MLA_HEADS, MLA_ROPE))
    k = rms_norm(jnp.concatenate([k_nope, k_pe], axis=-1), k_g)
    return k, v

def mla_out(o, w_o):
    B, L = o.shape[:2]
    return o.reshape(B, L, MLA_HEADS * MLA_VD) @ w_o

def modulation(cond, w_mod, b_mod):
    m = jax.nn.silu(cond) @ w_mod + b_mod
    return m.reshape(cond.shape[0], 1, N_MOD, D_MODEL)

def modulate(x, g, shift, scale):
    return rms_norm(x, g) * (1.0 + scale) + shift

def swiglu(h, w_in, w_out):
    g, u = jnp.split(h @ w_in, 2, axis=-1)
    return (jax.nn.silu(g) * u) @ w_out

def macaron_layer(x, mod, norm_g, w_in, w_out, mixer):
    m = [mod[:, :, i] for i in range(N_MOD)]
    x = x + m[2] * (0.5 * swiglu(modulate(x, norm_g[0], m[0], m[1]), w_in[0], w_out[0]))
    out, aux = mixer(modulate(x, norm_g[1], m[3], m[4]))
    x = x + m[5] * out
    x = x + m[8] * (0.5 * swiglu(modulate(x, norm_g[2], m[6], m[7]), w_in[1], w_out[1]))
    return x, aux

def setup_inputs(seed: int = 0) -> dict:
    key = jax.random.key(seed)
    ks = jax.random.split(key, 27)
    f32 = jnp.float32
    D = D_MODEL

    def nrm(k, shape, s):
        return jax.random.normal(k, shape, f32) * s

    def gain(k, shape):
        return 1.0 + 0.02 * jax.random.normal(k, shape, f32)

    return {
        "x_prompt": nrm(ks[0], (BATCH, SEQ, D), 1.0),
        "x_sample": nrm(ks[1], (DEC_BATCH, DEC_SEQ, D), 1.0),
        "c": nrm(ks[2], (DEC_BATCH, D), 1.0),
        "cache_diff_k": nrm(ks[3], (DEC_BATCH, N_DIFF, PAST_LEN, DIFF_HEADS, 2, DIFF_HD), 1.0),
        "cache_diff_v": nrm(ks[4], (DEC_BATCH, N_DIFF, PAST_LEN, DIFF_HEADS, DIFF_VD), 1.0),
        "cache_mla_ckv": nrm(ks[5], (DEC_BATCH, N_MLA, PAST_LEN, KV_RANK), 1.0),
        "cache_mla_kpe": nrm(ks[6], (DEC_BATCH, N_MLA, PAST_LEN, MLA_ROPE), 1.0),
        "c_ctx": nrm(ks[7], (D,), 1.0),
        "w_mod": nrm(ks[8], (DEPTH, D, N_MOD * D), 0.5 * D ** -0.5),
        "b_mod": nrm(ks[9], (DEPTH, N_MOD * D), 0.02),
        "norm_g": gain(ks[10], (DEPTH, 3, D)),
        "ffn_w_in": nrm(ks[11], (DEPTH, 2, D, 2 * D_FF), D ** -0.5),
        "ffn_w_out": nrm(ks[12], (DEPTH, 2, D_FF, D), D_FF ** -0.5),
        "diff_w_qkv": nrm(ks[13], (N_DIFF, D, 3 * DIFF_HEADS * DIFF_VD), D ** -0.5),
        "diff_q_norm": gain(ks[14], (N_DIFF, DIFF_HD)),
        "diff_k_norm": gain(ks[15], (N_DIFF, DIFF_HD)),
        "diff_lambda": nrm(ks[16], (N_DIFF, 4, DIFF_HD), 0.1),
        "diff_subln": gain(ks[17], (N_DIFF, DIFF_VD)),
        "diff_w_o": nrm(ks[18], (N_DIFF, DIFF_HEADS * DIFF_VD, D), (DIFF_HEADS * DIFF_VD) ** -0.5),
        "mla_w_down": nrm(ks[19], (N_MLA, D, Q_RANK + KV_RANK + MLA_ROPE), D ** -0.5),
        "mla_q_a_norm": gain(ks[20], (N_MLA, Q_RANK)),
        "mla_kv_a_norm": gain(ks[21], (N_MLA, KV_RANK)),
        "mla_w_q_up": nrm(ks[22], (N_MLA, Q_RANK, MLA_HEADS * MLA_QK), Q_RANK ** -0.5),
        "mla_w_kv_up": nrm(ks[23], (N_MLA, KV_RANK, MLA_HEADS * (MLA_NOPE + MLA_VD)), KV_RANK ** -0.5),
        "mla_q_norm": gain(ks[24], (N_MLA, MLA_QK)),
        "mla_k_norm": gain(ks[25], (N_MLA, MLA_QK)),
        "mla_w_o": nrm(ks[26], (N_MLA, MLA_HEADS * MLA_VD, D), (MLA_HEADS * MLA_VD) ** -0.5),
    }

def reference(x_prompt, x_sample, c, cache_diff_k, cache_diff_v, cache_mla_ckv, cache_mla_kpe, c_ctx,
              w_mod, b_mod, norm_g, ffn_w_in, ffn_w_out,
              diff_w_qkv, diff_q_norm, diff_k_norm, diff_lambda, diff_subln, diff_w_o,
              mla_w_down, mla_q_a_norm, mla_kv_a_norm, mla_w_q_up, mla_w_kv_up, mla_q_norm, mla_k_norm, mla_w_o):
    row, col = grid_positions(x_sample.shape[1])
    xp, xs = x_prompt, x_sample
    new_diff_k, new_diff_v, new_mla_ckv, new_mla_kpe = [], [], [], []
    for l in range(DEPTH):
        j = l // N_MIXERS
        mod_ctx = modulation(c_ctx[None, :], w_mod[l], b_mod[l])
        mod_lat = modulation(c, w_mod[l], b_mod[l])
        if l % N_MIXERS == 0:
            w_qkv, qg, kg = diff_w_qkv[j], diff_q_norm[j], diff_k_norm[j]
            sub_g, w_o = diff_subln[j], diff_w_o[j]
            lam, lam_init = lambda_value(diff_lambda[j], l)

            def ctx_mixer(h):
                q, k, v = diff_qkv(h, w_qkv, qg, kg)
                o = diff_attention(q, k, v, lam, DIFF_SCALE)
                return diff_out(o, lam_init, sub_g, w_o), (k, v)

            def lat_mixer(h):
                q, k, v = diff_qkv(h, w_qkv, qg, kg)
                q, k = rope_2d(q, row, col), rope_2d(k, row, col)
                k_all = jnp.concatenate([cache_diff_k[:, j], k], axis=1)
                v_all = jnp.concatenate([cache_diff_v[:, j], v], axis=1)
                o = diff_attention(q, k_all, v_all, lam, DIFF_SCALE)
                return diff_out(o, lam_init, sub_g, w_o), ()

            xp, (k_ctx, v_ctx) = macaron_layer(xp, mod_ctx, norm_g[l], ffn_w_in[l], ffn_w_out[l], ctx_mixer)
            new_diff_k.append(k_ctx)
            new_diff_v.append(v_ctx)
        else:
            w_down, qag, kvag = mla_w_down[j], mla_q_a_norm[j], mla_kv_a_norm[j]
            w_q_up, w_kv_up, qg, kg, w_o = mla_w_q_up[j], mla_w_kv_up[j], mla_q_norm[j], mla_k_norm[j], mla_w_o[j]

            def ctx_mixer(h):
                cq, ckv, kpe = mla_down(h, w_down, qag, kvag)
                q = mla_queries(cq, w_q_up, qg)
                k, v = mla_keys_values(ckv, kpe, w_kv_up, kg)
                return mla_out(mha(q, k, v, MLA_SCALE), w_o), (ckv, kpe)

            def lat_mixer(h):
                cq, ckv, kpe = mla_down(h, w_down, qag, kvag)
                q = rope_tail(mla_queries(cq, w_q_up, qg), row, col)
                k_lat, v_lat = mla_keys_values(ckv, kpe, w_kv_up, kg)
                k_lat = rope_tail(k_lat, row, col)
                k_ctx, v_ctx = mla_keys_values(cache_mla_ckv[:, j], cache_mla_kpe[:, j], w_kv_up, kg)
                k_all = jnp.concatenate([k_ctx, k_lat], axis=1)
                v_all = jnp.concatenate([v_ctx, v_lat], axis=1)
                return mla_out(mha(q, k_all, v_all, MLA_SCALE), w_o), ()

            xp, (ckv_ctx, kpe_ctx) = macaron_layer(xp, mod_ctx, norm_g[l], ffn_w_in[l], ffn_w_out[l], ctx_mixer)
            new_mla_ckv.append(ckv_ctx)
            new_mla_kpe.append(kpe_ctx)
        xs, _ = macaron_layer(xs, mod_lat, norm_g[l], ffn_w_in[l], ffn_w_out[l], lat_mixer)
    return (xp, xs, jnp.stack(new_diff_k, axis=1), jnp.stack(new_diff_v, axis=1),
            jnp.stack(new_mla_ckv, axis=1), jnp.stack(new_mla_kpe, axis=1))


_drawn_inputs = setup_inputs


def setup_inputs(seed=0):
    import zlib

    import numpy as np

    out = dict(_drawn_inputs(seed))
    spreads = {}
    factors = {'cache_mla_ckv': 3.499,
     'cache_mla_kpe': 6.855,
     'norm_g': 2.724,
     'diff_q_norm': 8.0,
     'diff_k_norm': 3.027,
     'diff_lambda': 4.175,
     'diff_subln': 8.0,
     'mla_q_a_norm': 8.0,
     'mla_kv_a_norm': 2.916,
     'mla_q_norm': 8.0,
     'mla_k_norm': 8.0,
     'cache_diff_k': 8.0,
     'cache_diff_v': 8.0}
    for name, (base, spread) in spreads.items():
        noise = np.random.default_rng([zlib.crc32(name.encode()), seed]).standard_normal(out[name].shape)
        drawn = base * np.exp(spread * noise) if base else spread * noise
        out[name] = __import__('jax').numpy.asarray(drawn.astype(out[name].dtype))
    for name, factor in factors.items():
        out[name] = (out[name] * factor).astype(out[name].dtype)
    return out
```

```python
import math
from contextlib import ExitStack

import concourse.bass as bass
from concourse import mybir
import numpy as np

F32 = mybir.dt.float32
F32R = mybir.dt.float32r
ALU = mybir.AluOpType
ACT = mybir.ActivationFunctionType
AX = mybir.AxisListType

D = 1024
FF = 2816
P = 128
KD = D // P
KF = FF // P
T = 384
LAT = slice(0, 256)
CTX = slice(256, 384)
SEGS = ((0, CTX), (1, LAT))
NB = T // P
EPS = 1e-6
DEPTH = 2
DIFF_HEADS, DIFF_HD, DIFF_VD = 8, 64, 128
MLA_HEADS, NOPE, ROPE, MLA_VD = 16, 64, 32, 64
QK = NOPE + ROPE
Q_RANK, KV_RANK = 768, 256
DIFF_SCALE = DIFF_HD ** -0.5
MLA_SCALE = QK ** -0.5
LAM_INIT = 0.8 - 0.6 * math.exp(-0.3 * 0)
ROW = 512

_ORDER = [("in", 0, KF, 16 * P), ("out", 0, 2 * KD, 11 * P), ("qkv", 0, 12, 4 * ROW), ("wo", 0, 4, 16 * P),
          ("in", 1, KF, 16 * P), ("out", 1, 2 * KD, 11 * P), ("in", 2, KF, 16 * P), ("out", 2, 2 * KD, 11 * P),
          ("down", 0, 4, 4 * ROW), ("qup", 0, 8, 3 * T), ("kvup", 0, 2, 4 * ROW), ("wo", 1, 4, 16 * P),
          ("in", 3, KF, 16 * P), ("out", 3, 2 * KD, 11 * P)]
PHASE = {}
_n = 0
for _name, _i, _count, _width in _ORDER:
    PHASE[_name, _i] = (_n, _count, _width)
    _n += _count
PANELS = _n
START = 2

PAIRS = DEPTH * 9 * 2
FIRST_PAIRS = 4
PAIR_BASE = {("in", 0): 4, ("out", 0): 15, ("wo", 0): 19, ("in", 1): 21, ("out", 1): 32}


def build_step(nc, d, o):
    ctx = ExitStack()
    with ctx:
        def sem(name):
            return ctx.enter_context(nc.semaphore(name))

        def sb(name, shape, dt=F32, where=ctx):
            return where.enter_context(nc.sbuf_tensor(name, shape, dt))

        x = sb("x", [P, KD, T])
        h_hi = sb("h_hi", [P, KD, T], F32R)
        h_lo = sb("h_lo", [P, KD, T], F32R)
        w_raw = sb("w_raw", [P, 2, 16 * P])
        w_hi = sb("w_hi", [P, 2, 16 * P], F32R)
        w_lo = sb("w_lo", [P, 2, 16 * P], F32R)
        hf = sb("hf", [P, 2, T])
        sqt = sb("sqt", [P, T])
        sqacc = sb("sqacc", [P, T])
        diag = sb("diag", [P, NB, P])
        mrow = sb("mrow", [P, ROW])
        modc = sb("modc", [P, DEPTH * 72, 2])
        bmod = sb("bmod", [P, DEPTH * 72, 2])
        norm_g = sb("norm_g", [P, 6, KD, 2])
        gmul = sb("gmul", [P, KD, 2])
        gres = sb("gres", [P, KD, 2])
        cond = sb("cond", [P, KD, 2])
        scond = sb("scond", [P, KD, 32])
        ones = sb("ones", [P, P])
        ident = sb("ident", [P, P])
        sel = sb("sel", [P, 2])
        epsc = sb("epsc", [P, 1])
        nhalf = sb("nhalf", [P, 8])
        var = sb("var", [P, 8])
        rstd = sb("rstd", [P, 8])
        ssq = sb("ssq", [P, 32])
        rms = sb("rms", [P, 32])
        rinv = sb("rinv", [P, 32])
        mx = sb("mx", [P, 2, 2])
        nm = sb("nm", [P, 2, 2])
        rs = sb("rs", [P, 2, 2])
        ri = sb("ri", [P, 2, 2])
        ri2 = sb("ri2", [P, 2])
        ropes = sb("ropes", [P, 2, 2, 64 + ROPE])
        gq = sb("gq", [P, 2, DIFF_HD])
        gm = sb("gm", [P, 2, QK])
        subg = sb("subg", [P, 2])
        gdown = sb("gdown", [P, KD])
        lamp = sb("lamp", [P, 4, DIFF_HD])
        lamt = sb("lamt", [P, 2, DIFF_HD])
        lams = sb("lams", [P, 2])
        lame = sb("lame", [P, 2])
        neglam = sb("neglam", [P, 2])
        kpw = sb("kpw", [P, KD, ROPE])
        kpw_hi = sb("kpw_hi", [P, KD, ROPE], F32R)
        kpw_lo = sb("kpw_lo", [P, KD, ROPE], F32R)
        t1 = sb("t1", [P, 8, 64])
        t2 = sb("t2", [P, 8, 64])

        early = ExitStack()
        wm = sb("wm", [P, 2, 4 * ROW], where=early)
        with ExitStack() as part:
            wm_first = sb("wm_first", [P, 2 * FIRST_PAIRS, 4 * ROW], where=part)
        with ExitStack() as part:
            g_hi = sb("g_hi", [P, KF, T], F32R, part)
            g_lo = sb("g_lo", [P, KF, T], F32R, part)
            sg = sb("sg", [P, 2, T], where=part)
            prod = sb("prod", [P, 2, T], where=part)
        with ExitStack() as part:
            v_all = sb("v_all", [P, 4, D], where=part)
            dqT = sb("dqT", [P, DIFF_HEADS, T], where=part)
            dkT = sb("dkT", [P, DIFF_HEADS, 4 * P], where=part)
            with ExitStack() as part2:
                qn = sb("qn", [P, NB, D], where=part2)
                kn = sb("kn", [P, 4, D], where=part2)
                sq3 = sb("sq3", [P, NB, ROW], where=part2)
            with ExitStack() as part2:
                e = sb("e", [P, 2, 2, T], where=part2)
                a2 = sb("a2", [P, T], where=part2)
                a = sb("a", [P, 2, T], where=part2)
                aT = sb("aT", [P, 2, T], where=part2)
                oraw = sb("oraw", [P, 2, NB, DIFF_VD], where=part2)
                onrm = sb("onrm", [P, 2, NB, DIFF_VD], where=part2)
                osq = sb("osq", [P, DIFF_VD], where=part2)
                oss = sb("oss", [P, 2, NB], where=part2)
                ovar = sb("ovar", [P, 2, NB], where=part2)
                orin = sb("orin", [P, 2, NB], where=part2)
                otf = sb("otf", [P, 2, T], where=part2)
        early.close()
        with ExitStack() as part:
            mv_all = sb("mv_all", [P, 4, D], where=part)
            mqT = sb("mqT", [QK, MLA_HEADS, T], where=part)
            kpe = sb("kpe", [P, 4, ROPE], where=part)
            kpg = sb("kpg", [P, 4, ROPE], where=part)
            kps = sb("kps", [P, 4, ROPE], where=part)
            kpss = sb("kpss", [P, 4], where=part)
            cck = sb("cck", [P, 2, P], where=part)
            cck_hi = sb("cck_hi", [P, 2, P], F32R, part)
            cck_lo = sb("cck_lo", [P, 2, P], F32R, part)
            dss = sb("dss", [P, NB, 3], where=part)
            dtot = sb("dtot", [P, NB], where=part)
            dvar = sb("dvar", [P, 2, NB], where=part)
            drms = sb("drms", [P, 2, NB], where=part)
            drin = sb("drin", [P, 2, NB], where=part)
            with ExitStack() as part2:
                mqn = sb("mqn", [P, NB, MLA_HEADS * QK], where=part2)
                cn = sb("cn", [P, NB, D], where=part2)
                msq3 = sb("msq3", [P, NB, ROW], where=part2)
                ckvf = sb("ckvf", [P, 2, T], where=part2)
            with ExitStack() as part2:
                mkT = sb("mkT", [QK, MLA_HEADS, 4 * P], where=part2)
                with ExitStack() as part3:
                    mkn = sb("mkn", [P, 4, 8, QK], where=part3)
                    msq4 = sb("msq4", [P, 4, ROW], where=part3)
                with ExitStack() as part3:
                    me = sb("me", [P, 2, T], where=part3)
                    ma = sb("ma", [P, 2, T], where=part3)
                    maT = sb("maT", [P, 2, T], where=part3)

        ps = ctx.enter_context(nc.psum_tensor("ps", [P, 8, ROW], F32))

        small_in = sem("small_in")
        x_in = sem("x_in")
        params_in = sem("params_in")
        diff_in = sem("diff_in")
        mla_in = sem("mla_in")
        out_done = sem("out_done")
        y_done = sem("y_done")
        w_loaded = [sem(f"w_loaded{i}") for i in range(2)]
        w_hi_done = sem("w_hi_done")
        w_lo_done = sem("w_lo_done")
        panel_used = sem("panel_used")
        wmf_loaded = [sem(f"wmf_loaded{i}") for i in range(2 * FIRST_PAIRS)]
        wm_loaded = [sem(f"wm_loaded{i}") for i in range(2)]
        pool_consts = sem("pool_consts")
        dve_consts = sem("dve_consts")
        out_ready = sem("out_ready")
        scond_ready = sem("scond_ready")
        rows_ready = sem("rows_ready")
        rows_copied = sem("rows_copied")
        cols_ready = sem("cols_ready")
        cols_done = sem("cols_done")
        res_step = sem("res_step")
        ss_ready = sem("ss_ready")
        var_ready = sem("var_ready")
        rstd_ready = sem("rstd_ready")
        diag_ready = sem("diag_ready")
        bc_ready = sem("bc_ready")
        h_tmp = sem("h_tmp")
        h_aff = sem("h_aff")
        h_hi_done = sem("h_hi_done")
        h_lo_done = sem("h_lo_done")
        gains = sem("gains")
        gate_ready = sem("gate_ready")
        silu_done = sem("silu_done")
        prod_ready = sem("prod_ready")
        g_hi_done = sem("g_hi_done")
        g_ready = sem("g_ready")
        lam_step = sem("lam_step")
        lam_exp = sem("lam_exp")
        dve = sem("dve")
        proj_free = sem("proj_free")
        sq_done = sem("sq_done")
        red_done = sem("red_done")
        rms_done = sem("rms_done")
        heads_ready = sem("heads_ready")
        v_done = sem("v_done")
        tr_ready = sem("tr_ready")
        tr_act = sem("tr_act")
        tr_dve = sem("tr_dve")
        s_ready = sem("s_ready")
        nm_ready = sem("nm_ready")
        exp_done = sem("exp_done")
        a_done = sem("a_done")
        t_ready = sem("t_ready")
        at_done = sem("at_done")
        pv_ready = sem("pv_ready")
        o_done = sem("o_done")
        on_done = sem("on_done")
        oT_ready = sem("oT_ready")
        oT_f = sem("oT_f")
        oT_hi = sem("oT_hi")
        oT_lo = sem("oT_lo")
        ovar_ready = sem("ovar_ready")
        orin_ready = sem("orin_ready")
        kpw_done = sem("kpw_done")
        dss_done = sem("dss_done")
        dvar_ready = sem("dvar_ready")
        kpe_prod = sem("kpe_prod")
        mproj_free = sem("mproj_free")
        kv_keys = sem("kv_keys")
        mkheads = sem("mkheads")
        cn_done = sem("cn_done")
        cT_ready = sem("cT_ready")
        cT_f = sem("cT_f")
        cT_hi = sem("cT_hi")
        cT_lo = sem("cT_lo")
        kpe_ready = sem("kpe_ready")
        cck_step = sem("cck_step")
        msq_done = sem("msq_done")
        mred_done = sem("mred_done")
        mrms_done = sem("mrms_done")
        mheads = sem("mheads")
        kbank_free = sem("kbank_free")
        mv_done = sem("mv_done")
        mtr_ready = sem("mtr_ready")
        mtr_act = sem("mtr_act")
        mtr_dve = sem("mtr_dve")
        ms_ready = sem("ms_ready")
        mnm_ready = sem("mnm_ready")
        mexp_done = sem("mexp_done")
        ma_done = sem("ma_done")
        mt_ready = sem("mt_ready")
        mat_done = sem("mat_done")
        mpv_ready = sem("mpv_ready")
        mo_hi = sem("mo_hi")
        mo_lo = sem("mo_lo")

        def src_of(name, i):
            arr = d[{"in": "w_in", "out": "w_out", "qkv": "w_qkv", "wo": "w_o", "down": "w_down",
                     "qup": "w_qup", "kvup": "w_kvup"}[name]]
            return arr[i] if name in ("in", "out", "wo") else arr

        norms = [("in", 0), ("qkv", 0), ("in", 1), ("in", 2), ("down", 0), ("in", 3)]
        ffns = [("in", i) for i in range(4)]
        residuals = [("out", 0), ("wo", 0), ("out", 1), ("out", 2), ("wo", 1), ("out", 3)]
        RES_BASE = {ph: KD * (n + 1) for n, ph in enumerate(residuals)}

        def mdst(t):
            if t < 12:
                return mqT[:, 4 * (t // 3):4 * (t // 3) + 4, (t % 3) * P:(t % 3 + 1) * P]
            g, slot = divmod(t - 12, 4)
            return mkT[:, 4 * g:4 * g + 4, slot * P:(slot + 1) * P]

        def ddst(t):
            if t < 6:
                return dqT[:, 4 * (t // 3):4 * (t // 3) + 4, (t % 3) * P:(t % 3 + 1) * P]
            g, slot = divmod(t - 6, 4)
            return dkT[:, 4 * g:4 * g + 4, slot * P:(slot + 1) * P]

        TURNS = []
        for u in range(3 * DIFF_HEADS + 3):
            if u < 3 * DIFF_HEADS:
                TURNS.append(("weights", u))
            if u >= 5 and u % 3 == 2:
                TURNS.append(("outputs", u // 3 - 1))
        TURN_BANK = {item: 4 + n % 2 for n, item in enumerate(TURNS)}

        def turn_free(eng, item):
            n = TURNS.index(item)
            if n >= 2:
                kind, i = TURNS[n - 2]
                eng.wait_ge(at_done if kind == "weights" else oT_f, i + 1)

        def h_val(n, k):
            return START + KD * n + k + 1

        block = ctx.enter_context(nc.Block())

        @block.sync
        def _(sp):
            def load(name, i, slot, at, n, guarded=True):
                base, count, width = PHASE[name, i]
                if guarded:
                    sp.wait_ge(w_hi_done, n - 1)
                    sp.wait_ge(w_lo_done, n - 1)
                sp.dma_start(w_raw[:, slot, 0:width], src_of(name, i)[at]).then_inc(w_loaded[slot], 16)

            def load_mod(j, guarded=True):
                if guarded:
                    sp.wait_ge(rows_ready, j)
                for kh in range(2):
                    sp.dma_start(wm[:, kh, :], d["w_mod"][2 * j + kh]).then_inc(wm_loaded[kh], 16)

            for j in range(2 * FIRST_PAIRS):
                sp.dma_start(wm_first[:, j, :], d["w_mod"][j]).then_inc(wmf_loaded[j], 16)
            for name, i, count, width in _ORDER:
                base = PHASE[name, i][0]
                per = 4 if name == "out" else 2
                mod = PAIR_BASE.get((name, i))
                first = 0
                if base == 0:
                    for s in range(2):
                        load(name, i, s, s, s, guarded=False)
                    load_mod(FIRST_PAIRS, guarded=False)
                    first = 1
                with sp.Fori(first, count // per) as it:
                    for s in range(per):
                        load(name, i, s % 2, it * per + s, base + it * per + s)
                    if mod is not None:
                        load_mod(mod + it)
            for k in range(0, KD, 2):
                sp.wait_ge(res_step, 4 * (START + RES_BASE["out", 3] + k + 2))
                sp.dma_start(o["yT"][k:k + 2].rearrange("k p t -> p k t"), x[:, k:k + 2, :]).then_inc(y_done, 16)
            sp.wait_ge(y_done, 16 * (KD // 2))

        @block.gpsimd
        def _(pool):
            nc.gpsimd.memset(ident[:], 0.0).then_inc(pool_consts, 1)
            nc.gpsimd.memset(ones[:], 1.0).then_inc(pool_consts, 1)
            pool.wait_ge(pool_consts, 2)
            nc.gpsimd.affine_select(out=ident[:], in_=ident[:], compare_op=ALU.not_equal, fill=1.0, base=0,
                                    pattern=[[-1, P]], channel_multiplier=1).then_inc(pool_consts, 1)

            def low(n, slot, width):
                pool.wait_ge(w_hi_done, n + 1)
                nc.gpsimd.tensor_tensor(w_lo[:, slot, 0:width], w_raw[:, slot, 0:width],
                                        w_hi[:, slot, 0:width].bitcast(F32), ALU.subtract).then_inc(w_lo_done, 1)

            def norm(n):
                pool.wait_ge(var_ready, n + 1)
                nc.gpsimd.tensor_tensor(rstd[:, 0:NB], var[:, 0:NB], nhalf[:, 0:NB], ALU.pow).then_inc(rstd_ready, 1)
                with pool.Fori(0, KD // 2) as i:
                    for b in range(2):
                        pool.wait_ge(h_hi_done, i * 2 + (KD * n + b + 1))
                        nc.gpsimd.tensor_tensor(h_lo[:, i * 2 + b, :], hf[:, b, :],
                                                h_hi[:, i * 2 + b, :].bitcast(F32),
                                                ALU.subtract).then_inc(h_lo_done, 1)

            def lows(name, i, frm=1):
                base, count, width = PHASE[name, i]
                if frm == 2:
                    pass
                else:
                    low(base + 1, 1, width)
                with pool.Fori(1, count // 2) as it:
                    for s in range(2):
                        low(base + it * 2 + s, s, width)

            def next_low(name, i):
                base, count, width = PHASE[name, i]
                low(base, 0, width)

            low(0, 0, PHASE["in", 0][2])
            norm(0)
            lows("in", 0)
            next_low("out", 0)
            lows("out", 0)
            next_low("qkv", 0)
            norm(1)
            lows("qkv", 0)
            next_low("wo", 0)
            low(PHASE["wo", 0][0] + 1, 1, PHASE["wo", 0][2])
            for h in range(DIFF_HEADS):
                pool.wait_ge(ovar_ready, h + 1)
                nc.gpsimd.tensor_tensor(orin[:, h % 2, :], ovar[:, h % 2, :], nhalf[:, 0:NB],
                                        ALU.pow).then_inc(orin_ready, 1)
                pool.wait_ge(oT_hi, h + 1)
                nc.gpsimd.tensor_tensor(h_lo[:, h, :], otf[:, h % 2, :], h_hi[:, h, :].bitcast(F32),
                                        ALU.subtract).then_inc(oT_lo, 1)
            lows("wo", 0, frm=2)
            next_low("in", 1)
            norm(2)
            lows("in", 1)
            next_low("out", 1)
            lows("out", 1)
            next_low("in", 2)
            norm(3)
            lows("in", 2)
            next_low("out", 2)
            lows("out", 2)
            next_low("down", 0)
            norm(4)
            lows("down", 0)
            next_low("qup", 0)
            low(PHASE["qup", 0][0] + 1, 1, PHASE["qup", 0][2])
            for j in range(KD):
                pool.wait_ge(cT_hi, j + 1)
                src = hf[:, j % 2, :] if j < 6 else ckvf[:, j - 6, :]
                nc.gpsimd.tensor_tensor(h_lo[:, j, :], src, h_hi[:, j, :].bitcast(F32),
                                        ALU.subtract).then_inc(cT_lo, 1)
            lows("qup", 0, frm=2)
            next_low("kvup", 0)
            low(PHASE["kvup", 0][0] + 1, 1, PHASE["kvup", 0][2])
            next_low("wo", 1)
            low(PHASE["wo", 1][0] + 1, 1, PHASE["wo", 1][2])
            lows("wo", 1, frm=2)
            next_low("in", 3)
            norm(5)
            lows("in", 3)
            next_low("out", 3)
            lows("out", 3)

        @block.scalar
        def _(act):
            def high(n, slot, width):
                act.wait_ge(w_loaded[slot], (n - slot) * 8 + 16)
                act.wait_ge(panel_used, n + 1)
                nc.scalar.activation(w_hi[:, slot, 0:width], w_raw[:, slot, 0:width], ACT.Copy).then_inc(w_hi_done, 1)

            def high_of(name, i, k):
                base, count, width = PHASE[name, i]
                high(base + k, k % 2, width)

            def copy_rows(j):
                act.wait_ge(rows_ready, j + 1)
                act.wait_ge(cols_ready, j)
                nc.scalar.activation(mrow[:], ps[:, 6, :], ACT.Copy).then_inc(rows_copied, 1)

            def h_high(n):
                with act.Fori(0, KD // 2) as i:
                    for b in range(2):
                        act.wait_ge(h_aff, i * 4 + (2 * KD * n + 2 * b + 2))
                        nc.scalar.activation(h_hi[:, i * 2 + b, :], hf[:, b, :], ACT.Copy).then_inc(h_hi_done, 1)

            def ffn_in(f):
                base, count, width = PHASE["in", f]
                mod = PAIR_BASE.get(("in", f))

                def pair(i, last):
                    for b in range(2):
                        if b == 1 and last:
                            high_of("out", f, 0)
                        else:
                            high(i * 2 + (base + b + 1), 1 - b, width)
                        act.wait_ge(gate_ready, i * 2 + (KF * f + b + 1))
                        nc.scalar.activation(sg[:, b, :], ps[:, 2 * b, 0:T], ACT.Silu).then_inc(silu_done, 1)
                        if b == 0 and mod is not None:
                            copy_rows(mod + i)
                with act.Fori(0, KF // 2 - 1) as i:
                    pair(i, False)
                pair(KF // 2 - 1, True)

            def ffn_out(f, after):
                base, count, width = PHASE["out", f]
                mod = PAIR_BASE.get(("out", f))

                def four(i, last):
                    for s in range(4):
                        if s == 3 and last:
                            if after:
                                high_of(*after, 0)
                        else:
                            high(i * 4 + (base + s + 1), (s + 1) % 2, width)
                        if s == 1 and mod is not None:
                            copy_rows(mod + i)
                with act.Fori(0, KD // 2 - 1) as i:
                    four(i, False)
                four(KD // 2 - 1, True)

            def wo(l, after):
                for i in range(2):
                    high_of("wo", l, 2) if i == 0 else high_of(*after, 0)
                    if i == 0:
                        if l == 0:
                            copy_rows(PAIR_BASE["wo", 0])
                        high_of("wo", l, 3)
                    elif l == 0:
                        copy_rows(PAIR_BASE["wo", 0] + 1)

            def diff():
                high_of("qkv", 0, 1)
                high_of("qkv", 0, 2)
                for c in range(6):
                    b0 = 3 * (c % 2)
                    base = PHASE["qkv", 0][0]
                    if 2 * c + 3 < 12:
                        high_of("qkv", 0, 2 * c + 3)
                    elif 2 * c + 3 == 13:
                        high_of("wo", 0, 1)
                    act.wait_ge(panel_used, START + base + 2 * c + 2)
                    if c < 4:
                        if c > 0:
                            act.wait_ge(red_done, c)
                        nc.scalar.activation(sq3[:], ps[:, b0:b0 + 3, :], ACT.Square).then_inc(sq_done, 1)
                        act.wait_ge(red_done, c + 1)
                        nc.scalar.activation(rms[:, 0:24], ssq[:, 0:24], ACT.Sqrt, bias=epsc[:, 0:1],
                                             scale=1.0 / DIFF_HD).then_inc(rms_done, 1)
                    else:
                        nc.scalar.activation(v_all[:, 1:4, (c - 4) * ROW:(c - 3) * ROW], ps[:, b0:b0 + 3, :],
                                             ACT.Copy).then_inc(v_done, 1)
                    if 2 * c + 4 < 12:
                        high_of("qkv", 0, 2 * c + 4)
                    elif 2 * c + 4 == 12:
                        high_of("wo", 0, 0)
                act.wait_ge(heads_ready, 4)
                act.dma_start(o["new_k"], kn[:, 3, :]).then_inc(out_done, 16)
                act.wait_ge(v_done, 2)
                act.dma_start(o["new_v"], v_all[:, 3, :]).then_inc(out_done, 16)
                for t in range(0, 14, 2):
                    act.wait_ge(tr_ready, t + 1)
                    nc.scalar.activation(ddst(t), ps[:, 6, :].rearrange("p (h t) -> p h t", h=4),
                                         ACT.Copy).then_inc(tr_act, 1)
                act.wait_ge(lam_step, 2)
                nc.scalar.activation(lame[:], lams[:], ACT.Exp).then_inc(lam_exp, 1)
                act.wait_ge(out_done, 32)
                U = 3 * DIFF_HEADS

                def exps(u):
                    p, keys = u % 2, (3 * P if u % 3 < 2 else P)
                    act.wait_ge(nm_ready, u + 1)
                    if u >= 2:
                        act.wait_ge(a_done, u - 1)
                    for c in range(2):
                        nc.scalar.activation(e[:, p, c, 0:keys], ps[:, 2 * p + c, 0:keys], ACT.Exp,
                                             bias=nm[:, p, c:c + 1], scale=DIFF_SCALE,
                                             accum_out=rs[:, p, c:c + 1]).then_inc(exp_done, 1)

                def evac_aT(u):
                    p, keys = u % 2, (3 * P if u % 3 < 2 else P)
                    act.wait_ge(t_ready, u + 1)
                    if u >= 2:
                        act.wait_ge(pv_ready, u - 1)
                    nc.scalar.activation(aT[:, p, 0:keys], ps[:, TURN_BANK["weights", u], 0:keys], ACT.Copy).then_inc(at_done, 1)

                def evac_o(u):
                    h, qb = divmod(u, 3)
                    act.wait_ge(pv_ready, u + 1)
                    if h >= 2:
                        act.wait_ge(on_done, h - 1)
                    nc.scalar.activation(oraw[:, h % 2, qb, :], ps[:, 6 + u % 2, 0:P], ACT.Copy).then_inc(o_done, 1)
                    act.wait_ge(o_done, 2 * u + 1)
                    nc.scalar.activation(osq[:], oraw[:, h % 2, qb, :], ACT.Square,
                                         accum_out=oss[:, h % 2, qb:qb + 1]).then_inc(o_done, 1)

                def out_head(h):
                    act.wait_ge(oT_f, h + 1)
                    nc.scalar.activation(h_hi[:, h, :], otf[:, h % 2, :], ACT.Copy).then_inc(oT_hi, 1)

                exps(0)
                for u in range(U + 4):
                    if u + 1 < U:
                        exps(u + 1)
                    if u < U:
                        evac_aT(u)
                    if 1 <= u <= U:
                        evac_o(u - 1)
                    if u >= 6 and u % 3 == 0:
                        out_head(u // 3 - 2)

            def mla():
                base = PHASE["down", 0][0]
                high_of("down", 0, 1)
                high_of("down", 0, 2)
                high_of("down", 0, 3)
                act.wait_ge(panel_used, START + base + 2)
                for blk in range(NB):
                    nc.scalar.activation(msq3[:, blk, 0:ROW], ps[:, blk, :], ACT.Square,
                                         accum_out=dss[:, blk, 0:1]).then_inc(dss_done, 1)
                high_of("qup", 0, 0)
                act.wait_ge(dss_done, 3)
                act.wait_ge(panel_used, START + base + 4)
                for blk in range(NB):
                    nc.scalar.activation(msq3[:, blk, 0:256], ps[:, 3 + blk, 0:256], ACT.Square,
                                         accum_out=dss[:, blk, 1:2]).then_inc(dss_done, 1)
                    nc.scalar.activation(msq3[:, blk, 256:512], ps[:, 3 + blk, 256:512], ACT.Square,
                                         accum_out=dss[:, blk, 2:3]).then_inc(dss_done, 1)
                act.wait_ge(dvar_ready, 1)
                nc.scalar.activation(drms[:], dvar[:], ACT.Sqrt).then_inc(rms_done, 1)
                high_of("qup", 0, 1)
                act.wait_ge(kpe_ready, 1)
                act.dma_start(o["new_kpe"], kpe[:, 3, :]).then_inc(out_done, 16)
                for j in range(KD):
                    act.wait_ge(cT_f, j + 1)
                    src = hf[:, j % 2, :] if j < 6 else ckvf[:, j - 6, :]
                    nc.scalar.activation(h_hi[:, j, :], src, ACT.Copy).then_inc(cT_hi, 1)
                act.dma_start(o["new_ckvT"].rearrange("k p t -> p k t"), ckvf[:, :, CTX]).then_inc(out_done, 16)
                high_of("qup", 0, 2)
                for c in range(4):
                    b0 = 3 * (c % 2)
                    if 2 * c + 3 < 8:
                        high_of("qup", 0, 2 * c + 3)
                    else:
                        high_of("kvup", 0, 2 * c + 3 - 8)
                    act.wait_ge(panel_used, START + PHASE["qup", 0][0] + 2 * c + 2)
                    act.wait_ge(mred_done, c) if c else act.wait_ge(dss_done, 9)
                    nc.scalar.activation(msq3[:, :, 0:T], ps[:, b0:b0 + 3, 0:T], ACT.Square).then_inc(msq_done, 1)
                    act.wait_ge(mred_done, c + 1)
                    nc.scalar.activation(rms[:, 0:12], ssq[:, 0:12], ACT.Sqrt, bias=epsc[:, 0:1],
                                         scale=1.0 / QK).then_inc(mrms_done, 1)
                    if 2 * c + 4 < 8:
                        high_of("qup", 0, 2 * c + 4)
                    elif c == 2:
                        high_of("kvup", 0, 0)
                def evac(t):
                    act.wait_ge(mtr_ready, t + 1)
                    nc.scalar.activation(mdst(t), ps[0:QK, 6, :].rearrange("p (h t) -> p h t", h=4),
                                         ACT.Copy).then_inc(mtr_act, 1)
                for half in range(2):
                    act.wait_ge(kv_keys, half + 1)
                    if half:
                        act.wait_ge(mred_done, 5)
                    nc.scalar.activation(msq4[:], ps[:, 0:4, :], ACT.Square).then_inc(msq_done, 1)
                    act.wait_ge(panel_used, START + PHASE["kvup", 0][0] + half + 1)
                    nc.scalar.activation(mv_all[:, :, half * ROW:(half + 1) * ROW], ps[:, 4:8, :],
                                         ACT.Copy).then_inc(mv_done, 1)
                    act.wait_ge(mred_done, 5 + half)
                    nc.scalar.activation(rms[:, 0:32], ssq[:, 0:32], ACT.Sqrt, bias=epsc[:, 0:1],
                                         scale=1.0 / QK).then_inc(mrms_done, 1)
                    high_of("wo", 1, half)
                    for t in (range(0, 20, 2) if half == 0 else range(20, 28, 2)):
                        evac(t)
                act.wait_ge(out_done, 64)
                U = 3 * MLA_HEADS

                def exps(u):
                    p, keys = u % 2, (3 * P if u % 3 < 2 else P)
                    act.wait_ge(mnm_ready, u + 1)
                    if u >= 2:
                        act.wait_ge(ma_done, u - 1)
                    nc.scalar.activation(me[:, p, 0:keys], ps[:, p, 0:keys], ACT.Exp, bias=nm[:, p, 0:1],
                                         scale=MLA_SCALE, accum_out=rs[:, p, 0:1]).then_inc(mexp_done, 1)

                def evac_aT(u):
                    p, keys = u % 2, (3 * P if u % 3 < 2 else P)
                    act.wait_ge(mt_ready, u + 1)
                    if u >= 2:
                        act.wait_ge(mpv_ready, u - 1)
                    nc.scalar.activation(maT[:, p, 0:keys], ps[:, 2 + p, 0:keys], ACT.Copy).then_inc(mat_done, 1)

                exps(0)
                for u in range(U):
                    if u + 1 < U:
                        exps(u + 1)
                    evac_aT(u)

            for dst, name in ((cond, "cond"), (bmod, "b_mod"), (norm_g, "norm_g")):
                act.dma_start(dst[:], d[name]).then_inc(small_in, 16)
            act.dma_start(x[:], d["xT"]).then_inc(x_in, 16)
            for dst, name in ((ropes, "ropes"), (gq, "gq"), (gm, "gm"), (subg, "subg"), (gdown, "gdown"),
                              (lamp, "lamp"), (kpw, "kpw")):
                act.dma_start(dst[:], d[name]).then_inc(params_in, 16)
            act.wait_ge(small_in, 48)
            act.wait_ge(dve_consts, 1)
            nc.scalar.activation(scond[:, :, 0:2], cond[:], ACT.Silu).then_inc(scond_ready, 1)
            for j in range(FIRST_PAIRS):
                if j == 0:
                    act.wait_ge(rows_ready, 1)
                    nc.scalar.activation(mrow[:], ps[:, 6, :], ACT.Copy).then_inc(rows_copied, 1)
                else:
                    copy_rows(j)
            high_of("in", 0, 0)
            h_high(0)
            ffn_in(0)
            ffn_out(0, ("qkv", 0))
            act.wait_ge(panel_used, START + PHASE["qkv", 0][0])
            act.dma_start(kn[:, 0, :], d["cache_k"]).then_inc(diff_in, 16)
            act.dma_start(v_all[:, 0, :], d["cache_v"]).then_inc(diff_in, 16)
            h_high(1)
            diff()
            wo(0, ("in", 1))
            h_high(2)
            ffn_in(1)
            ffn_out(1, ("in", 2))
            h_high(3)
            ffn_in(2)
            ffn_out(2, ("down", 0))
            act.wait_ge(panel_used, START + PHASE["down", 0][0])
            act.dma_start(cck[:], d["cache_ckv"]).then_inc(mla_in, 16)
            act.dma_start(kpe[:, 0, :], d["cache_kpe"]).then_inc(mla_in, 16)
            h_high(4)
            mla()
            wo(1, ("in", 3))
            h_high(5)
            ffn_in(3)
            ffn_out(3, None)

        @block.vector
        def _(v):
            nc.vector.memset(scond[:], 0.0).then_inc(dve_consts, 1)
            nc.vector.memset(epsc[:], EPS).then_inc(dve_consts, 1)
            nc.vector.memset(nhalf[:], -0.5).then_inc(dve_consts, 1)
            v.sem_inc(panel_used, START)
            v.sem_inc(prod_ready, START)
            v.sem_inc(h_lo_done, START)
            v.sem_inc(proj_free, START)
            v.sem_inc(res_step, 4 * START)
            v.wait_ge(pool_consts, 3)
            nc.vector.tensor_reduce(sel[:], ident[:].rearrange("p (j c) -> p c j", j=4)[:, 0:2, :], AX.X,
                                    ALU.add).then_inc(dve_consts, 1)

            def squares(i_dc, k, last_inc=1):
                v.wait_ge(res_step, i_dc * 4 + (4 * START + 2))
                nc.vector.tensor_tensor(sqt[:], x[:, k, :], x[:, k, :], ALU.mult).then_inc(res_step, 1)
                v.wait_ge(res_step, i_dc * 4 + (4 * START + 3))
                nc.vector.tensor_tensor(sqacc[:], sqacc[:], sqt[:], ALU.add).then_inc(res_step, 1)

            def mod_cols(j):
                v.wait_ge(cols_ready, j + 1)
                nc.vector.tensor_tensor(modc[:, bass.ds(j * 4, 4), :],
                                        ps[:, 7, 0:8].rearrange("p (c s) -> p c s", c=4),
                                        bmod[:, bass.ds(j * 4, 4), :], ALU.add).then_inc(cols_done, 1)

            def norm(n, layer, part):
                shift, scale = 72 * layer + 24 * part, 72 * layer + 24 * part + 8
                v.wait_ge(cols_done, (scale + 8) // 4)
                nc.vector.scalar_tensor_tensor(gmul[:], modc[:, scale:scale + 8, :], 1.0,
                                               norm_g[:, 3 * layer + part], ALU.add, ALU.mult).then_inc(gains, 1)
                v.wait_ge(ss_ready, n + 1)
                nc.vector.tensor_scalar(var[:, 0:NB], ps[:, 5, 0:NB], 1.0 / D, EPS, ALU.mult,
                                        ALU.add).then_inc(var_ready, 1)
                v.wait_ge(rstd_ready, n + 1)
                for b in range(NB):
                    nc.vector.tensor_scalar(diag[:, b, :], ident[:], rstd[:, b:b + 1], None,
                                            ALU.mult).then_inc(diag_ready, 1)
                v.wait_ge(gains, gain_count[("norm", n)])
                v.wait_ge(bc_ready, n + 1)
                with v.Fori(0, KD // 2) as i:
                    for b in range(2):
                        v.wait_ge(h_lo_done, i * 2 + (KD * n + b + 1))
                        nc.vector.tensor_tensor(hf[:, b, :], x[:, i * 2 + b, :], ps[:, 4, 0:T],
                                                ALU.mult).then_inc(h_tmp, 1)
                        v.wait_ge(h_tmp, i * 2 + (KD * n + b + 1))
                        for s, seg in SEGS:
                            nc.vector.tensor_scalar(hf[:, b, seg], hf[:, b, seg], gmul[:, bass.ds(i * 2 + b, 1), s],
                                                    modc[:, bass.ds(i * 2 + (shift + b), 1), s], ALU.mult,
                                                    ALU.add).then_inc(h_aff, 1)

            gain_count = {}
            for n in range(6):
                gain_count["norm", n] = 1 + 1 + 3 * n
                gain_count["res", n] = 1 + 3 + 3 * n

            def residual(n, layer, part, factor):
                name, f = residuals[n]
                base = PHASE[name, f][0]
                gate = 72 * layer + 24 * part + 16
                mod = PAIR_BASE.get((name, f))
                final = n == 5
                v.wait_ge(cols_done, (gate + 8) // 4)
                nc.vector.tensor_scalar(gres[:], modc[:, gate:gate + 8, :], factor, None,
                                        ALU.mult).then_inc(gains, 1)
                nc.vector.memset(sqacc[:], 0.0).then_inc(gains, 1)
                v.wait_ge(gains, gain_count["res", n])
                rb = RES_BASE[name, f]

                def chunk(k, b, dc):
                    for s, seg in SEGS:
                        nc.vector.scalar_tensor_tensor(x[:, bass.ds(k, 1), seg].rearrange("p a t -> p (a t)"),
                                                       ps[:, 4 + b, seg], gres[:, bass.ds(k, 1), s],
                                                       x[:, bass.ds(k, 1), seg].rearrange("p a t -> p (a t)"),
                                                       ALU.mult, ALU.add).then_inc(res_step, 3 if final and s else 1)
                    if not final:
                        squares(dc, k)

                if name == "out":
                    with v.Fori(0, KD // 2) as i:
                        for b in range(2):
                            v.wait_ge(panel_used, i * 4 + (START + base + 2 * b + 2))
                            chunk(i * 2 + b, b, i * 2 + (rb + b))
                        if mod is not None:
                            mod_cols(mod + i)
                else:
                    with v.Fori(0, 2) as i:
                        for pn in range(2):
                            v.wait_ge(out_ready, i * 2 + (4 * f + pn + 1))
                            chunk(i * 4 + 2 * pn, 0, i * 4 + (rb + 2 * pn))
                            v.wait_ge(panel_used, i * 2 + (START + base + pn + 1))
                            chunk(i * 4 + 2 * pn + 1, 1, i * 4 + (rb + 2 * pn + 1))
                        if mod is not None:
                            mod_cols(mod + i)

            def ffn_in(f):
                base = PHASE["in", f][0]
                mod = PAIR_BASE.get(("in", f))
                with v.Fori(0, KF // 2) as i:
                    for b in range(2):
                        m = KF * f + b + 1
                        v.wait_ge(panel_used, i * 2 + (START + base + b + 1))
                        v.wait_ge(silu_done, i * 2 + m)
                        nc.vector.tensor_tensor(prod[:, b, :], ps[:, 2 * b + 1, 0:T], sg[:, b, :],
                                                ALU.mult).then_inc(prod_ready, 1)
                        v.wait_ge(prod_ready, i * 2 + (START + m))
                        nc.vector.tensor_copy(g_hi[:, i * 2 + b, :], prod[:, b, :]).then_inc(g_hi_done, 1)
                        v.wait_ge(g_hi_done, i * 2 + m)
                        nc.vector.tensor_tensor(g_lo[:, i * 2 + b, :], prod[:, b, :],
                                                g_hi[:, i * 2 + b, :].bitcast(F32), ALU.subtract).then_inc(g_ready, 1)
                    if mod is not None:
                        mod_cols(mod + i)

            count = [0]

            def step(ins):
                count[0] += 1
                ins.then_inc(dve, 1)
                v.wait_ge(dve, count[0])

            def rope(X, groups, half, off, blk):
                r = 4 * half
                cos = ropes[:, 0, blk, off:off + r].unsqueeze(1).to_broadcast([P, groups, r])
                sin = ropes[:, 1, blk, off:off + r].rearrange("p (c h f) -> p c h f", c=2, h=2)
                a1 = t1[:, 0:groups, 0:r]
                b1 = t2[:, 0:groups, 0:r]
                X4 = X.rearrange("p g (c h f) -> p g c h f", c=2, h=2)
                B4 = b1.rearrange("p g (c h f) -> p g c h f", c=2, h=2)
                nc.vector.tensor_tensor(a1, X, cos, ALU.mult)
                for h in range(2):
                    sh = sin[:, :, h, :].unsqueeze(1).to_broadcast([P, groups, 2, half])
                    ins = nc.vector.tensor_tensor(B4[:, :, :, h, :], X4[:, :, :, 1 - h, :], sh, ALU.mult)
                step(ins)
                step(nc.vector.tensor_tensor(X, a1, b1, ALU.add))

            def diff():
                for c in range(4):
                    b0 = 3 * (c % 2)
                    is_k = c // 2
                    v.wait_ge(sq_done, c + 1)
                    nc.vector.tensor_reduce(ssq[:, 0:24].rearrange("p (b g) -> p b g", b=NB),
                                            sq3[:].rearrange("p b (g e) -> p b g e", g=8), AX.X,
                                            ALU.add).then_inc(red_done, 1)
                    v.wait_ge(rms_done, c + 1)
                    step(nc.vector.reciprocal(rinv[:, 0:24], rms[:, 0:24]))
                    to = (kn[:, 1:4, :] if is_k else qn[:])[:, :, (c % 2) * ROW:(c % 2 + 1) * ROW]
                    for b in range(NB):
                        t8 = to[:, b, :].rearrange("p (g e) -> p g e", g=8)
                        nc.vector.tensor_tensor(t8, ps[:, b0 + b, :].rearrange("p (g e) -> p g e", g=8),
                                                rinv[:, 8 * b:8 * b + 8].unsqueeze(2).to_broadcast([P, 8, DIFF_HD]),
                                                ALU.mult).then_inc(*((proj_free, 1) if b == 2 else (dve, 1)))
                    count[0] += 2
                    v.wait_ge(proj_free, START + c + 1)
                    v.wait_ge(dve, count[0])
                    for b in range(NB):
                        t8 = to[:, b, :].rearrange("p (g e) -> p g e", g=8)
                        g8 = gq[:, is_k, :].unsqueeze(1).to_broadcast([P, 8, DIFF_HD])
                        step(nc.vector.tensor_tensor(t8, t8, g8, ALU.mult))
                    for b in range(2):
                        rope(to[:, b, :].rearrange("p (g e) -> p g e", g=8), 8, 16, 0, b)
                    v.sem_inc(heads_ready, 1)
                for t in range(1, 14, 2):
                    v.wait_ge(tr_ready, t + 1)
                    nc.vector.tensor_copy(ddst(t), ps[:, 7, :].rearrange("p (h t) -> p h t", h=4)).then_inc(tr_dve, 1)
                v.wait_ge(lam_exp, 1)
                step(nc.vector.tensor_tensor(neglam[:, 1:2], lame[:, 1:2], lame[:, 0:1], ALU.subtract))
                step(nc.vector.tensor_scalar(neglam[:, 0:1], neglam[:, 1:2], -LAM_INIT, None, ALU.add))
                U = 3 * DIFF_HEADS

                def top(u):
                    p, keys = u % 2, (3 * P if u % 3 < 2 else P)
                    v.wait_ge(s_ready, u + 1)
                    if u >= 2:
                        v.wait_ge(exp_done, 2 * u - 2)
                    step(nc.vector.tensor_reduce(mx[:, p, :], ps[:, 2 * p:2 * p + 2, 0:keys], AX.X, ALU.max))
                    nc.vector.tensor_scalar(nm[:, p, :], mx[:, p, :], -DIFF_SCALE, None, ALU.mult).then_inc(nm_ready, 1)

                def mix(u):
                    p, keys = u % 2, (3 * P if u % 3 < 2 else P)
                    v.wait_ge(exp_done, 2 * u + 2)
                    step(nc.vector.reciprocal(ri[:, p, :], rs[:, p, :]))
                    step(nc.vector.tensor_tensor(ri2[:, p:p + 1], ri[:, p, 1:2], neglam[:, 0:1], ALU.mult))
                    step(nc.vector.tensor_scalar(a2[:, 0:keys], e[:, p, 1, 0:keys], ri2[:, p:p + 1], None, ALU.mult))
                    if u >= 2:
                        v.wait_ge(t_ready, u - 1)
                    nc.vector.scalar_tensor_tensor(a[:, p, 0:keys], e[:, p, 0, 0:keys], ri[:, p, 0:1],
                                                   a2[:, 0:keys], ALU.mult, ALU.add).then_inc(a_done, 1)

                v.wait_ge(out_done, 32)
                top(0)
                for u in range(U + 4):
                    if u >= 6 and u % 3 == 0:
                        h = u // 3 - 2
                        v.wait_ge(oT_ready, h + 1)
                        if h >= 2:
                            v.wait_ge(oT_lo, h - 1)
                        nc.vector.tensor_scalar(otf[:, h % 2, :], ps[:, TURN_BANK["outputs", h], 0:T], subg[:, 0:1],
                                                1.0 - LAM_INIT, ALU.mult, ALU.mult).then_inc(oT_f, 1)
                    if u + 1 < U:
                        top(u + 1)
                    if u < U:
                        mix(u)
                    if u >= 4 and u % 3 == 1:
                        h = u // 3 - 1
                        v.wait_ge(o_done, 6 * h + 6)
                        nc.vector.tensor_scalar(ovar[:, h % 2, :], oss[:, h % 2, :], 1.0 / DIFF_VD, EPS, ALU.mult,
                                                ALU.add).then_inc(ovar_ready, 1)
                    if u >= 5 and u % 3 == 2:
                        h = u // 3 - 1
                        v.wait_ge(orin_ready, h + 1)
                        if h >= 2:
                            v.wait_ge(oT_ready, h - 1)
                        nc.vector.tensor_tensor(onrm[:, h % 2], oraw[:, h % 2],
                                                orin[:, h % 2, :].unsqueeze(2).to_broadcast([P, NB, DIFF_VD]),
                                                ALU.mult).then_inc(on_done, 1)

            def mla():
                v.wait_ge(mla_in, 32)
                nc.vector.tensor_copy(cck_hi[:], cck[:]).then_inc(cck_step, 1)
                v.wait_ge(cck_step, 1)
                nc.vector.tensor_tensor(cck_lo[:], cck[:], cck_hi[:].bitcast(F32), ALU.subtract).then_inc(cck_step, 1)
                v.wait_ge(kpe_prod, 1)
                nc.vector.tensor_copy(kpe[:, 1:4, :], ps[:, 6, 0:NB * ROPE].rearrange("p (b r) -> p b r", b=NB)
                                      ).then_inc(kpe_ready, 1)
                v.wait_ge(kpe_ready, 1)
                v.wait_ge(dss_done, 9)
                step(nc.vector.tensor_tensor(dtot[:], dss[:, :, 0], dss[:, :, 1], ALU.add))
                nc.vector.tensor_scalar(dvar[:, 1, :], dss[:, :, 2], 1.0 / KV_RANK, EPS, ALU.mult, ALU.add)
                step(nc.vector.tensor_scalar(dvar[:, 0, :], dtot[:], 1.0 / Q_RANK, EPS, ALU.mult, ALU.add))
                v.sem_inc(dvar_ready, 1)
                step(nc.vector.tensor_tensor(kps[:], kpe[:], kpe[:], ALU.mult))
                step(nc.vector.tensor_reduce(kpss[:], kps[:], AX.X, ALU.add))
                step(nc.vector.tensor_tensor(kpg[:], kpe[:],
                                             gm[:, 1, NOPE:QK].unsqueeze(1).to_broadcast([P, 4, ROPE]), ALU.mult))
                for b in range(2):
                    rope(kpg[:, 1 + b:2 + b, :], 1, 8, 64, b)
                v.wait_ge(rms_done, 5)
                step(nc.vector.reciprocal(drin[:], drms[:]))
                for b in range(NB):
                    nc.vector.tensor_scalar(cn[:, b, 0:ROW], ps[:, b, :], drin[:, 0, b:b + 1], None,
                                            ALU.mult).then_inc(cn_done, 1)
                    nc.vector.tensor_scalar(cn[:, b, ROW:Q_RANK], ps[:, 3 + b, 0:256], drin[:, 0, b:b + 1], None,
                                            ALU.mult).then_inc(cn_done, 1)
                    nc.vector.tensor_scalar(cn[:, b, Q_RANK:D], ps[:, 3 + b, 256:512], drin[:, 1, b:b + 1], None,
                                            ALU.mult).then_inc(cn_done, 1)
                for j in range(KD):
                    v.wait_ge(cT_ready, j + 1)
                    if 2 <= j < 6:
                        v.wait_ge(cT_lo, j - 1)
                    dst = hf[:, j % 2, :] if j < 6 else ckvf[:, j - 6, :]
                    nc.vector.tensor_scalar(dst, ps[:, 6 + j % 2, 0:T], gdown[:, j:j + 1], None,
                                            ALU.mult).then_inc(cT_f, 1)
                for c in range(4):
                    b0 = 3 * (c % 2)
                    v.wait_ge(msq_done, c + 1)
                    nc.vector.tensor_reduce(ssq[:, 0:12].rearrange("p (b g) -> p b g", b=NB),
                                            msq3[:, :, 0:T].rearrange("p b (g e) -> p b g e", g=4), AX.X,
                                            ALU.add).then_inc(mred_done, 1)
                    v.wait_ge(mrms_done, c + 1)
                    step(nc.vector.reciprocal(rinv[:, 0:12], rms[:, 0:12]))
                    for b in range(NB):
                        t4 = mqn[:, b, c * T:(c + 1) * T].rearrange("p (g e) -> p g e", g=4)
                        ins = nc.vector.tensor_tensor(t4, ps[:, b0 + b, 0:T].rearrange("p (g e) -> p g e", g=4),
                                                      rinv[:, 4 * b:4 * b + 4].unsqueeze(2).to_broadcast([P, 4, QK]),
                                                      ALU.mult)
                        if b < 2:
                            step(ins)
                    ins.then_inc(mproj_free, 1)
                    v.wait_ge(mproj_free, c + 1)
                    for b in range(NB):
                        t4 = mqn[:, b, c * T:(c + 1) * T].rearrange("p (g e) -> p g e", g=4)
                        step(nc.vector.tensor_tensor(t4, t4, gm[:, 0, :].unsqueeze(1).to_broadcast([P, 4, QK]),
                                                     ALU.mult))
                        if b < 2:
                            rope(t4[:, :, NOPE:QK], 4, 8, 64, b)
                    v.sem_inc(mheads, 1)
                for half in range(2):
                    v.wait_ge(msq_done, 5 + half)
                    step(nc.vector.tensor_reduce(ssq[:, 0:32].rearrange("p (b g) -> p b g", b=4),
                                                 msq4[:].rearrange("p b (g e) -> p b g e", g=8), AX.X, ALU.add))
                    s4 = ssq[:, 0:32].rearrange("p (b g) -> p b g", b=4)
                    nc.vector.tensor_tensor(s4, s4, kpss[:].unsqueeze(2).to_broadcast([P, 4, 8]),
                                            ALU.add).then_inc(mred_done, 1)
                    v.wait_ge(mrms_done, 5 + half)
                    step(nc.vector.reciprocal(rinv[:, 0:32], rms[:, 0:32]))
                    if half:
                        v.wait_ge(mtr_ready, 20)
                    else:
                        v.wait_ge(out_done, 64)
                    r4 = rinv[:, 0:32].rearrange("p (b g) -> p b g", b=4)
                    for b in range(4):
                        r8 = r4[:, b, :].unsqueeze(2)
                        ins = nc.vector.tensor_tensor(mkn[:, b, :, 0:NOPE],
                                                      ps[:, b, :].rearrange("p (g e) -> p g e", g=8),
                                                      r8.to_broadcast([P, 8, NOPE]), ALU.mult)
                        if b < 3:
                            step(ins)
                        else:
                            ins.then_inc(kbank_free, 1)
                            v.wait_ge(kbank_free, half + 1)
                        step(nc.vector.tensor_tensor(mkn[:, b, :, NOPE:QK],
                                                     kpg[:, b, :].unsqueeze(1).to_broadcast([P, 8, ROPE]),
                                                     r8.to_broadcast([P, 8, ROPE]), ALU.mult))
                        step(nc.vector.tensor_tensor(mkn[:, b, :, 0:NOPE], mkn[:, b, :, 0:NOPE],
                                                     gm[:, 1, 0:NOPE].unsqueeze(1).to_broadcast([P, 8, NOPE]),
                                                     ALU.mult))
                    v.sem_inc(mkheads, 1)
                    for t in (range(1, 20, 2) if half == 0 else range(21, 28, 2)):
                        v.wait_ge(mtr_ready, t + 1)
                        nc.vector.tensor_copy(mdst(t), ps[0:QK, 7, :].rearrange("p (h t) -> p h t", h=4)
                                              ).then_inc(mtr_dve, 1)
                U = 3 * MLA_HEADS

                def top(u):
                    p, keys = u % 2, (3 * P if u % 3 < 2 else P)
                    v.wait_ge(ms_ready, u + 1)
                    if u >= 2:
                        v.wait_ge(mexp_done, u - 1)
                    step(nc.vector.tensor_reduce(mx[:, p, 0:1], ps[:, p, 0:keys], AX.X, ALU.max))
                    nc.vector.tensor_scalar(nm[:, p, 0:1], mx[:, p, 0:1], -MLA_SCALE, None,
                                            ALU.mult).then_inc(mnm_ready, 1)

                def scale(u):
                    p, keys = u % 2, (3 * P if u % 3 < 2 else P)
                    v.wait_ge(mexp_done, u + 1)
                    step(nc.vector.reciprocal(ri[:, p, 0:1], rs[:, p, 0:1]))
                    if u >= 2:
                        v.wait_ge(mt_ready, u - 1)
                    nc.vector.tensor_scalar(ma[:, p, 0:keys], me[:, p, 0:keys], ri[:, p, 0:1], None,
                                            ALU.mult).then_inc(ma_done, 1)

                top(0)
                for u in range(U + 2):
                    if u + 1 < U:
                        top(u + 1)
                    if u < U:
                        scale(u)
                    if u >= 7 and u % 6 == 1:
                        pr = u // 6 - 1
                        v.wait_ge(mpv_ready, 6 * pr + 6)
                        nc.vector.tensor_copy(h_hi[:, pr, :], ps[:, 4 + pr % 2, 0:T]).then_inc(mo_hi, 1)
                        v.wait_ge(mo_hi, pr + 1)
                        nc.vector.tensor_tensor(h_lo[:, pr, :], ps[:, 4 + pr % 2, 0:T],
                                                h_hi[:, pr, :].bitcast(F32), ALU.subtract).then_inc(mo_lo, 1)

            nc.vector.memset(sqacc[:], 0.0).then_inc(gains, 1)
            v.wait_ge(gains, 1)
            v.wait_ge(x_in, 16)
            with v.Fori(0, KD) as k:
                nc.vector.tensor_tensor(sqt[:], x[:, k, :], x[:, k, :], ALU.mult).then_inc(res_step, 3)
                v.wait_ge(res_step, k * 4 + (4 * START + 3))
                nc.vector.tensor_tensor(sqacc[:], sqacc[:], sqt[:], ALU.add).then_inc(res_step, 1)
                v.wait_ge(res_step, k * 4 + (4 * START + 4))
            v.wait_ge(params_in, 112)
            nc.vector.tensor_tensor(lamt[:], lamp[:, 0::2, :], lamp[:, 1::2, :], ALU.mult).then_inc(lam_step, 1)
            v.wait_ge(lam_step, 1)
            nc.vector.tensor_reduce(lams[:], lamt[:], AX.X, ALU.add).then_inc(lam_step, 1)
            nc.vector.tensor_copy(kpw_hi[:], kpw[:]).then_inc(kpw_done, 1)
            v.wait_ge(kpw_done, 1)
            nc.vector.tensor_tensor(kpw_lo[:], kpw[:], kpw_hi[:].bitcast(F32), ALU.subtract).then_inc(kpw_done, 1)
            v.wait_ge(small_in, 48)
            for j in range(FIRST_PAIRS):
                mod_cols(j)
            norm(0, 0, 0)
            ffn_in(0)
            residual(0, 0, 0, 0.5)
            norm(1, 0, 1)
            diff()
            residual(1, 0, 1, 1.0)
            norm(2, 0, 2)
            ffn_in(1)
            residual(2, 0, 2, 0.5)
            norm(3, 1, 0)
            ffn_in(2)
            residual(3, 1, 0, 0.5)
            norm(4, 1, 1)
            mla()
            residual(4, 1, 1, 1.0)
            norm(5, 1, 2)
            ffn_in(3)
            residual(5, 1, 2, 0.5)

        @block.tensor
        def _(pe):
            def mm3(out, l_hi, l_lo, r_hi, r_lo, first, last):
                nc.tensor.matmul(out, l_hi, r_hi, start=first, stop=False)
                nc.tensor.matmul(out, l_hi, r_lo, start=False, stop=False)
                return nc.tensor.matmul(out, l_lo, r_hi, start=False, stop=last)

            def mod_pair(j, panels, loaded):
                for kh in range(2):
                    pe.wait_ge(*loaded[kh])
                    if kh == 0 and not (isinstance(j, int) and j == 0):
                        pe.wait_ge(rows_copied, j)
                    for kk in range(4):
                        mm = nc.tensor.matmul(ps[32 * kk:32 * kk + 32, 6, :], scond[:, 4 * kh + kk, :],
                                              panels[kh][:, kk * ROW:(kk + 1) * ROW], start=kh == 0, stop=kh == 1,
                                              tile_position=(0, 32 * kk))
                mm.then_inc(rows_ready, 1)

            def mod_ring(j):
                mod_pair(j, [wm[:, 0, :], wm[:, 1, :]],
                         [(wm_loaded[kh], (j - (FIRST_PAIRS - 1)) * 16) for kh in range(2)])

            def mod_cols(j):
                pe.wait_ge(rows_copied, j + 1)
                if not (isinstance(j, int) and j == 0):
                    pe.wait_ge(cols_done, j)
                for c in range(4):
                    mm = nc.tensor.matmul(ps[:, 7, 2 * c:2 * c + 2], mrow[:, c * P:(c + 1) * P], sel[:],
                                          start=True, stop=True)
                mm.then_inc(cols_ready, 1)

            def norm(n):
                pe.wait_ge(res_step, 4 * (START + KD * (n + 1)))
                for b in range(NB):
                    mm = nc.tensor.matmul(ps[:, 5, b:b + 1], sqacc[:, b * P:(b + 1) * P], ones[:, 0:1],
                                          start=True, stop=True)
                mm.then_inc(ss_ready, 1)
                pe.wait_ge(diag_ready, NB * (n + 1))
                nc.tensor.matmul(ps[:, 4, 0:T], ones[:], diag[:].rearrange("p b t -> p (b t)"), start=True,
                                 stop=True).then_inc(bc_ready, 1)

            def w_tile(slot, t, n=P):
                return w_hi[:, slot, t * n:(t + 1) * n], w_lo[:, slot, t * n:(t + 1) * n]

            def ffn_in(f, n):
                base = PHASE["in", f][0]
                mod = PAIR_BASE.get(("in", f))
                with pe.Fori(0, KF // 2) as i:
                    for b in range(2):
                        pe.wait_ge(w_lo_done, i * 2 + (base + b + 1))
                        pe.wait_ge(prod_ready, i * 2 + (KF * f + b + 1))
                        for half, done in ((0, gate_ready), (1, panel_used)):
                            for k in range(KD):
                                if b == 0 and half == 0:
                                    pe.wait_ge(h_lo_done, h_val(n, k))
                                mm = mm3(ps[:, 2 * b + half, 0:T], *w_tile(b, KD * half + k), h_hi[:, k, :],
                                         h_lo[:, k, :], k == 0, k == KD - 1)
                            mm.then_inc(done, 1)
                        if mod is not None:
                            (mod_ring if b == 0 else mod_cols)(mod + i)

            def ffn_out(f):
                base = PHASE["out", f][0]
                mod = PAIR_BASE.get(("out", f))
                rb = RES_BASE["out", f]
                kh = KF // 2
                with pe.Fori(0, KD // 2) as i:
                    for b in range(2):
                        pe.wait_ge(res_step, i * 8 + (4 * (rb + b) + 2))
                        for half in range(2):
                            pe.wait_ge(w_lo_done, i * 4 + (base + 2 * b + half + 1))
                            for k in range(kh):
                                if b == 0 and (k == 0 or half and k == kh - 1):
                                    pe.wait_ge(g_ready, KF * f + (kh if not half else KF - 1 if k == 0 else KF))
                                mm = mm3(ps[:, 4 + b, 0:T], *w_tile(half, k), g_hi[:, kh * half + k, :],
                                         g_lo[:, kh * half + k, :], half == 0 and k == 0, half == 1 and k == kh - 1)
                            mm.then_inc(panel_used, 1)
                        if mod is not None:
                            (mod_ring if b == 0 else mod_cols)(mod + i)

            def wo(layer, parts):
                base = PHASE["wo", layer][0]
                mod = PAIR_BASE.get(("wo", layer))
                rb = RES_BASE["wo", layer]
                with pe.Fori(0, 2) as i:
                    for pn in range(2):
                        pe.wait_ge(w_lo_done, i * 2 + (base + pn + 1))
                        for b in range(2):
                            pe.wait_ge(res_step, i * 16 + (4 * (rb + 2 * pn + b) + 2))
                            for k in range(KD):
                                if pn == 0 and b == 0:
                                    pe.wait_ge(parts, k + 1)
                                mm = mm3(ps[:, 4 + b, 0:T], *w_tile(pn, KD * b + k), h_hi[:, k, :], h_lo[:, k, :],
                                         k == 0, k == KD - 1)
                            mm.then_inc(out_ready if b == 0 else panel_used, 1)
                        if mod is not None:
                            (mod_ring if pn == 0 else mod_cols)(mod + i)

            def project(s, kh, per, width, hk, banks, first, last, waits=None):
                for kk in range(per):
                    if waits is not None:
                        pe.wait_ge(waits[0], waits[1] + kh * per + kk)
                    for blk in range(NB):
                        k = hk + kh * per + kk
                        mm = mm3(ps[:, banks + blk, 0:width], h_hi[:, k, blk * P:(blk + 1) * P],
                                 h_lo[:, k, blk * P:(blk + 1) * P], *w_tile(s, kk, width),
                                 first and kk == 0, last and kk == per - 1)
                return mm

            def diff():
                base = PHASE["qkv", 0][0]
                with pe.Fori(0, 3) as i:
                    for c in range(2):
                        pe.wait_ge(proj_free, i * 2 + (c + 1))
                        for kh in range(2):
                            pe.wait_ge(w_lo_done, i * 4 + (base + 2 * c + kh + 1))
                            project(kh, kh, 4, ROW, 0, 3 * c, kh == 0, kh == 1,
                                    (h_lo_done, h_val(1, 0)) if c == 0 else None).then_inc(panel_used, 1)
                for t in range(14):
                    pe.wait_ge(heads_ready, 2 if t < 6 else 4)
                    if t == 6:
                        pe.wait_ge(diff_in, 32)
                    if t >= 2:
                        pe.wait_ge(tr_dve if t % 2 else tr_act, t // 2)
                    for i in range(4):
                        if t < 6:
                            src = qn[:, t % 3, (4 * (t // 3) + i) * P:(4 * (t // 3) + i + 1) * P]
                        else:
                            g, slot = divmod(t - 6, 4)
                            src = kn[:, slot, (4 * g + i) * P:(4 * g + i + 1) * P]
                        mm = nc.tensor.transpose(ps[:, 6 + t % 2, i * P:(i + 1) * P], src, ident[:])
                    mm.then_inc(tr_ready, 1)
                U = 3 * DIFF_HEADS

                def scores(u):
                    h, qb = divmod(u, 3)
                    keys = slice(0, 3 * P) if qb < 2 else slice(3 * P, 4 * P)
                    n = keys.stop - keys.start
                    if u >= 2:
                        pe.wait_ge(exp_done, 2 * u - 2)
                    for c in range(2):
                        r = slice(DIFF_HD * c, DIFF_HD * (c + 1))
                        mm = nc.tensor.matmul(ps[:, 2 * (u % 2) + c, 0:n], dqT[r, h, qb * P:(qb + 1) * P],
                                              dkT[r, h, keys], start=True, stop=True)
                    mm.then_inc(s_ready, 1)

                def turn(u):
                    p = u % 2
                    pe.wait_ge(a_done, u + 1)
                    turn_free(pe, ("weights", u))
                    for kb in range(3 if u % 3 < 2 else 1):
                        mm = nc.tensor.transpose(ps[:, TURN_BANK["weights", u], kb * P:(kb + 1) * P], a[:, p, kb * P:(kb + 1) * P],
                                                 ident[:])
                    mm.then_inc(t_ready, 1)

                def values(u):
                    h, qb = divmod(u, 3)
                    slots = (0, 1, 2) if qb < 2 else (3,)
                    pe.wait_ge(at_done, u + 1)
                    if u >= 2:
                        pe.wait_ge(o_done, 2 * u - 3)
                    for kb, slot in enumerate(slots):
                        mm = nc.tensor.matmul(ps[:, 6 + u % 2, 0:P], aT[:, u % 2, kb * P:(kb + 1) * P],
                                              v_all[:, slot, h * DIFF_VD:(h + 1) * DIFF_VD], start=kb == 0,
                                              stop=kb == len(slots) - 1)
                    mm.then_inc(pv_ready, 1)

                def out_turn(h):
                    pe.wait_ge(on_done, h + 1)
                    turn_free(pe, ("outputs", h))
                    for b in range(NB):
                        mm = nc.tensor.transpose(ps[:, TURN_BANK["outputs", h], b * P:(b + 1) * P], onrm[:, h % 2, b, :],
                                                 ident[:])
                    mm.then_inc(oT_ready, 1)

                pe.wait_ge(tr_act, 7)
                pe.wait_ge(tr_dve, 7)
                pe.wait_ge(v_done, 2)
                scores(0)
                for u in range(U + 3):
                    if u + 1 < U:
                        scores(u + 1)
                    if u < U:
                        turn(u)
                    if 1 <= u <= U:
                        values(u - 1)
                    if u >= 5 and u % 3 == 2:
                        out_turn(u // 3 - 1)

            def mla():
                base = PHASE["down", 0][0]
                for c in range(2):
                    for kh in range(2):
                        pe.wait_ge(w_lo_done, base + 2 * c + kh + 1)
                        project(kh, kh, 4, ROW, 0, 3 * c, kh == 0, kh == 1,
                                (h_lo_done, h_val(4, 0)) if c == 0 else None).then_inc(panel_used, 1)
                pe.wait_ge(kpw_done, 2)
                for blk in range(NB):
                    for k in range(KD):
                        mm = mm3(ps[:, 6, blk * ROPE:(blk + 1) * ROPE], h_hi[:, k, blk * P:(blk + 1) * P],
                                 h_lo[:, k, blk * P:(blk + 1) * P], kpw_hi[:, k, :], kpw_lo[:, k, :], k == 0,
                                 k == KD - 1)
                mm.then_inc(kpe_prod, 1)
                pe.wait_ge(kpe_ready, 1)
                pe.wait_ge(cn_done, 9)
                for j in range(KD):
                    if j >= 2:
                        pe.wait_ge(cT_f, j - 1)
                    for b in range(NB):
                        mm = nc.tensor.transpose(ps[:, 6 + j % 2, b * P:(b + 1) * P], cn[:, b, j * P:(j + 1) * P],
                                                 ident[:])
                    mm.then_inc(cT_ready, 1)
                base = PHASE["qup", 0][0]
                for c in range(4):
                    if c >= 2:
                        pe.wait_ge(mproj_free, c - 1)
                    for kh in range(2):
                        pe.wait_ge(w_lo_done, base + 2 * c + kh + 1)
                        project(kh, kh, 3, T, 0, 3 * (c % 2), kh == 0, kh == 1,
                                (cT_lo, 1) if c == 0 else None).then_inc(panel_used, 1)
                base = PHASE["kvup", 0][0]

                def up(half, part, bank):
                    for slot in range(4):
                        for kk in range(2):
                            l_hi = cck_hi[:, kk, :] if slot == 0 else h_hi[:, 6 + kk, (slot - 1) * P:slot * P]
                            l_lo = cck_lo[:, kk, :] if slot == 0 else h_lo[:, 6 + kk, (slot - 1) * P:slot * P]
                            mm = mm3(ps[:, bank + slot, :], l_hi, l_lo, *w_tile(half, 2 * part + kk, ROW), kk == 0,
                                     kk == 1)
                    return mm

                def turns(ts):
                    for t in ts:
                        if t >= 2:
                            pe.wait_ge(mtr_dve if t % 2 else mtr_act, t // 2)
                        for i in range(4):
                            if t < 12:
                                h = 4 * (t // 3) + i
                                src = mqn[:, t % 3, h * QK:(h + 1) * QK]
                            else:
                                g, slot = divmod(t - 12, 4)
                                src = mkn[:, slot, 4 * (g % 2) + i, :]
                            mm = nc.tensor.transpose(ps[0:QK, 6 + t % 2, i * P:(i + 1) * P], src, ident[:])
                        mm.then_inc(mtr_ready, 1)

                pe.wait_ge(cck_step, 2)
                pe.wait_ge(cT_f, 8)
                pe.wait_ge(cT_lo, 8)
                for half in range(2):
                    pe.wait_ge(w_lo_done, base + half + 1)
                    if half == 0:
                        pe.wait_ge(mproj_free, 4)
                    else:
                        pe.wait_ge(kbank_free, 1)
                    up(half, 0, 0).then_inc(kv_keys, 1)
                    if half:
                        pe.wait_ge(mtr_act, 10)
                        pe.wait_ge(mtr_dve, 10)
                    up(half, 1, 4).then_inc(panel_used, 1)
                    pe.wait_ge(mv_done, half + 1)
                    if half == 0:
                        pe.wait_ge(mheads, 4)
                        turns(range(12))
                    pe.wait_ge(mkheads, half + 1)
                    turns(range(12 + 8 * half, 20 + 8 * half))
                U = 3 * MLA_HEADS

                def scores(u):
                    h, qb = divmod(u, 3)
                    keys = slice(0, 3 * P) if qb < 2 else slice(3 * P, 4 * P)
                    if u >= 2:
                        pe.wait_ge(mexp_done, u - 1)
                    nc.tensor.matmul(ps[:, u % 2, 0:keys.stop - keys.start], mqT[:, h, qb * P:(qb + 1) * P],
                                     mkT[:, h, keys], start=True, stop=True).then_inc(ms_ready, 1)

                def turn(u):
                    p = u % 2
                    pe.wait_ge(ma_done, u + 1)
                    if u >= 2:
                        pe.wait_ge(mat_done, u - 1)
                    for kb in range(3 if u % 3 < 2 else 1):
                        mm = nc.tensor.transpose(ps[:, 2 + p, kb * P:(kb + 1) * P], ma[:, p, kb * P:(kb + 1) * P],
                                                 ident[:])
                    mm.then_inc(mt_ready, 1)

                def values(u):
                    h, qb = divmod(u, 3)
                    slots = (0, 1, 2) if qb < 2 else (3,)
                    pe.wait_ge(mat_done, u + 1)
                    if u % 6 == 0 and u >= 12:
                        pe.wait_ge(mo_lo, u // 6 - 1)
                    row = MLA_VD * (h % 2)
                    for kb, slot in enumerate(slots):
                        mm = nc.tensor.matmul(ps[row:row + MLA_VD, 4 + (h // 2) % 2, qb * P:(qb + 1) * P],
                                              mv_all[:, slot, h * MLA_VD:(h + 1) * MLA_VD],
                                              maT[:, u % 2, kb * P:(kb + 1) * P], start=kb == 0,
                                              stop=kb == len(slots) - 1)
                    mm.then_inc(mpv_ready, 1)

                pe.wait_ge(kbank_free, 2)
                pe.wait_ge(mtr_act, 14)
                pe.wait_ge(mtr_dve, 14)
                scores(0)
                for u in range(U + 1):
                    if u + 1 < U:
                        scores(u + 1)
                    if u < U:
                        turn(u)
                    if u >= 1:
                        values(u - 1)

            pe.wait_ge(pool_consts, 3)
            pe.wait_ge(dve_consts, 4)
            pe.wait_ge(scond_ready, 1)
            for j in range(FIRST_PAIRS):
                mod_pair(j, [wm_first[:, 2 * j, :], wm_first[:, 2 * j + 1, :]],
                         [(wmf_loaded[2 * j + kh], 16) for kh in range(2)])
                mod_cols(j)
            norm(0)
            ffn_in(0, 0)
            ffn_out(0)
            norm(1)
            diff()
            wo(0, oT_lo)
            norm(2)
            ffn_in(1, 2)
            ffn_out(1)
            norm(3)
            ffn_in(2, 3)
            ffn_out(2)
            norm(4)
            mla()
            wo(1, mo_lo)
            norm(5)
            ffn_in(3, 5)
            ffn_out(3)


def rope_table():
    out = np.zeros((2, 2, P, 64 + ROPE), np.float32)
    tok = np.arange(256)
    for off, r in ((0, 64), (64, ROPE)):
        half = r // 4
        n = r // 2
        freqs = (np.float32(10000.0) ** (-np.arange(0, n, 2, dtype=np.float32) / np.float32(n))).astype(np.float32)
        for c, pos in enumerate((tok // 64, tok % 64)):
            ang = (pos.astype(np.float32)[:, None] * freqs[None, :]).astype(np.float32)
            cos, sin = np.cos(ang), np.sin(ang)
            for h in range(2):
                at = off + c * 2 * half + h * half
                out[0, :, :, at:at + half] = cos.reshape(2, P, half)
                out[1, :, :, at:at + half] = (sin if h else -sin).reshape(2, P, half)
    return np.ascontiguousarray(out.transpose(2, 0, 1, 3))


def kernel(x_prompt, x_sample, c, cache_diff_k, cache_diff_v, cache_mla_ckv, cache_mla_kpe, c_ctx,
           w_mod, b_mod, norm_g, ffn_w_in, ffn_w_out,
           diff_w_qkv, diff_q_norm, diff_k_norm, diff_lambda, diff_subln, diff_w_o,
           mla_w_down, mla_q_a_norm, mla_kv_a_norm, mla_w_q_up, mla_w_kv_up, mla_q_norm, mla_k_norm, mla_w_o):
    import concourse.bacc as bacc
    from concourse.bass_utils import run_bass_kernel_spmd

    A = np.asarray

    def every(a, *shape):
        return np.broadcast_to(A(a).reshape((1,) + shape), (P,) + shape)

    tokens = np.concatenate([A(x_sample)[0], A(x_prompt)[0]])
    kv = A(mla_w_kv_up)[0].reshape(2, P, MLA_HEADS, 2, NOPE)
    kv = kv.reshape(2, P, 2, 8, 2, NOPE).transpose(2, 1, 4, 0, 3, 5)
    both = np.stack([A(diff_w_o)[0], A(mla_w_o)[0]])
    arrays = {
        "xT": tokens.reshape(T, KD, P).transpose(2, 1, 0),
        "cond": np.stack([A(c_ctx), A(c)[0]], -1).reshape(KD, P, 2).transpose(1, 0, 2),
        "b_mod": np.broadcast_to(A(b_mod).reshape(DEPTH * 72, P).T[:, :, None], (P, DEPTH * 72, 2)),
        "norm_g": np.broadcast_to(A(norm_g).reshape(6, KD, P).transpose(2, 0, 1)[..., None], (P, 6, KD, 2)),
        "w_mod": A(w_mod).reshape(DEPTH, 2, 4, P, 18, ROW).transpose(0, 4, 1, 3, 2, 5).reshape(2 * PAIRS, P, 4 * ROW),
        "w_in": A(ffn_w_in).reshape(4, KD, P, 2, KF, P).transpose(0, 4, 2, 3, 1, 5).reshape(4, KF, P, 16 * P),
        "w_out": A(ffn_w_out).reshape(4, 2, KF // 2, P, KD, P).transpose(0, 4, 1, 3, 2, 5)
                  .reshape(4, 2 * KD, P, 11 * P),
        "w_qkv": A(diff_w_qkv)[0].reshape(2, 4, P, 6, ROW).transpose(3, 0, 2, 1, 4).reshape(12, P, 4 * ROW),
        "w_o": both.reshape(2, KD, P, 4, 2, P).transpose(0, 3, 2, 4, 1, 5).reshape(2, 4, P, 16 * P),
        "w_down": A(mla_w_down)[0, :, :D].reshape(2, 4, P, 2, ROW).transpose(3, 0, 2, 1, 4).reshape(4, P, 4 * ROW),
        "kpw": A(mla_w_down)[0, :, D:].reshape(KD, P, ROPE).transpose(1, 0, 2),
        "w_qup": A(mla_w_q_up)[0].reshape(2, 3, P, 4, T).transpose(3, 0, 2, 1, 4).reshape(8, P, 3 * T),
        "w_kvup": kv.reshape(2, P, 4 * ROW),
        "ropes": rope_table(),
        "gq": every(np.stack([A(diff_q_norm)[0], A(diff_k_norm)[0]]), 2, DIFF_HD),
        "gm": every(np.stack([A(mla_q_norm)[0], A(mla_k_norm)[0]]), 2, QK),
        "subg": np.broadcast_to(A(diff_subln)[0][:, None], (P, 2)),
        "gdown": np.concatenate([A(mla_q_a_norm)[0], A(mla_kv_a_norm)[0]]).reshape(KD, P).T,
        "lamp": every(diff_lambda, 4, DIFF_HD),
        "cache_k": A(cache_diff_k)[0, 0].reshape(P, D),
        "cache_v": A(cache_diff_v)[0, 0].reshape(P, D),
        "cache_ckv": A(cache_mla_ckv)[0, 0].reshape(P, 2, P).transpose(2, 1, 0),
        "cache_kpe": A(cache_mla_kpe)[0, 0],
    }
    arrays = {k: np.ascontiguousarray(a) for k, a in arrays.items()}
    outs = {"yT": (KD, P, T), "new_k": (P, D), "new_v": (P, D), "new_ckvT": (2, P, P), "new_kpe": (P, ROPE)}
    nc = bacc.Bacc("TRN2", target_bir_lowering=False, num_devices=1)
    d = {k: nc.dram_tensor("in_" + k, a.shape, F32, kind="ExternalInput").ap() for k, a in arrays.items()}
    o = {k: nc.dram_tensor("out_" + k, s, F32, kind="ExternalOutput").ap() for k, s in outs.items()}
    build_step(nc, d, o)
    r = run_bass_kernel_spmd(nc, [{"in_" + k: a for k, a in arrays.items()}], core_ids=[0]).results[0]
    r = {k: r["out_" + k] for k in outs}
    y = r["yT"].reshape(D, T).T
    return (y[None, 256:], y[None, :256],
            r["new_k"].reshape(1, 1, P, DIFF_HEADS, 2, DIFF_HD), r["new_v"].reshape(1, 1, P, DIFF_HEADS, DIFF_VD),
            r["new_ckvT"].reshape(KV_RANK, P).T[None, None], r["new_kpe"][None, None])
```

```python
import math
from contextlib import ExitStack

import concourse.bass as bass
from concourse import mybir
import numpy as np

F32 = mybir.dt.float32
F32R = mybir.dt.float32r
ALU = mybir.AluOpType
ACT = mybir.ActivationFunctionType
AX = mybir.AxisListType

D = 1024
FF = 2816
P = 128
KD = D // P
KF = FF // P
T = 384
LAT = slice(0, 256)
CTX = slice(256, 384)
SEGS = ((0, CTX), (1, LAT))
NB = T // P
EPS = 1e-6
DEPTH = 2
DIFF_HEADS, DIFF_HD, DIFF_VD = 8, 64, 128
MLA_HEADS, NOPE, ROPE, MLA_VD = 16, 64, 32, 64
QK = NOPE + ROPE
Q_RANK, KV_RANK = 768, 256
DIFF_SCALE = DIFF_HD ** -0.5
MLA_SCALE = QK ** -0.5
LAM_INIT = 0.8 - 0.6 * math.exp(-0.3 * 0)
ROW = 512

_ORDER = [("in", 0, KF, 16 * P), ("out", 0, 2 * KD, 11 * P), ("qkv", 0, 12, 4 * ROW), ("wo", 0, 4, 16 * P),
          ("in", 1, KF, 16 * P), ("out", 1, 2 * KD, 11 * P), ("in", 2, KF, 16 * P), ("out", 2, 2 * KD, 11 * P),
          ("down", 0, 4, 4 * ROW), ("qup", 0, 8, 3 * T), ("kvup", 0, 2, 4 * ROW), ("wo", 1, 4, 16 * P),
          ("in", 3, KF, 16 * P), ("out", 3, 2 * KD, 11 * P)]
PHASE = {}
_n = 0
for _name, _i, _count, _width in _ORDER:
    PHASE[_name, _i] = (_n, _count, _width)
    _n += _count
PANELS = _n
START = 2

PAIRS = DEPTH * 9 * 2
FIRST_PAIRS = 4
PAIR_BASE = {("in", 0): 4, ("out", 0): 15, ("wo", 0): 19, ("in", 1): 21, ("out", 1): 32}


def build_step(nc, d, o):
    ctx = ExitStack()
    with ctx:
        def sem(name):
            return ctx.enter_context(nc.semaphore(name))

        def sb(name, shape, dt=F32, where=ctx):
            return where.enter_context(nc.sbuf_tensor(name, shape, dt))

        x = sb("x", [P, KD, T])
        h_hi = sb("h_hi", [P, KD, T], F32R)
        h_lo = sb("h_lo", [P, KD, T], F32R)
        w_raw = sb("w_raw", [P, 2, 16 * P])
        w_hi = sb("w_hi", [P, 2, 16 * P], F32R)
        w_lo = sb("w_lo", [P, 2, 16 * P], F32R)
        hf = sb("hf", [P, 2, T])
        sqt = sb("sqt", [P, T])
        sqacc = sb("sqacc", [P, T])
        diag = sb("diag", [P, NB, P])
        mrow = sb("mrow", [P, ROW])
        modc = sb("modc", [P, DEPTH * 72, 2])
        bmod = sb("bmod", [P, DEPTH * 72, 2])
        norm_g = sb("norm_g", [P, 6, KD, 2])
        gmul = sb("gmul", [P, KD, 2])
        gres = sb("gres", [P, KD, 2])
        cond = sb("cond", [P, KD, 2])
        scond = sb("scond", [P, KD, 32])
        ones = sb("ones", [P, P])
        ident = sb("ident", [P, P])
        sel = sb("sel", [P, 2])
        epsc = sb("epsc", [P, 1])
        nhalf = sb("nhalf", [P, 8])
        var = sb("var", [P, 8])
        rstd = sb("rstd", [P, 8])
        ssq = sb("ssq", [P, 32])
        rms = sb("rms", [P, 32])
        rinv = sb("rinv", [P, 32])
        mx = sb("mx", [P, 2, 4])
        nm = sb("nm", [P, 2, 4])
        rs = sb("rs", [P, 2, 4])
        ri = sb("ri", [P, 2, 4])
        ri2 = sb("ri2", [P, 2, 2])
        ropes = sb("ropes", [P, 2, 2, 64 + ROPE])
        gq = sb("gq", [P, 2, DIFF_HD])
        gm = sb("gm", [P, 2, QK])
        subg = sb("subg", [P, 2])
        gdown = sb("gdown", [P, KD])
        lamp = sb("lamp", [P, 4, DIFF_HD])
        lamt = sb("lamt", [P, 2, DIFF_HD])
        lams = sb("lams", [P, 2])
        lame = sb("lame", [P, 2])
        neglam = sb("neglam", [P, 2])
        kpw = sb("kpw", [P, KD, ROPE])
        kpw_hi = sb("kpw_hi", [P, KD, ROPE], F32R)
        kpw_lo = sb("kpw_lo", [P, KD, ROPE], F32R)
        t1 = sb("t1", [P, 8, 64])
        t2 = sb("t2", [P, 8, 64])

        early = ExitStack()
        wm = sb("wm", [P, 2, 4 * ROW], where=early)
        with ExitStack() as part:
            wm_first = sb("wm_first", [P, 2 * FIRST_PAIRS, 4 * ROW], where=part)
        with ExitStack() as part:
            g_hi = sb("g_hi", [P, KF, T], F32R, part)
            g_lo = sb("g_lo", [P, KF, T], F32R, part)
            sg = sb("sg", [P, 2, T], where=part)
            prod = sb("prod", [P, 2, T], where=part)
        with ExitStack() as part:
            v_all = sb("v_all", [P, 4, D], where=part)
            dqT = sb("dqT", [P, DIFF_HEADS, T], where=part)
            dkT = sb("dkT", [P, DIFF_HEADS, 4 * P], where=part)
            with ExitStack() as part2:
                qn = sb("qn", [P, NB, D], where=part2)
                kn = sb("kn", [P, 4, D], where=part2)
                sq3 = sb("sq3", [P, NB, ROW], where=part2)
            with ExitStack() as part2:
                e = sb("e", [P, 2, 2, ROW], where=part2)
                a2 = sb("a2", [P, ROW], where=part2)
                a = sb("a", [P, 2, ROW], where=part2)
                aT = sb("aT", [P, 2, ROW], where=part2)
                oraw = sb("oraw", [P, 2, NB, DIFF_VD], where=part2)
                onrm = sb("onrm", [P, 2, NB, DIFF_VD], where=part2)
                osq = sb("osq", [P, NB, DIFF_VD], where=part2)
                oss = sb("oss", [P, 2, NB], where=part2)
                ovar = sb("ovar", [P, 2, NB], where=part2)
                orin = sb("orin", [P, 2, NB], where=part2)
                otf = sb("otf", [P, 2, T], where=part2)
        early.close()
        with ExitStack() as part:
            mv_all = sb("mv_all", [P, 4, D], where=part)
            mqT = sb("mqT", [QK, MLA_HEADS, T], where=part)
            kpe = sb("kpe", [P, 4, ROPE], where=part)
            kpg = sb("kpg", [P, 4, ROPE], where=part)
            kps = sb("kps", [P, 4, ROPE], where=part)
            kpss = sb("kpss", [P, 4], where=part)
            cck = sb("cck", [P, 2, P], where=part)
            cck_hi = sb("cck_hi", [P, 2, P], F32R, part)
            cck_lo = sb("cck_lo", [P, 2, P], F32R, part)
            dss = sb("dss", [P, NB, 3], where=part)
            dtot = sb("dtot", [P, NB], where=part)
            dvar = sb("dvar", [P, 2, NB], where=part)
            drms = sb("drms", [P, 2, NB], where=part)
            drin = sb("drin", [P, 2, NB], where=part)
            with ExitStack() as part2:
                mqn = sb("mqn", [P, NB, MLA_HEADS * QK], where=part2)
                cn = sb("cn", [P, NB, D], where=part2)
                msq3 = sb("msq3", [P, NB, ROW], where=part2)
                ckvf = sb("ckvf", [P, 2, T], where=part2)
            with ExitStack() as part2:
                mkT = sb("mkT", [QK, MLA_HEADS, 4 * P], where=part2)
                with ExitStack() as part3:
                    mkn = sb("mkn", [P, 4, 8, QK], where=part3)
                    msq4 = sb("msq4", [P, 4, ROW], where=part3)
                with ExitStack() as part3:
                    me = sb("me", [P, 2, ROW], where=part3)
                    ma = sb("ma", [P, 2, ROW], where=part3)
                    maT = sb("maT", [P, 2, ROW], where=part3)

        ps = ctx.enter_context(nc.psum_tensor("ps", [P, 8, ROW], F32))

        small_in = sem("small_in")
        x_in = sem("x_in")
        params_in = sem("params_in")
        diff_in = sem("diff_in")
        mla_in = sem("mla_in")
        out_done = sem("out_done")
        y_done = sem("y_done")
        w_loaded = [sem(f"w_loaded{i}") for i in range(2)]
        w_hi_done = sem("w_hi_done")
        w_lo_done = sem("w_lo_done")
        panel_used = sem("panel_used")
        wmf_loaded = [sem(f"wmf_loaded{i}") for i in range(2 * FIRST_PAIRS)]
        wm_loaded = [sem(f"wm_loaded{i}") for i in range(2)]
        pool_consts = sem("pool_consts")
        dve_consts = sem("dve_consts")
        out_ready = sem("out_ready")
        scond_ready = sem("scond_ready")
        rows_ready = sem("rows_ready")
        rows_copied = sem("rows_copied")
        cols_ready = sem("cols_ready")
        cols_done = sem("cols_done")
        res_step = sem("res_step")
        ss_ready = sem("ss_ready")
        var_ready = sem("var_ready")
        rstd_ready = sem("rstd_ready")
        diag_ready = sem("diag_ready")
        bc_ready = sem("bc_ready")
        h_tmp = sem("h_tmp")
        h_aff = sem("h_aff")
        h_hi_done = sem("h_hi_done")
        h_lo_done = sem("h_lo_done")
        gains = sem("gains")
        gate_ready = sem("gate_ready")
        silu_done = sem("silu_done")
        prod_ready = sem("prod_ready")
        g_hi_done = sem("g_hi_done")
        g_ready = sem("g_ready")
        lam_step = sem("lam_step")
        lam_exp = sem("lam_exp")
        dve = sem("dve")
        proj_free = sem("proj_free")
        sq_done = sem("sq_done")
        red_done = sem("red_done")
        rms_done = sem("rms_done")
        heads_ready = sem("heads_ready")
        v_done = sem("v_done")
        tr_ready = sem("tr_ready")
        tr_act = sem("tr_act")
        tr_dve = sem("tr_dve")
        s_ready = sem("s_ready")
        nm_ready = sem("nm_ready")
        exp_done = sem("exp_done")
        a_done = sem("a_done")
        t_ready = sem("t_ready")
        at_done = sem("at_done")
        pv_ready = sem("pv_ready")
        o_done = sem("o_done")
        osq_done = sem("osq_done")
        on_done = sem("on_done")
        oT_ready = sem("oT_ready")
        oT_f = sem("oT_f")
        oT_hi = sem("oT_hi")
        oT_lo = sem("oT_lo")
        ovar_ready = sem("ovar_ready")
        orin_ready = sem("orin_ready")
        kpw_done = sem("kpw_done")
        dss_done = sem("dss_done")
        dvar_ready = sem("dvar_ready")
        kpe_prod = sem("kpe_prod")
        mproj_free = sem("mproj_free")
        kv_keys = sem("kv_keys")
        mkheads = sem("mkheads")
        cn_done = sem("cn_done")
        cT_ready = sem("cT_ready")
        cT_f = sem("cT_f")
        cT_hi = sem("cT_hi")
        cT_lo = sem("cT_lo")
        kpe_ready = sem("kpe_ready")
        cck_step = sem("cck_step")
        msq_done = sem("msq_done")
        mred_done = sem("mred_done")
        mrms_done = sem("mrms_done")
        mheads = sem("mheads")
        kbank_free = sem("kbank_free")
        mv_done = sem("mv_done")
        mtr_ready = sem("mtr_ready")
        mtr_act = sem("mtr_act")
        mtr_dve = sem("mtr_dve")
        ms_ready = sem("ms_ready")
        mnm_ready = sem("mnm_ready")
        mexp_done = sem("mexp_done")
        ma_done = sem("ma_done")
        mt_ready = sem("mt_ready")
        mat_done = sem("mat_done")
        mpv_ready = sem("mpv_ready")
        mo_hi = sem("mo_hi")
        mo_lo = sem("mo_lo")

        def src_of(name, i):
            arr = d[{"in": "w_in", "out": "w_out", "qkv": "w_qkv", "wo": "w_o", "down": "w_down",
                     "qup": "w_qup", "kvup": "w_kvup"}[name]]
            return arr[i] if name in ("in", "out", "wo") else arr

        norms = [("in", 0), ("qkv", 0), ("in", 1), ("in", 2), ("down", 0), ("in", 3)]
        ffns = [("in", i) for i in range(4)]
        residuals = [("out", 0), ("wo", 0), ("out", 1), ("out", 2), ("wo", 1), ("out", 3)]
        RES_BASE = {ph: KD * (n + 1) for n, ph in enumerate(residuals)}

        def mdst(t):
            if t < 12:
                return mqT[:, 4 * (t // 3):4 * (t // 3) + 4, (t % 3) * P:(t % 3 + 1) * P]
            g, slot = divmod(t - 12, 4)
            return mkT[:, 4 * g:4 * g + 4, slot * P:(slot + 1) * P]

        def ddst(t):
            if t < 6:
                return dqT[:, 4 * (t // 3):4 * (t // 3) + 4, (t % 3) * P:(t % 3 + 1) * P]
            g, slot = divmod(t - 6, 4)
            return dkT[:, 4 * g:4 * g + 4, slot * P:(slot + 1) * P]

        PIECES = (((0, 0, (0, 1, 2)), (2, 3 * P, (3,))), ((1, 0, (0, 1, 2)),))

        def pieces(u):
            return PIECES[u % 2]

        def exps_upto(u, per):
            return per * (3 * (u // 2) + (2 if u % 2 == 0 else 3))

        def h_val(n, k):
            return START + KD * n + k + 1

        block = ctx.enter_context(nc.Block())

        @block.sync
        def _(sp):
            def load(name, i, slot, at, n, guarded=True):
                base, count, width = PHASE[name, i]
                if guarded:
                    sp.wait_ge(w_hi_done, n - 1)
                    sp.wait_ge(w_lo_done, n - 1)
                sp.dma_start(w_raw[:, slot, 0:width], src_of(name, i)[at]).then_inc(w_loaded[slot], 16)

            def load_mod(j, guarded=True):
                if guarded:
                    sp.wait_ge(rows_ready, j)
                for kh in range(2):
                    sp.dma_start(wm[:, kh, :], d["w_mod"][2 * j + kh]).then_inc(wm_loaded[kh], 16)

            for j in range(2 * FIRST_PAIRS):
                sp.dma_start(wm_first[:, j, :], d["w_mod"][j]).then_inc(wmf_loaded[j], 16)
            for name, i, count, width in _ORDER:
                base = PHASE[name, i][0]
                per = 4 if name == "out" else 2
                mod = PAIR_BASE.get((name, i))
                first = 0
                if base == 0:
                    for s in range(2):
                        load(name, i, s, s, s, guarded=False)
                    load_mod(FIRST_PAIRS, guarded=False)
                    first = 1
                with sp.Fori(first, count // per) as it:
                    for s in range(per):
                        load(name, i, s % 2, it * per + s, base + it * per + s)
                        if mod is not None and s == 1:
                            load_mod(mod + it)
            for k in range(0, KD, 2):
                sp.wait_ge(res_step, 4 * (START + RES_BASE["out", 3] + k + 2))
                sp.dma_start(o["yT"][k:k + 2].rearrange("k p t -> p k t"), x[:, k:k + 2, :]).then_inc(y_done, 16)
            sp.wait_ge(y_done, 16 * (KD // 2))

        @block.gpsimd
        def _(pool):
            nc.gpsimd.memset(ident[:], 0.0).then_inc(pool_consts, 1)
            nc.gpsimd.memset(ones[:], 1.0).then_inc(pool_consts, 1)
            pool.wait_ge(pool_consts, 2)
            nc.gpsimd.affine_select(out=ident[:], in_=ident[:], compare_op=ALU.not_equal, fill=1.0, base=0,
                                    pattern=[[-1, P]], channel_multiplier=1).then_inc(pool_consts, 1)

            def low(n, slot, width):
                pool.wait_ge(w_hi_done, n + 1)
                nc.gpsimd.tensor_tensor(w_lo[:, slot, 0:width], w_raw[:, slot, 0:width],
                                        w_hi[:, slot, 0:width].bitcast(F32), ALU.subtract).then_inc(w_lo_done, 1)

            def norm(n):
                pool.wait_ge(var_ready, n + 1)
                nc.gpsimd.tensor_tensor(rstd[:, 0:NB], var[:, 0:NB], nhalf[:, 0:NB], ALU.pow).then_inc(rstd_ready, 1)
                with pool.Fori(0, KD // 2) as i:
                    for b in range(2):
                        pool.wait_ge(h_hi_done, i * 2 + (KD * n + b + 1))
                        nc.gpsimd.tensor_tensor(h_lo[:, i * 2 + b, :], hf[:, b, :],
                                                h_hi[:, i * 2 + b, :].bitcast(F32),
                                                ALU.subtract).then_inc(h_lo_done, 1)

            def lows(name, i, frm=1):
                base, count, width = PHASE[name, i]
                if frm == 2:
                    pass
                else:
                    low(base + 1, 1, width)
                with pool.Fori(1, count // 2) as it:
                    for s in range(2):
                        low(base + it * 2 + s, s, width)

            def next_low(name, i):
                base, count, width = PHASE[name, i]
                low(base, 0, width)

            low(0, 0, PHASE["in", 0][2])
            norm(0)
            lows("in", 0)
            next_low("out", 0)
            lows("out", 0)
            next_low("qkv", 0)
            norm(1)
            lows("qkv", 0)
            next_low("wo", 0)
            low(PHASE["wo", 0][0] + 1, 1, PHASE["wo", 0][2])
            for h in range(DIFF_HEADS):
                pool.wait_ge(ovar_ready, h + 1)
                nc.gpsimd.tensor_tensor(orin[:, h % 2, :], ovar[:, h % 2, :], nhalf[:, 0:NB],
                                        ALU.pow).then_inc(orin_ready, 1)
                pool.wait_ge(orin_ready, h + 1)
                if h >= 2:
                    pool.wait_ge(oT_ready, h - 1)
                nc.gpsimd.tensor_tensor(onrm[:, h % 2], oraw[:, h % 2],
                                        orin[:, h % 2, :].unsqueeze(2).to_broadcast([P, NB, DIFF_VD]),
                                        ALU.mult).then_inc(on_done, 1)
                pool.wait_ge(oT_hi, h + 1)
                nc.gpsimd.tensor_tensor(h_lo[:, h, :], otf[:, h % 2, :], h_hi[:, h, :].bitcast(F32),
                                        ALU.subtract).then_inc(oT_lo, 1)
            lows("wo", 0, frm=2)
            next_low("in", 1)
            norm(2)
            lows("in", 1)
            next_low("out", 1)
            lows("out", 1)
            next_low("in", 2)
            norm(3)
            lows("in", 2)
            next_low("out", 2)
            lows("out", 2)
            next_low("down", 0)
            norm(4)
            lows("down", 0)
            next_low("qup", 0)
            low(PHASE["qup", 0][0] + 1, 1, PHASE["qup", 0][2])
            for j in range(KD):
                pool.wait_ge(cT_hi, j + 1)
                src = hf[:, j % 2, :] if j < 6 else ckvf[:, j - 6, :]
                nc.gpsimd.tensor_tensor(h_lo[:, j, :], src, h_hi[:, j, :].bitcast(F32),
                                        ALU.subtract).then_inc(cT_lo, 1)
            lows("qup", 0, frm=2)
            next_low("kvup", 0)
            low(PHASE["kvup", 0][0] + 1, 1, PHASE["kvup", 0][2])
            next_low("wo", 1)
            low(PHASE["wo", 1][0] + 1, 1, PHASE["wo", 1][2])
            lows("wo", 1, frm=2)
            next_low("in", 3)
            norm(5)
            lows("in", 3)
            next_low("out", 3)
            lows("out", 3)

        @block.scalar
        def _(act):
            def high(n, slot, width):
                act.wait_ge(w_loaded[slot], (n - slot) * 8 + 16)
                act.wait_ge(panel_used, n + 1)
                nc.scalar.activation(w_hi[:, slot, 0:width], w_raw[:, slot, 0:width], ACT.Copy).then_inc(w_hi_done, 1)

            def high_of(name, i, k):
                base, count, width = PHASE[name, i]
                high(base + k, k % 2, width)

            def copy_rows(j):
                act.wait_ge(rows_ready, j + 1)
                act.wait_ge(cols_ready, j)
                nc.scalar.activation(mrow[:], ps[:, 6, :], ACT.Copy).then_inc(rows_copied, 1)

            def h_high(n):
                with act.Fori(0, KD // 2) as i:
                    for b in range(2):
                        act.wait_ge(h_aff, i * 4 + (2 * KD * n + 2 * b + 2))
                        nc.scalar.activation(h_hi[:, i * 2 + b, :], hf[:, b, :], ACT.Copy).then_inc(h_hi_done, 1)

            def ffn_in(f):
                base, count, width = PHASE["in", f]
                mod = PAIR_BASE.get(("in", f))

                def pair(i, last):
                    for b in range(2):
                        if b == 1 and last:
                            high_of("out", f, 0)
                        else:
                            high(i * 2 + (base + b + 1), 1 - b, width)
                        act.wait_ge(gate_ready, i * 2 + (KF * f + b + 1))
                        nc.scalar.activation(sg[:, b, :], ps[:, 2 * b, 0:T], ACT.Silu).then_inc(silu_done, 1)
                        if b == 0 and mod is not None:
                            copy_rows(mod + i)
                with act.Fori(0, KF // 2 - 1) as i:
                    pair(i, False)
                pair(KF // 2 - 1, True)

            def ffn_out(f, after):
                base, count, width = PHASE["out", f]
                mod = PAIR_BASE.get(("out", f))

                def four(i, last):
                    for s in range(4):
                        if s == 3 and last:
                            if after:
                                high_of(*after, 0)
                        else:
                            high(i * 4 + (base + s + 1), (s + 1) % 2, width)
                        if s == 1 and mod is not None:
                            copy_rows(mod + i)
                with act.Fori(0, KD // 2 - 1) as i:
                    four(i, False)
                four(KD // 2 - 1, True)

            def wo(l, after):
                for i in range(2):
                    high_of("wo", l, 2) if i == 0 else high_of(*after, 0)
                    if i == 0:
                        if l == 0:
                            copy_rows(PAIR_BASE["wo", 0])
                        high_of("wo", l, 3)
                    elif l == 0:
                        copy_rows(PAIR_BASE["wo", 0] + 1)

            def diff():
                high_of("qkv", 0, 1)
                high_of("qkv", 0, 2)
                for c in range(6):
                    b0 = 3 * (c % 2)
                    base = PHASE["qkv", 0][0]
                    if 2 * c + 3 < 12:
                        high_of("qkv", 0, 2 * c + 3)
                    elif 2 * c + 3 == 13:
                        high_of("wo", 0, 1)
                    act.wait_ge(panel_used, START + base + 2 * c + 2)
                    if c < 4:
                        if c > 0:
                            act.wait_ge(red_done, c)
                        nc.scalar.activation(sq3[:], ps[:, b0:b0 + 3, :], ACT.Square).then_inc(sq_done, 1)
                        act.wait_ge(red_done, c + 1)
                        nc.scalar.activation(rms[:, 0:24], ssq[:, 0:24], ACT.Sqrt, bias=epsc[:, 0:1],
                                             scale=1.0 / DIFF_HD).then_inc(rms_done, 1)
                    else:
                        nc.scalar.activation(v_all[:, 1:4, (c - 4) * ROW:(c - 3) * ROW], ps[:, b0:b0 + 3, :],
                                             ACT.Copy).then_inc(v_done, 1)
                    if 2 * c + 4 < 12:
                        high_of("qkv", 0, 2 * c + 4)
                    elif 2 * c + 4 == 12:
                        high_of("wo", 0, 0)
                act.wait_ge(heads_ready, 4)
                act.dma_start(o["new_k"], kn[:, 3, :]).then_inc(out_done, 16)
                act.wait_ge(v_done, 2)
                act.dma_start(o["new_v"], v_all[:, 3, :]).then_inc(out_done, 16)
                for t in range(0, 14, 2):
                    act.wait_ge(tr_ready, t + 1)
                    nc.scalar.activation(ddst(t), ps[:, 6, :].rearrange("p (h t) -> p h t", h=4),
                                         ACT.Copy).then_inc(tr_act, 1)
                act.wait_ge(lam_step, 2)
                nc.scalar.activation(lame[:], lams[:], ACT.Exp).then_inc(lam_exp, 1)
                act.wait_ge(out_done, 32)
                U = 2 * DIFF_HEADS

                def exps(u):
                    act.wait_ge(nm_ready, u + 1)
                    for j, (qb, at, slots) in enumerate(pieces(u)):
                        cols = slice(at, at + len(slots) * P)
                        for c in range(2):
                            n = 2 * j + c
                            nc.scalar.activation(e[:, u % 2, c, cols], ps[:, 2 * (u % 3) + c, cols], ACT.Exp,
                                                 bias=nm[:, u % 2, n:n + 1], scale=DIFF_SCALE,
                                                 accum_out=rs[:, u % 2, n:n + 1]).then_inc(exp_done, 1)

                def evac_aT(u):
                    n = ROW if u % 2 == 0 else T
                    act.wait_ge(t_ready, u + 1)
                    if u >= 2:
                        act.wait_ge(pv_ready, u - 1)
                    nc.scalar.activation(aT[:, u % 2, 0:n], ps[:, 6, 0:n], ACT.Copy).then_inc(at_done, 1)

                def out_squares(u):
                    act.wait_ge(o_done, u + 1)
                    for qb, at, slots in pieces(u):
                        nc.scalar.activation(osq[:, qb, :], oraw[:, (u // 2) % 2, qb, :], ACT.Square,
                                             accum_out=oss[:, (u // 2) % 2, qb:qb + 1]).then_inc(osq_done, 1)

                def out_head(h):
                    act.wait_ge(oT_f, h + 1)
                    nc.scalar.activation(h_hi[:, h, :], otf[:, h % 2, :], ACT.Copy).then_inc(oT_hi, 1)

                exps(0)
                exps(1)
                for u in range(U + 3):
                    if u + 2 < U:
                        exps(u + 2)
                    if u < U:
                        evac_aT(u)
                    if 1 <= u <= U:
                        out_squares(u - 1)
                    if u >= 4 and u % 2 == 0:
                        out_head(u // 2 - 2)

            def mla():
                base = PHASE["down", 0][0]
                high_of("down", 0, 1)
                high_of("down", 0, 2)
                high_of("down", 0, 3)
                act.wait_ge(panel_used, START + base + 2)
                for blk in range(NB):
                    nc.scalar.activation(msq3[:, blk, 0:ROW], ps[:, blk, :], ACT.Square,
                                         accum_out=dss[:, blk, 0:1]).then_inc(dss_done, 1)
                high_of("qup", 0, 0)
                act.wait_ge(dss_done, 3)
                act.wait_ge(panel_used, START + base + 4)
                for blk in range(NB):
                    nc.scalar.activation(msq3[:, blk, 0:256], ps[:, 3 + blk, 0:256], ACT.Square,
                                         accum_out=dss[:, blk, 1:2]).then_inc(dss_done, 1)
                    nc.scalar.activation(msq3[:, blk, 256:512], ps[:, 3 + blk, 256:512], ACT.Square,
                                         accum_out=dss[:, blk, 2:3]).then_inc(dss_done, 1)
                act.wait_ge(dvar_ready, 1)
                nc.scalar.activation(drms[:], dvar[:], ACT.Sqrt).then_inc(rms_done, 1)
                high_of("qup", 0, 1)
                act.wait_ge(kpe_ready, 1)
                act.dma_start(o["new_kpe"], kpe[:, 3, :]).then_inc(out_done, 16)
                for j in range(KD):
                    act.wait_ge(cT_f, j + 1)
                    src = hf[:, j % 2, :] if j < 6 else ckvf[:, j - 6, :]
                    nc.scalar.activation(h_hi[:, j, :], src, ACT.Copy).then_inc(cT_hi, 1)
                act.dma_start(o["new_ckvT"].rearrange("k p t -> p k t"), ckvf[:, :, CTX]).then_inc(out_done, 16)
                high_of("qup", 0, 2)
                for c in range(4):
                    b0 = 3 * (c % 2)
                    if 2 * c + 3 < 8:
                        high_of("qup", 0, 2 * c + 3)
                    else:
                        high_of("kvup", 0, 2 * c + 3 - 8)
                    act.wait_ge(panel_used, START + PHASE["qup", 0][0] + 2 * c + 2)
                    act.wait_ge(mred_done, c) if c else act.wait_ge(dss_done, 9)
                    nc.scalar.activation(msq3[:, :, 0:T], ps[:, b0:b0 + 3, 0:T], ACT.Square).then_inc(msq_done, 1)
                    act.wait_ge(mred_done, c + 1)
                    nc.scalar.activation(rms[:, 0:12], ssq[:, 0:12], ACT.Sqrt, bias=epsc[:, 0:1],
                                         scale=1.0 / QK).then_inc(mrms_done, 1)
                    if 2 * c + 4 < 8:
                        high_of("qup", 0, 2 * c + 4)
                    elif c == 2:
                        high_of("kvup", 0, 0)
                def evac(t):
                    act.wait_ge(mtr_ready, t + 1)
                    nc.scalar.activation(mdst(t), ps[0:QK, 6, :].rearrange("p (h t) -> p h t", h=4),
                                         ACT.Copy).then_inc(mtr_act, 1)
                for half in range(2):
                    act.wait_ge(kv_keys, half + 1)
                    if half:
                        act.wait_ge(mred_done, 5)
                    nc.scalar.activation(msq4[:], ps[:, 0:4, :], ACT.Square).then_inc(msq_done, 1)
                    act.wait_ge(panel_used, START + PHASE["kvup", 0][0] + half + 1)
                    nc.scalar.activation(mv_all[:, :, half * ROW:(half + 1) * ROW], ps[:, 4:8, :],
                                         ACT.Copy).then_inc(mv_done, 1)
                    act.wait_ge(mred_done, 5 + half)
                    nc.scalar.activation(rms[:, 0:32], ssq[:, 0:32], ACT.Sqrt, bias=epsc[:, 0:1],
                                         scale=1.0 / QK).then_inc(mrms_done, 1)
                    high_of("wo", 1, half)
                    for t in (range(0, 20, 2) if half == 0 else range(20, 28, 2)):
                        evac(t)
                act.wait_ge(out_done, 64)
                U = 2 * MLA_HEADS

                def exps(u):
                    act.wait_ge(mnm_ready, u + 1)
                    for j, (qb, at, slots) in enumerate(pieces(u)):
                        cols = slice(at, at + len(slots) * P)
                        nc.scalar.activation(me[:, u % 2, cols], ps[:, u % 4, cols], ACT.Exp,
                                             bias=nm[:, u % 2, j:j + 1], scale=MLA_SCALE,
                                             accum_out=rs[:, u % 2, j:j + 1]).then_inc(mexp_done, 1)

                def evac_aT(u):
                    n = ROW if u % 2 == 0 else T
                    act.wait_ge(mt_ready, u + 1)
                    if u >= 2:
                        act.wait_ge(mpv_ready, u - 1)
                    nc.scalar.activation(maT[:, u % 2, 0:n], ps[:, 4 + u % 2, 0:n], ACT.Copy).then_inc(mat_done, 1)

                exps(0)
                exps(1)
                for u in range(U):
                    if u + 2 < U:
                        exps(u + 2)
                    evac_aT(u)

            for dst, name in ((cond, "cond"), (bmod, "b_mod"), (norm_g, "norm_g")):
                act.dma_start(dst[:], d[name]).then_inc(small_in, 16)
            act.dma_start(x[:], d["xT"]).then_inc(x_in, 16)
            for dst, name in ((ropes, "ropes"), (gq, "gq"), (gm, "gm"), (subg, "subg"), (gdown, "gdown"),
                              (lamp, "lamp"), (kpw, "kpw")):
                act.dma_start(dst[:], d[name]).then_inc(params_in, 16)
            act.wait_ge(small_in, 48)
            act.wait_ge(dve_consts, 1)
            nc.scalar.activation(scond[:, :, 0:2], cond[:], ACT.Silu).then_inc(scond_ready, 1)
            for j in range(FIRST_PAIRS):
                if j == 0:
                    act.wait_ge(rows_ready, 1)
                    nc.scalar.activation(mrow[:], ps[:, 6, :], ACT.Copy).then_inc(rows_copied, 1)
                else:
                    copy_rows(j)
            high_of("in", 0, 0)
            h_high(0)
            ffn_in(0)
            ffn_out(0, ("qkv", 0))
            act.wait_ge(panel_used, START + PHASE["qkv", 0][0])
            act.dma_start(kn[:, 0, :], d["cache_k"]).then_inc(diff_in, 16)
            act.dma_start(v_all[:, 0, :], d["cache_v"]).then_inc(diff_in, 16)
            h_high(1)
            diff()
            wo(0, ("in", 1))
            h_high(2)
            ffn_in(1)
            ffn_out(1, ("in", 2))
            h_high(3)
            ffn_in(2)
            ffn_out(2, ("down", 0))
            act.wait_ge(panel_used, START + PHASE["down", 0][0])
            act.dma_start(cck[:], d["cache_ckv"]).then_inc(mla_in, 16)
            act.dma_start(kpe[:, 0, :], d["cache_kpe"]).then_inc(mla_in, 16)
            h_high(4)
            mla()
            wo(1, ("in", 3))
            h_high(5)
            ffn_in(3)
            ffn_out(3, None)

        @block.vector
        def _(v):
            nc.vector.memset(scond[:], 0.0).then_inc(dve_consts, 1)
            nc.vector.memset(epsc[:], EPS).then_inc(dve_consts, 1)
            nc.vector.memset(nhalf[:], -0.5).then_inc(dve_consts, 1)
            v.sem_inc(panel_used, START)
            v.sem_inc(prod_ready, START)
            v.sem_inc(h_lo_done, START)
            v.sem_inc(proj_free, START)
            v.sem_inc(res_step, 4 * START)
            v.wait_ge(pool_consts, 3)
            nc.vector.tensor_reduce(sel[:], ident[:].rearrange("p (j c) -> p c j", j=4)[:, 0:2, :], AX.X,
                                    ALU.add).then_inc(dve_consts, 1)

            def squares(i_dc, k, last_inc=1):
                v.wait_ge(res_step, i_dc * 4 + (4 * START + 2))
                nc.vector.tensor_tensor(sqt[:], x[:, k, :], x[:, k, :], ALU.mult).then_inc(res_step, 1)
                v.wait_ge(res_step, i_dc * 4 + (4 * START + 3))
                nc.vector.tensor_tensor(sqacc[:], sqacc[:], sqt[:], ALU.add).then_inc(res_step, 1)

            def mod_cols(j):
                v.wait_ge(cols_ready, j + 1)
                nc.vector.tensor_tensor(modc[:, bass.ds(j * 4, 4), :],
                                        ps[:, 7, 0:8].rearrange("p (c s) -> p c s", c=4),
                                        bmod[:, bass.ds(j * 4, 4), :], ALU.add).then_inc(cols_done, 1)

            def norm(n, layer, part):
                shift, scale = 72 * layer + 24 * part, 72 * layer + 24 * part + 8
                v.wait_ge(cols_done, (scale + 8) // 4)
                nc.vector.scalar_tensor_tensor(gmul[:], modc[:, scale:scale + 8, :], 1.0,
                                               norm_g[:, 3 * layer + part], ALU.add, ALU.mult).then_inc(gains, 1)
                v.wait_ge(ss_ready, n + 1)
                nc.vector.tensor_scalar(var[:, 0:NB], ps[:, 5, 0:NB], 1.0 / D, EPS, ALU.mult,
                                        ALU.add).then_inc(var_ready, 1)
                v.wait_ge(rstd_ready, n + 1)
                for b in range(NB):
                    nc.vector.tensor_scalar(diag[:, b, :], ident[:], rstd[:, b:b + 1], None,
                                            ALU.mult).then_inc(diag_ready, 1)
                v.wait_ge(gains, gain_count[("norm", n)])
                v.wait_ge(bc_ready, n + 1)
                with v.Fori(0, KD // 2) as i:
                    for b in range(2):
                        v.wait_ge(h_lo_done, i * 2 + (KD * n + b + 1))
                        nc.vector.tensor_tensor(hf[:, b, :], x[:, i * 2 + b, :], ps[:, 4, 0:T],
                                                ALU.mult).then_inc(h_tmp, 1)
                        v.wait_ge(h_tmp, i * 2 + (KD * n + b + 1))
                        for s, seg in SEGS:
                            nc.vector.tensor_scalar(hf[:, b, seg], hf[:, b, seg], gmul[:, bass.ds(i * 2 + b, 1), s],
                                                    modc[:, bass.ds(i * 2 + (shift + b), 1), s], ALU.mult,
                                                    ALU.add).then_inc(h_aff, 1)

            gain_count = {}
            for n in range(6):
                gain_count["norm", n] = 1 + 1 + 3 * n
                gain_count["res", n] = 1 + 3 + 3 * n

            def residual(n, layer, part, factor):
                name, f = residuals[n]
                base = PHASE[name, f][0]
                gate = 72 * layer + 24 * part + 16
                mod = PAIR_BASE.get((name, f))
                final = n == 5
                v.wait_ge(cols_done, (gate + 8) // 4)
                nc.vector.tensor_scalar(gres[:], modc[:, gate:gate + 8, :], factor, None,
                                        ALU.mult).then_inc(gains, 1)
                nc.vector.memset(sqacc[:], 0.0).then_inc(gains, 1)
                v.wait_ge(gains, gain_count["res", n])
                rb = RES_BASE[name, f]

                def chunk(k, b, dc):
                    for s, seg in SEGS:
                        nc.vector.scalar_tensor_tensor(x[:, bass.ds(k, 1), seg].rearrange("p a t -> p (a t)"),
                                                       ps[:, 4 + b, seg], gres[:, bass.ds(k, 1), s],
                                                       x[:, bass.ds(k, 1), seg].rearrange("p a t -> p (a t)"),
                                                       ALU.mult, ALU.add).then_inc(res_step, 3 if final and s else 1)
                    if not final:
                        squares(dc, k)

                if name == "out":
                    with v.Fori(0, KD // 2) as i:
                        for b in range(2):
                            v.wait_ge(panel_used, i * 4 + (START + base + 2 * b + 2))
                            chunk(i * 2 + b, b, i * 2 + (rb + b))
                        if mod is not None:
                            mod_cols(mod + i)
                else:
                    with v.Fori(0, 2) as i:
                        for pn in range(2):
                            v.wait_ge(out_ready, i * 2 + (4 * f + pn + 1))
                            chunk(i * 4 + 2 * pn, 0, i * 4 + (rb + 2 * pn))
                            v.wait_ge(panel_used, i * 2 + (START + base + pn + 1))
                            chunk(i * 4 + 2 * pn + 1, 1, i * 4 + (rb + 2 * pn + 1))
                        if mod is not None:
                            mod_cols(mod + i)

            def ffn_in(f):
                base = PHASE["in", f][0]
                mod = PAIR_BASE.get(("in", f))
                with v.Fori(0, KF // 2) as i:
                    for b in range(2):
                        m = KF * f + b + 1
                        v.wait_ge(panel_used, i * 2 + (START + base + b + 1))
                        v.wait_ge(silu_done, i * 2 + m)
                        nc.vector.tensor_tensor(prod[:, b, :], ps[:, 2 * b + 1, 0:T], sg[:, b, :],
                                                ALU.mult).then_inc(prod_ready, 1)
                        v.wait_ge(prod_ready, i * 2 + (START + m))
                        nc.vector.tensor_copy(g_hi[:, i * 2 + b, :], prod[:, b, :]).then_inc(g_hi_done, 1)
                        v.wait_ge(g_hi_done, i * 2 + m)
                        nc.vector.tensor_tensor(g_lo[:, i * 2 + b, :], prod[:, b, :],
                                                g_hi[:, i * 2 + b, :].bitcast(F32), ALU.subtract).then_inc(g_ready, 1)
                    if mod is not None:
                        mod_cols(mod + i)

            count = [0]

            def step(ins):
                count[0] += 1
                ins.then_inc(dve, 1)
                v.wait_ge(dve, count[0])

            def rope(X, groups, half, off, blk):
                r = 4 * half
                cos = ropes[:, 0, blk, off:off + r].unsqueeze(1).to_broadcast([P, groups, r])
                sin = ropes[:, 1, blk, off:off + r].rearrange("p (c h f) -> p c h f", c=2, h=2)
                a1 = t1[:, 0:groups, 0:r]
                b1 = t2[:, 0:groups, 0:r]
                X4 = X.rearrange("p g (c h f) -> p g c h f", c=2, h=2)
                B4 = b1.rearrange("p g (c h f) -> p g c h f", c=2, h=2)
                nc.vector.tensor_tensor(a1, X, cos, ALU.mult)
                for h in range(2):
                    sh = sin[:, :, h, :].unsqueeze(1).to_broadcast([P, groups, 2, half])
                    ins = nc.vector.tensor_tensor(B4[:, :, :, h, :], X4[:, :, :, 1 - h, :], sh, ALU.mult)
                step(ins)
                step(nc.vector.tensor_tensor(X, a1, b1, ALU.add))

            def diff():
                for c in range(4):
                    b0 = 3 * (c % 2)
                    is_k = c // 2
                    v.wait_ge(sq_done, c + 1)
                    nc.vector.tensor_reduce(ssq[:, 0:24].rearrange("p (b g) -> p b g", b=NB),
                                            sq3[:].rearrange("p b (g e) -> p b g e", g=8), AX.X,
                                            ALU.add).then_inc(red_done, 1)
                    v.wait_ge(rms_done, c + 1)
                    step(nc.vector.reciprocal(rinv[:, 0:24], rms[:, 0:24]))
                    to = (kn[:, 1:4, :] if is_k else qn[:])[:, :, (c % 2) * ROW:(c % 2 + 1) * ROW]
                    for b in range(NB):
                        t8 = to[:, b, :].rearrange("p (g e) -> p g e", g=8)
                        nc.vector.tensor_tensor(t8, ps[:, b0 + b, :].rearrange("p (g e) -> p g e", g=8),
                                                rinv[:, 8 * b:8 * b + 8].unsqueeze(2).to_broadcast([P, 8, DIFF_HD]),
                                                ALU.mult).then_inc(*((proj_free, 1) if b == 2 else (dve, 1)))
                    count[0] += 2
                    v.wait_ge(proj_free, START + c + 1)
                    v.wait_ge(dve, count[0])
                    for b in range(NB):
                        t8 = to[:, b, :].rearrange("p (g e) -> p g e", g=8)
                        g8 = gq[:, is_k, :].unsqueeze(1).to_broadcast([P, 8, DIFF_HD])
                        step(nc.vector.tensor_tensor(t8, t8, g8, ALU.mult))
                    for b in range(2):
                        rope(to[:, b, :].rearrange("p (g e) -> p g e", g=8), 8, 16, 0, b)
                    v.sem_inc(heads_ready, 1)
                for t in range(1, 14, 2):
                    v.wait_ge(tr_ready, t + 1)
                    nc.vector.tensor_copy(ddst(t), ps[:, 7, :].rearrange("p (h t) -> p h t", h=4)).then_inc(tr_dve, 1)
                v.wait_ge(lam_exp, 1)
                step(nc.vector.tensor_tensor(neglam[:, 1:2], lame[:, 1:2], lame[:, 0:1], ALU.subtract))
                step(nc.vector.tensor_scalar(neglam[:, 0:1], neglam[:, 1:2], -LAM_INIT, None, ALU.add))
                U = 2 * DIFF_HEADS

                def top(u):
                    v.wait_ge(s_ready, u + 1)
                    for j, (qb, at, slots) in enumerate(pieces(u)):
                        ins = nc.vector.tensor_reduce(mx[:, u % 2, 2 * j:2 * j + 2],
                                                      ps[:, 2 * (u % 3):2 * (u % 3) + 2, at:at + len(slots) * P],
                                                      AX.X, ALU.max)
                    n = 2 * len(pieces(u))
                    step(ins)
                    nc.vector.tensor_scalar(nm[:, u % 2, 0:n], mx[:, u % 2, 0:n], -DIFF_SCALE, None,
                                            ALU.mult).then_inc(nm_ready, 1)

                def mix(u):
                    n = len(pieces(u))
                    v.wait_ge(exp_done, exps_upto(u, 2))
                    step(nc.vector.reciprocal(ri[:, u % 2, 0:2 * n], rs[:, u % 2, 0:2 * n]))
                    step(nc.vector.tensor_scalar(ri2[:, u % 2, 0:n],
                                                 ri[:, u % 2, 0:2 * n].rearrange("p (j c) -> p j c", c=2)[:, :, 1],
                                                 neglam[:, 0:1], None, ALU.mult))
                    for j, (qb, at, slots) in enumerate(pieces(u)):
                        cols = slice(at, at + len(slots) * P)
                        ins = nc.vector.tensor_scalar(a2[:, cols], e[:, u % 2, 1, cols], ri2[:, u % 2, j:j + 1],
                                                      None, ALU.mult)
                    step(ins)
                    if u >= 2:
                        v.wait_ge(t_ready, u - 1)
                    for j, (qb, at, slots) in enumerate(pieces(u)):
                        cols = slice(at, at + len(slots) * P)
                        ins = nc.vector.scalar_tensor_tensor(a[:, u % 2, cols], e[:, u % 2, 0, cols],
                                                             ri[:, u % 2, 2 * j:2 * j + 1], a2[:, cols], ALU.mult,
                                                             ALU.add)
                    ins.then_inc(a_done, 1)

                def out_copy(u):
                    h = u // 2
                    v.wait_ge(pv_ready, u + 1)
                    if h >= 2:
                        v.wait_ge(on_done, h - 1)
                    dst, n = (oraw[:, h % 2, 0::2, :], 2) if u % 2 == 0 else (oraw[:, h % 2, 1:2, :], 1)
                    nc.vector.tensor_copy(dst, ps[:, 7, 0:n * P].rearrange("p (b t) -> p b t", b=n)
                                          ).then_inc(o_done, 1)

                v.wait_ge(out_done, 32)
                top(0)
                top(1)
                for u in range(U + 3):
                    if u < U:
                        mix(u)
                    if u >= 4 and u % 2 == 0:
                        h = u // 2 - 2
                        v.wait_ge(oT_ready, h + 1)
                        if h >= 2:
                            v.wait_ge(oT_lo, h - 1)
                        nc.vector.tensor_scalar(otf[:, h % 2, :], ps[:, 6, 0:T], subg[:, 0:1],
                                                1.0 - LAM_INIT, ALU.mult, ALU.mult).then_inc(oT_f, 1)
                    if u + 2 < U:
                        top(u + 2)
                    if 1 <= u <= U:
                        out_copy(u - 1)
                    if u >= 3 and u % 2 == 1:
                        h = (u - 3) // 2
                        v.wait_ge(osq_done, 3 * h + 3)
                        nc.vector.tensor_scalar(ovar[:, h % 2, :], oss[:, h % 2, :], 1.0 / DIFF_VD, EPS, ALU.mult,
                                                ALU.add).then_inc(ovar_ready, 1)

            def mla():
                v.wait_ge(mla_in, 32)
                nc.vector.tensor_copy(cck_hi[:], cck[:]).then_inc(cck_step, 1)
                v.wait_ge(cck_step, 1)
                nc.vector.tensor_tensor(cck_lo[:], cck[:], cck_hi[:].bitcast(F32), ALU.subtract).then_inc(cck_step, 1)
                v.wait_ge(kpe_prod, 1)
                nc.vector.tensor_copy(kpe[:, 1:4, :], ps[:, 6, 0:NB * ROPE].rearrange("p (b r) -> p b r", b=NB)
                                      ).then_inc(kpe_ready, 1)
                v.wait_ge(kpe_ready, 1)
                v.wait_ge(dss_done, 9)
                step(nc.vector.tensor_tensor(dtot[:], dss[:, :, 0], dss[:, :, 1], ALU.add))
                nc.vector.tensor_scalar(dvar[:, 1, :], dss[:, :, 2], 1.0 / KV_RANK, EPS, ALU.mult, ALU.add)
                step(nc.vector.tensor_scalar(dvar[:, 0, :], dtot[:], 1.0 / Q_RANK, EPS, ALU.mult, ALU.add))
                v.sem_inc(dvar_ready, 1)
                step(nc.vector.tensor_tensor(kps[:], kpe[:], kpe[:], ALU.mult))
                step(nc.vector.tensor_reduce(kpss[:], kps[:], AX.X, ALU.add))
                step(nc.vector.tensor_tensor(kpg[:], kpe[:],
                                             gm[:, 1, NOPE:QK].unsqueeze(1).to_broadcast([P, 4, ROPE]), ALU.mult))
                for b in range(2):
                    rope(kpg[:, 1 + b:2 + b, :], 1, 8, 64, b)
                v.wait_ge(rms_done, 5)
                step(nc.vector.reciprocal(drin[:], drms[:]))
                for b in range(NB):
                    nc.vector.tensor_scalar(cn[:, b, 0:ROW], ps[:, b, :], drin[:, 0, b:b + 1], None,
                                            ALU.mult).then_inc(cn_done, 1)
                    nc.vector.tensor_scalar(cn[:, b, ROW:Q_RANK], ps[:, 3 + b, 0:256], drin[:, 0, b:b + 1], None,
                                            ALU.mult).then_inc(cn_done, 1)
                    nc.vector.tensor_scalar(cn[:, b, Q_RANK:D], ps[:, 3 + b, 256:512], drin[:, 1, b:b + 1], None,
                                            ALU.mult).then_inc(cn_done, 1)
                for j in range(KD):
                    v.wait_ge(cT_ready, j + 1)
                    if 2 <= j < 6:
                        v.wait_ge(cT_lo, j - 1)
                    dst = hf[:, j % 2, :] if j < 6 else ckvf[:, j - 6, :]
                    nc.vector.tensor_scalar(dst, ps[:, 6 + j % 2, 0:T], gdown[:, j:j + 1], None,
                                            ALU.mult).then_inc(cT_f, 1)
                for c in range(4):
                    b0 = 3 * (c % 2)
                    v.wait_ge(msq_done, c + 1)
                    nc.vector.tensor_reduce(ssq[:, 0:12].rearrange("p (b g) -> p b g", b=NB),
                                            msq3[:, :, 0:T].rearrange("p b (g e) -> p b g e", g=4), AX.X,
                                            ALU.add).then_inc(mred_done, 1)
                    v.wait_ge(mrms_done, c + 1)
                    step(nc.vector.reciprocal(rinv[:, 0:12], rms[:, 0:12]))
                    for b in range(NB):
                        t4 = mqn[:, b, c * T:(c + 1) * T].rearrange("p (g e) -> p g e", g=4)
                        ins = nc.vector.tensor_tensor(t4, ps[:, b0 + b, 0:T].rearrange("p (g e) -> p g e", g=4),
                                                      rinv[:, 4 * b:4 * b + 4].unsqueeze(2).to_broadcast([P, 4, QK]),
                                                      ALU.mult)
                        if b < 2:
                            step(ins)
                    ins.then_inc(mproj_free, 1)
                    v.wait_ge(mproj_free, c + 1)
                    for b in range(NB):
                        t4 = mqn[:, b, c * T:(c + 1) * T].rearrange("p (g e) -> p g e", g=4)
                        step(nc.vector.tensor_tensor(t4, t4, gm[:, 0, :].unsqueeze(1).to_broadcast([P, 4, QK]),
                                                     ALU.mult))
                        if b < 2:
                            rope(t4[:, :, NOPE:QK], 4, 8, 64, b)
                    v.sem_inc(mheads, 1)
                for half in range(2):
                    v.wait_ge(msq_done, 5 + half)
                    step(nc.vector.tensor_reduce(ssq[:, 0:32].rearrange("p (b g) -> p b g", b=4),
                                                 msq4[:].rearrange("p b (g e) -> p b g e", g=8), AX.X, ALU.add))
                    s4 = ssq[:, 0:32].rearrange("p (b g) -> p b g", b=4)
                    nc.vector.tensor_tensor(s4, s4, kpss[:].unsqueeze(2).to_broadcast([P, 4, 8]),
                                            ALU.add).then_inc(mred_done, 1)
                    v.wait_ge(mrms_done, 5 + half)
                    step(nc.vector.reciprocal(rinv[:, 0:32], rms[:, 0:32]))
                    if half:
                        v.wait_ge(mtr_ready, 20)
                    else:
                        v.wait_ge(out_done, 64)
                    r4 = rinv[:, 0:32].rearrange("p (b g) -> p b g", b=4)
                    for b in range(4):
                        r8 = r4[:, b, :].unsqueeze(2)
                        ins = nc.vector.tensor_tensor(mkn[:, b, :, 0:NOPE],
                                                      ps[:, b, :].rearrange("p (g e) -> p g e", g=8),
                                                      r8.to_broadcast([P, 8, NOPE]), ALU.mult)
                        if b < 3:
                            step(ins)
                        else:
                            ins.then_inc(kbank_free, 1)
                            v.wait_ge(kbank_free, half + 1)
                        step(nc.vector.tensor_tensor(mkn[:, b, :, NOPE:QK],
                                                     kpg[:, b, :].unsqueeze(1).to_broadcast([P, 8, ROPE]),
                                                     r8.to_broadcast([P, 8, ROPE]), ALU.mult))
                        step(nc.vector.tensor_tensor(mkn[:, b, :, 0:NOPE], mkn[:, b, :, 0:NOPE],
                                                     gm[:, 1, 0:NOPE].unsqueeze(1).to_broadcast([P, 8, NOPE]),
                                                     ALU.mult))
                    v.sem_inc(mkheads, 1)
                    for t in (range(1, 20, 2) if half == 0 else range(21, 28, 2)):
                        v.wait_ge(mtr_ready, t + 1)
                        nc.vector.tensor_copy(mdst(t), ps[0:QK, 7, :].rearrange("p (h t) -> p h t", h=4)
                                              ).then_inc(mtr_dve, 1)
                U = 2 * MLA_HEADS

                def top(u):
                    v.wait_ge(ms_ready, u + 1)
                    for j, (qb, at, slots) in enumerate(pieces(u)):
                        ins = nc.vector.tensor_reduce(mx[:, u % 2, j:j + 1], ps[:, u % 4, at:at + len(slots) * P],
                                                      AX.X, ALU.max)
                    n = len(pieces(u))
                    step(ins)
                    nc.vector.tensor_scalar(nm[:, u % 2, 0:n], mx[:, u % 2, 0:n], -MLA_SCALE, None,
                                            ALU.mult).then_inc(mnm_ready, 1)

                def scale(u):
                    n = len(pieces(u))
                    v.wait_ge(mexp_done, exps_upto(u, 1))
                    step(nc.vector.reciprocal(ri[:, u % 2, 0:n], rs[:, u % 2, 0:n]))
                    if u >= 2:
                        v.wait_ge(mt_ready, u - 1)
                    for j, (qb, at, slots) in enumerate(pieces(u)):
                        cols = slice(at, at + len(slots) * P)
                        ins = nc.vector.tensor_scalar(ma[:, u % 2, cols], me[:, u % 2, cols],
                                                      ri[:, u % 2, j:j + 1], None, ALU.mult)
                    ins.then_inc(ma_done, 1)

                top(0)
                top(1)
                for u in range(U + 2):
                    if u < U:
                        scale(u)
                    if u + 2 < U:
                        top(u + 2)
                    if u >= 5 and u % 4 == 1:
                        pr = u // 4 - 1
                        bank = 6 + pr % 2
                        v.wait_ge(mpv_ready, 4 * pr + 4)
                        nc.vector.tensor_copy(h_hi[:, pr, :], ps[:, bank, 0:T]).then_inc(mo_hi, 1)
                        v.wait_ge(mo_hi, pr + 1)
                        nc.vector.tensor_tensor(h_lo[:, pr, :], ps[:, bank, 0:T],
                                                h_hi[:, pr, :].bitcast(F32), ALU.subtract).then_inc(mo_lo, 1)

            nc.vector.memset(sqacc[:], 0.0).then_inc(gains, 1)
            v.wait_ge(gains, 1)
            v.wait_ge(x_in, 16)
            with v.Fori(0, KD) as k:
                nc.vector.tensor_tensor(sqt[:], x[:, k, :], x[:, k, :], ALU.mult).then_inc(res_step, 3)
                v.wait_ge(res_step, k * 4 + (4 * START + 3))
                nc.vector.tensor_tensor(sqacc[:], sqacc[:], sqt[:], ALU.add).then_inc(res_step, 1)
                v.wait_ge(res_step, k * 4 + (4 * START + 4))
            v.wait_ge(params_in, 112)
            nc.vector.tensor_tensor(lamt[:], lamp[:, 0::2, :], lamp[:, 1::2, :], ALU.mult).then_inc(lam_step, 1)
            v.wait_ge(lam_step, 1)
            nc.vector.tensor_reduce(lams[:], lamt[:], AX.X, ALU.add).then_inc(lam_step, 1)
            nc.vector.tensor_copy(kpw_hi[:], kpw[:]).then_inc(kpw_done, 1)
            v.wait_ge(kpw_done, 1)
            nc.vector.tensor_tensor(kpw_lo[:], kpw[:], kpw_hi[:].bitcast(F32), ALU.subtract).then_inc(kpw_done, 1)
            v.wait_ge(small_in, 48)
            for j in range(FIRST_PAIRS):
                mod_cols(j)
            norm(0, 0, 0)
            ffn_in(0)
            residual(0, 0, 0, 0.5)
            norm(1, 0, 1)
            diff()
            residual(1, 0, 1, 1.0)
            norm(2, 0, 2)
            ffn_in(1)
            residual(2, 0, 2, 0.5)
            norm(3, 1, 0)
            ffn_in(2)
            residual(3, 1, 0, 0.5)
            norm(4, 1, 1)
            mla()
            residual(4, 1, 1, 1.0)
            norm(5, 1, 2)
            ffn_in(3)
            residual(5, 1, 2, 0.5)

        @block.tensor
        def _(pe):
            def mm3(out, l_hi, l_lo, r_hi, r_lo, first, last):
                nc.tensor.matmul(out, l_hi, r_hi, start=first, stop=False)
                nc.tensor.matmul(out, l_hi, r_lo, start=False, stop=False)
                return nc.tensor.matmul(out, l_lo, r_hi, start=False, stop=last)

            def mod_pair(j, panels, loaded):
                for kh in range(2):
                    pe.wait_ge(*loaded[kh])
                    if kh == 0 and not (isinstance(j, int) and j == 0):
                        pe.wait_ge(rows_copied, j)
                    for kk in range(4):
                        mm = nc.tensor.matmul(ps[32 * kk:32 * kk + 32, 6, :], scond[:, 4 * kh + kk, :],
                                              panels[kh][:, kk * ROW:(kk + 1) * ROW], start=kh == 0, stop=kh == 1,
                                              tile_position=(0, 32 * kk))
                mm.then_inc(rows_ready, 1)

            def mod_ring(j):
                mod_pair(j, [wm[:, 0, :], wm[:, 1, :]],
                         [(wm_loaded[kh], (j - (FIRST_PAIRS - 1)) * 16) for kh in range(2)])

            def mod_cols(j):
                pe.wait_ge(rows_copied, j + 1)
                if not (isinstance(j, int) and j == 0):
                    pe.wait_ge(cols_done, j)
                for c in range(4):
                    mm = nc.tensor.matmul(ps[:, 7, 2 * c:2 * c + 2], mrow[:, c * P:(c + 1) * P], sel[:],
                                          start=True, stop=True)
                mm.then_inc(cols_ready, 1)

            def norm(n):
                pe.wait_ge(res_step, 4 * (START + KD * (n + 1)))
                for b in range(NB):
                    mm = nc.tensor.matmul(ps[:, 5, b:b + 1], sqacc[:, b * P:(b + 1) * P], ones[:, 0:1],
                                          start=True, stop=True)
                mm.then_inc(ss_ready, 1)
                pe.wait_ge(diag_ready, NB * (n + 1))
                nc.tensor.matmul(ps[:, 4, 0:T], ones[:], diag[:].rearrange("p b t -> p (b t)"), start=True,
                                 stop=True).then_inc(bc_ready, 1)

            def w_tile(slot, t, n=P):
                return w_hi[:, slot, t * n:(t + 1) * n], w_lo[:, slot, t * n:(t + 1) * n]

            def ffn_in(f, n):
                base = PHASE["in", f][0]
                mod = PAIR_BASE.get(("in", f))
                with pe.Fori(0, KF // 2) as i:
                    for b in range(2):
                        pe.wait_ge(w_lo_done, i * 2 + (base + b + 1))
                        pe.wait_ge(prod_ready, i * 2 + (KF * f + b + 1))
                        for half, done in ((0, gate_ready), (1, panel_used)):
                            for k in range(KD):
                                if b == 0 and half == 0:
                                    pe.wait_ge(h_lo_done, h_val(n, k))
                                mm = mm3(ps[:, 2 * b + half, 0:T], *w_tile(b, KD * half + k), h_hi[:, k, :],
                                         h_lo[:, k, :], k == 0, k == KD - 1)
                            mm.then_inc(done, 1)
                        if mod is not None:
                            (mod_ring if b == 0 else mod_cols)(mod + i)

            def ffn_out(f):
                base = PHASE["out", f][0]
                mod = PAIR_BASE.get(("out", f))
                rb = RES_BASE["out", f]
                kh = KF // 2
                with pe.Fori(0, KD // 2) as i:
                    for b in range(2):
                        pe.wait_ge(res_step, i * 8 + (4 * (rb + b) + 2))
                        for half in range(2):
                            pe.wait_ge(w_lo_done, i * 4 + (base + 2 * b + half + 1))
                            for k in range(kh):
                                if b == 0 and (k == 0 or half and k == kh - 1):
                                    pe.wait_ge(g_ready, KF * f + (kh if not half else KF - 1 if k == 0 else KF))
                                mm = mm3(ps[:, 4 + b, 0:T], *w_tile(half, k), g_hi[:, kh * half + k, :],
                                         g_lo[:, kh * half + k, :], half == 0 and k == 0, half == 1 and k == kh - 1)
                            mm.then_inc(panel_used, 1)
                        if mod is not None:
                            (mod_ring if b == 0 else mod_cols)(mod + i)

            def wo(layer, parts):
                base = PHASE["wo", layer][0]
                mod = PAIR_BASE.get(("wo", layer))
                rb = RES_BASE["wo", layer]
                with pe.Fori(0, 2) as i:
                    for pn in range(2):
                        pe.wait_ge(w_lo_done, i * 2 + (base + pn + 1))
                        for b in range(2):
                            pe.wait_ge(res_step, i * 16 + (4 * (rb + 2 * pn + b) + 2))
                            for k in range(KD):
                                if pn == 0 and b == 0:
                                    pe.wait_ge(parts, k + 1)
                                mm = mm3(ps[:, 4 + b, 0:T], *w_tile(pn, KD * b + k), h_hi[:, k, :], h_lo[:, k, :],
                                         k == 0, k == KD - 1)
                            mm.then_inc(out_ready if b == 0 else panel_used, 1)
                        if mod is not None:
                            (mod_ring if pn == 0 else mod_cols)(mod + i)

            def project(s, kh, per, width, hk, banks, first, last, waits=None):
                for kk in range(per):
                    if waits is not None:
                        pe.wait_ge(waits[0], waits[1] + kh * per + kk)
                    for blk in range(NB):
                        k = hk + kh * per + kk
                        mm = mm3(ps[:, banks + blk, 0:width], h_hi[:, k, blk * P:(blk + 1) * P],
                                 h_lo[:, k, blk * P:(blk + 1) * P], *w_tile(s, kk, width),
                                 first and kk == 0, last and kk == per - 1)
                return mm

            def diff():
                base = PHASE["qkv", 0][0]
                with pe.Fori(0, 3) as i:
                    for c in range(2):
                        pe.wait_ge(proj_free, i * 2 + (c + 1))
                        for kh in range(2):
                            pe.wait_ge(w_lo_done, i * 4 + (base + 2 * c + kh + 1))
                            project(kh, kh, 4, ROW, 0, 3 * c, kh == 0, kh == 1,
                                    (h_lo_done, h_val(1, 0)) if c == 0 else None).then_inc(panel_used, 1)
                for t in range(14):
                    pe.wait_ge(heads_ready, 2 if t < 6 else 4)
                    if t == 6:
                        pe.wait_ge(diff_in, 32)
                    if t >= 2:
                        pe.wait_ge(tr_dve if t % 2 else tr_act, t // 2)
                    for i in range(4):
                        if t < 6:
                            src = qn[:, t % 3, (4 * (t // 3) + i) * P:(4 * (t // 3) + i + 1) * P]
                        else:
                            g, slot = divmod(t - 6, 4)
                            src = kn[:, slot, (4 * g + i) * P:(4 * g + i + 1) * P]
                        mm = nc.tensor.transpose(ps[:, 6 + t % 2, i * P:(i + 1) * P], src, ident[:])
                    mm.then_inc(tr_ready, 1)
                U = 2 * DIFF_HEADS

                def scores(u):
                    h = u // 2
                    if u >= 3:
                        pe.wait_ge(exp_done, exps_upto(u - 3, 2))
                    for qb, at, slots in pieces(u):
                        n = len(slots) * P
                        for c in range(2):
                            r = slice(DIFF_HD * c, DIFF_HD * (c + 1))
                            mm = nc.tensor.matmul(ps[:, 2 * (u % 3) + c, at:at + n], dqT[r, h, qb * P:(qb + 1) * P],
                                                  dkT[r, h, slots[0] * P:slots[0] * P + n], start=True, stop=True)
                    mm.then_inc(s_ready, 1)

                def turn(u):
                    pe.wait_ge(a_done, u + 1)
                    for kb in range(4 if u % 2 == 0 else 3):
                        mm = nc.tensor.transpose(ps[:, 6, kb * P:(kb + 1) * P], a[:, u % 2, kb * P:(kb + 1) * P],
                                                 ident[:])
                    mm.then_inc(t_ready, 1)

                def values(u):
                    h = u // 2
                    pe.wait_ge(at_done, u + 1)
                    if u >= 1:
                        pe.wait_ge(o_done, u)
                    for j, (qb, at, slots) in enumerate(pieces(u)):
                        for kb, slot in enumerate(slots):
                            mm = nc.tensor.matmul(ps[:, 7, j * P:(j + 1) * P],
                                                  aT[:, u % 2, at + kb * P:at + (kb + 1) * P],
                                                  v_all[:, slot, h * DIFF_VD:(h + 1) * DIFF_VD], start=kb == 0,
                                                  stop=kb == len(slots) - 1)
                    mm.then_inc(pv_ready, 1)

                def out_turn(h):
                    pe.wait_ge(on_done, h + 1)
                    for b in range(NB):
                        mm = nc.tensor.transpose(ps[:, 6, b * P:(b + 1) * P], onrm[:, h % 2, b, :], ident[:])
                    mm.then_inc(oT_ready, 1)

                pe.wait_ge(tr_act, 7)
                pe.wait_ge(tr_dve, 7)
                pe.wait_ge(v_done, 2)
                scores(0)
                scores(1)
                for u in range(U + 3):
                    if u + 2 < U:
                        scores(u + 2)
                    if u >= 4 and u % 2 == 0:
                        pe.wait_ge(at_done, min(u, U))
                        out_turn(u // 2 - 2)
                    if 1 <= u <= U:
                        values(u - 1)
                    if u < U:
                        if u >= 4 and u % 2 == 0:
                            pe.wait_ge(oT_f, u // 2 - 1)
                        turn(u)

            def mla():
                base = PHASE["down", 0][0]
                for c in range(2):
                    for kh in range(2):
                        pe.wait_ge(w_lo_done, base + 2 * c + kh + 1)
                        project(kh, kh, 4, ROW, 0, 3 * c, kh == 0, kh == 1,
                                (h_lo_done, h_val(4, 0)) if c == 0 else None).then_inc(panel_used, 1)
                pe.wait_ge(kpw_done, 2)
                for blk in range(NB):
                    for k in range(KD):
                        mm = mm3(ps[:, 6, blk * ROPE:(blk + 1) * ROPE], h_hi[:, k, blk * P:(blk + 1) * P],
                                 h_lo[:, k, blk * P:(blk + 1) * P], kpw_hi[:, k, :], kpw_lo[:, k, :], k == 0,
                                 k == KD - 1)
                mm.then_inc(kpe_prod, 1)
                pe.wait_ge(kpe_ready, 1)
                pe.wait_ge(cn_done, 9)
                for j in range(KD):
                    if j >= 2:
                        pe.wait_ge(cT_f, j - 1)
                    for b in range(NB):
                        mm = nc.tensor.transpose(ps[:, 6 + j % 2, b * P:(b + 1) * P], cn[:, b, j * P:(j + 1) * P],
                                                 ident[:])
                    mm.then_inc(cT_ready, 1)
                base = PHASE["qup", 0][0]
                for c in range(4):
                    if c >= 2:
                        pe.wait_ge(mproj_free, c - 1)
                    for kh in range(2):
                        pe.wait_ge(w_lo_done, base + 2 * c + kh + 1)
                        project(kh, kh, 3, T, 0, 3 * (c % 2), kh == 0, kh == 1,
                                (cT_lo, 1) if c == 0 else None).then_inc(panel_used, 1)
                base = PHASE["kvup", 0][0]

                def up(half, part, bank):
                    for slot in range(4):
                        for kk in range(2):
                            l_hi = cck_hi[:, kk, :] if slot == 0 else h_hi[:, 6 + kk, (slot - 1) * P:slot * P]
                            l_lo = cck_lo[:, kk, :] if slot == 0 else h_lo[:, 6 + kk, (slot - 1) * P:slot * P]
                            mm = mm3(ps[:, bank + slot, :], l_hi, l_lo, *w_tile(half, 2 * part + kk, ROW), kk == 0,
                                     kk == 1)
                    return mm

                def turns(ts):
                    for t in ts:
                        if t >= 2:
                            pe.wait_ge(mtr_dve if t % 2 else mtr_act, t // 2)
                        for i in range(4):
                            if t < 12:
                                h = 4 * (t // 3) + i
                                src = mqn[:, t % 3, h * QK:(h + 1) * QK]
                            else:
                                g, slot = divmod(t - 12, 4)
                                src = mkn[:, slot, 4 * (g % 2) + i, :]
                            mm = nc.tensor.transpose(ps[0:QK, 6 + t % 2, i * P:(i + 1) * P], src, ident[:])
                        mm.then_inc(mtr_ready, 1)

                pe.wait_ge(cck_step, 2)
                pe.wait_ge(cT_f, 8)
                pe.wait_ge(cT_lo, 8)
                for half in range(2):
                    pe.wait_ge(w_lo_done, base + half + 1)
                    if half == 0:
                        pe.wait_ge(mproj_free, 4)
                    else:
                        pe.wait_ge(kbank_free, 1)
                    up(half, 0, 0).then_inc(kv_keys, 1)
                    if half:
                        pe.wait_ge(mtr_act, 10)
                        pe.wait_ge(mtr_dve, 10)
                    up(half, 1, 4).then_inc(panel_used, 1)
                    pe.wait_ge(mv_done, half + 1)
                    if half == 0:
                        pe.wait_ge(mheads, 4)
                        turns(range(12))
                    pe.wait_ge(mkheads, half + 1)
                    turns(range(12 + 8 * half, 20 + 8 * half))
                U = 2 * MLA_HEADS

                def scores(u):
                    h = u // 2
                    if u >= 4:
                        pe.wait_ge(mexp_done, exps_upto(u - 4, 1))
                    for qb, at, slots in pieces(u):
                        n = len(slots) * P
                        mm = nc.tensor.matmul(ps[:, u % 4, at:at + n], mqT[:, h, qb * P:(qb + 1) * P],
                                              mkT[:, h, slots[0] * P:slots[0] * P + n], start=True, stop=True)
                    mm.then_inc(ms_ready, 1)

                def turn(u):
                    pe.wait_ge(ma_done, u + 1)
                    if u >= 2:
                        pe.wait_ge(mat_done, u - 1)
                    for kb in range(4 if u % 2 == 0 else 3):
                        mm = nc.tensor.transpose(ps[:, 4 + u % 2, kb * P:(kb + 1) * P],
                                                 ma[:, u % 2, kb * P:(kb + 1) * P], ident[:])
                    mm.then_inc(mt_ready, 1)

                def values(u):
                    h = u // 2
                    row = MLA_VD * (h % 2)
                    pe.wait_ge(mat_done, u + 1)
                    if u % 4 == 0 and u >= 8:
                        pe.wait_ge(mo_lo, u // 4 - 1)
                    for qb, at, slots in pieces(u):
                        for kb, slot in enumerate(slots):
                            mm = nc.tensor.matmul(ps[row:row + MLA_VD, 6 + (h // 2) % 2, qb * P:(qb + 1) * P],
                                                  mv_all[:, slot, h * MLA_VD:(h + 1) * MLA_VD],
                                                  maT[:, u % 2, at + kb * P:at + (kb + 1) * P], start=kb == 0,
                                                  stop=kb == len(slots) - 1)
                    mm.then_inc(mpv_ready, 1)

                pe.wait_ge(kbank_free, 2)
                pe.wait_ge(mtr_act, 14)
                pe.wait_ge(mtr_dve, 14)
                scores(0)
                scores(1)
                for u in range(U + 1):
                    if u + 2 < U:
                        scores(u + 2)
                    if u >= 1:
                        values(u - 1)
                    if u < U:
                        turn(u)

            pe.wait_ge(pool_consts, 3)
            pe.wait_ge(dve_consts, 4)
            pe.wait_ge(scond_ready, 1)
            for j in range(FIRST_PAIRS):
                mod_pair(j, [wm_first[:, 2 * j, :], wm_first[:, 2 * j + 1, :]],
                         [(wmf_loaded[2 * j + kh], 16) for kh in range(2)])
                mod_cols(j)
            norm(0)
            ffn_in(0, 0)
            ffn_out(0)
            norm(1)
            diff()
            wo(0, oT_lo)
            norm(2)
            ffn_in(1, 2)
            ffn_out(1)
            norm(3)
            ffn_in(2, 3)
            ffn_out(2)
            norm(4)
            mla()
            wo(1, mo_lo)
            norm(5)
            ffn_in(3, 5)
            ffn_out(3)


def rope_table():
    out = np.zeros((2, 2, P, 64 + ROPE), np.float32)
    tok = np.arange(256)
    for off, r in ((0, 64), (64, ROPE)):
        half = r // 4
        n = r // 2
        freqs = (np.float32(10000.0) ** (-np.arange(0, n, 2, dtype=np.float32) / np.float32(n))).astype(np.float32)
        for c, pos in enumerate((tok // 64, tok % 64)):
            ang = (pos.astype(np.float32)[:, None] * freqs[None, :]).astype(np.float32)
            cos, sin = np.cos(ang), np.sin(ang)
            for h in range(2):
                at = off + c * 2 * half + h * half
                out[0, :, :, at:at + half] = cos.reshape(2, P, half)
                out[1, :, :, at:at + half] = (sin if h else -sin).reshape(2, P, half)
    return np.ascontiguousarray(out.transpose(2, 0, 1, 3))


def kernel(x_prompt, x_sample, c, cache_diff_k, cache_diff_v, cache_mla_ckv, cache_mla_kpe, c_ctx,
           w_mod, b_mod, norm_g, ffn_w_in, ffn_w_out,
           diff_w_qkv, diff_q_norm, diff_k_norm, diff_lambda, diff_subln, diff_w_o,
           mla_w_down, mla_q_a_norm, mla_kv_a_norm, mla_w_q_up, mla_w_kv_up, mla_q_norm, mla_k_norm, mla_w_o):
    import concourse.bacc as bacc
    from concourse.bass_utils import run_bass_kernel_spmd

    A = np.asarray

    def every(a, *shape):
        return np.broadcast_to(A(a).reshape((1,) + shape), (P,) + shape)

    tokens = np.concatenate([A(x_sample)[0], A(x_prompt)[0]])
    kv = A(mla_w_kv_up)[0].reshape(2, P, MLA_HEADS, 2, NOPE)
    kv = kv.reshape(2, P, 2, 8, 2, NOPE).transpose(2, 1, 4, 0, 3, 5)
    both = np.stack([A(diff_w_o)[0], A(mla_w_o)[0]])
    arrays = {
        "xT": tokens.reshape(T, KD, P).transpose(2, 1, 0),
        "cond": np.stack([A(c_ctx), A(c)[0]], -1).reshape(KD, P, 2).transpose(1, 0, 2),
        "b_mod": np.broadcast_to(A(b_mod).reshape(DEPTH * 72, P).T[:, :, None], (P, DEPTH * 72, 2)),
        "norm_g": np.broadcast_to(A(norm_g).reshape(6, KD, P).transpose(2, 0, 1)[..., None], (P, 6, KD, 2)),
        "w_mod": A(w_mod).reshape(DEPTH, 2, 4, P, 18, ROW).transpose(0, 4, 1, 3, 2, 5).reshape(2 * PAIRS, P, 4 * ROW),
        "w_in": A(ffn_w_in).reshape(4, KD, P, 2, KF, P).transpose(0, 4, 2, 3, 1, 5).reshape(4, KF, P, 16 * P),
        "w_out": A(ffn_w_out).reshape(4, 2, KF // 2, P, KD, P).transpose(0, 4, 1, 3, 2, 5)
                  .reshape(4, 2 * KD, P, 11 * P),
        "w_qkv": A(diff_w_qkv)[0].reshape(2, 4, P, 6, ROW).transpose(3, 0, 2, 1, 4).reshape(12, P, 4 * ROW),
        "w_o": both.reshape(2, KD, P, 4, 2, P).transpose(0, 3, 2, 4, 1, 5).reshape(2, 4, P, 16 * P),
        "w_down": A(mla_w_down)[0, :, :D].reshape(2, 4, P, 2, ROW).transpose(3, 0, 2, 1, 4).reshape(4, P, 4 * ROW),
        "kpw": A(mla_w_down)[0, :, D:].reshape(KD, P, ROPE).transpose(1, 0, 2),
        "w_qup": A(mla_w_q_up)[0].reshape(2, 3, P, 4, T).transpose(3, 0, 2, 1, 4).reshape(8, P, 3 * T),
        "w_kvup": kv.reshape(2, P, 4 * ROW),
        "ropes": rope_table(),
        "gq": every(np.stack([A(diff_q_norm)[0], A(diff_k_norm)[0]]), 2, DIFF_HD),
        "gm": every(np.stack([A(mla_q_norm)[0], A(mla_k_norm)[0]]), 2, QK),
        "subg": np.broadcast_to(A(diff_subln)[0][:, None], (P, 2)),
        "gdown": np.concatenate([A(mla_q_a_norm)[0], A(mla_kv_a_norm)[0]]).reshape(KD, P).T,
        "lamp": every(diff_lambda, 4, DIFF_HD),
        "cache_k": A(cache_diff_k)[0, 0].reshape(P, D),
        "cache_v": A(cache_diff_v)[0, 0].reshape(P, D),
        "cache_ckv": A(cache_mla_ckv)[0, 0].reshape(P, 2, P).transpose(2, 1, 0),
        "cache_kpe": A(cache_mla_kpe)[0, 0],
    }
    arrays = {k: np.ascontiguousarray(a) for k, a in arrays.items()}
    outs = {"yT": (KD, P, T), "new_k": (P, D), "new_v": (P, D), "new_ckvT": (2, P, P), "new_kpe": (P, ROPE)}
    nc = bacc.Bacc("TRN2", target_bir_lowering=False, num_devices=1)
    d = {k: nc.dram_tensor("in_" + k, a.shape, F32, kind="ExternalInput").ap() for k, a in arrays.items()}
    o = {k: nc.dram_tensor("out_" + k, s, F32, kind="ExternalOutput").ap() for k, s in outs.items()}
    build_step(nc, d, o)
    r = run_bass_kernel_spmd(nc, [{"in_" + k: a for k, a in arrays.items()}], core_ids=[0]).results[0]
    r = {k: r["out_" + k] for k in outs}
    y = r["yT"].reshape(D, T).T
    return (y[None, 256:], y[None, :256],
            r["new_k"].reshape(1, 1, P, DIFF_HEADS, 2, DIFF_HD), r["new_v"].reshape(1, 1, P, DIFF_HEADS, DIFF_VD),
            r["new_ckvT"].reshape(KV_RANK, P).T[None, None], r["new_kpe"][None, None])
```

```python
import math
from contextlib import ExitStack

import concourse.bass as bass
from concourse import mybir
import numpy as np

F32 = mybir.dt.float32
F32R = mybir.dt.float32r
ALU = mybir.AluOpType
ACT = mybir.ActivationFunctionType
AX = mybir.AxisListType

D = 1024
FF = 2816
P = 128
KD = D // P
KF = FF // P
T = 384
LAT = slice(0, 256)
CTX = slice(256, 384)
SEGS = ((0, CTX), (1, LAT))
NB = T // P
EPS = 1e-6
DEPTH = 2
DIFF_HEADS, DIFF_HD, DIFF_VD = 8, 64, 128
MLA_HEADS, NOPE, ROPE, MLA_VD = 16, 64, 32, 64
QK = NOPE + ROPE
Q_RANK, KV_RANK = 768, 256
DIFF_SCALE = DIFF_HD ** -0.5
MLA_SCALE = QK ** -0.5
LAM_INIT = 0.8 - 0.6 * math.exp(-0.3 * 0)
ROW = 512

_ORDER = [("in", 0, KF, 16 * P), ("out", 0, 2 * KD, 11 * P), ("qkv", 0, 12, 4 * ROW), ("wo", 0, 4, 16 * P),
          ("in", 1, KF, 16 * P), ("out", 1, 2 * KD, 11 * P), ("in", 2, KF, 16 * P), ("out", 2, 2 * KD, 11 * P),
          ("down", 0, 4, 4 * ROW), ("qup", 0, 8, 3 * T), ("kvup", 0, 2, 4 * ROW), ("wo", 1, 4, 16 * P),
          ("in", 3, KF, 16 * P), ("out", 3, 2 * KD, 11 * P)]
PHASE = {}
_n = 0
for _name, _i, _count, _width in _ORDER:
    PHASE[_name, _i] = (_n, _count, _width)
    _n += _count
PANELS = _n
START = 2
H_START = 4

MODS = DEPTH * 9 * KD
FIRST_MODS = 2 * KD
MOD_PLAN = {("in", 0): 4, ("out", 0): 2, ("in", 1): 2, ("out", 1): 4, ("in", 2): 2, ("out", 2): 4}
MODS_OF = {}
_n = FIRST_MODS
for _ph, _per in MOD_PLAN.items():
    MODS_OF[_ph] = (_n, _per)
    _n += _per * (KF if _ph[0] == "in" else KD) // 2
assert _n == MODS


def build_step(nc, d, o):
    ctx = ExitStack()
    with ctx:
        def sem(name):
            return ctx.enter_context(nc.semaphore(name))

        def sb(name, shape, dt=F32, where=ctx):
            return where.enter_context(nc.sbuf_tensor(name, shape, dt))

        x = sb("x", [P, KD, T])
        h_hi = sb("h_hi", [P, KD, T], F32R)
        h_lo = sb("h_lo", [P, KD, T], F32R)
        w_raw = sb("w_raw", [P, 2, 16 * P])
        w_hi = sb("w_hi", [P, 2, 16 * P], F32R)
        w_lo = sb("w_lo", [P, 2, 16 * P], F32R)
        hf = sb("hf", [P, 4, T])
        sg, prod = hf[:, 0:2, :], hf[:, 2:4, :]
        square = hf[:, 0, :]
        t1, t2 = (hf[:].rearrange("p a t -> p (a t)")[:, at:at + 512].rearrange("p (g e) -> p g e", g=8)
                  for at in (0, 2 * T))
        sqacc = sb("sqacc", [P, T])
        diag = sb("diag", [P, NB, P])
        var = sb("var", [P, NB])
        rstd = sb("rstd", [P, NB])
        modc = sb("modc", [P, DEPTH * 72, 2])
        bmod = sb("bmod", [P, DEPTH * 72, 2])
        norm_g = sb("norm_g", [P, 6, KD, 2])
        gmul = sb("gmul", [P, KD, 2])
        gres = sb("gres", [P, KD, 2])
        ones = sb("ones", [P, P])
        ident = sb("ident", [P, P])
        epsc = sb("epsc", [P, 1])
        nhalf = sb("nhalf", [P, 8])
        ssq = sb("ssq", [P, 32])
        rms = sb("rms", [P, 32])
        rinv = sb("rinv", [P, 32])
        mx = sb("mx", [P, 3, 4])
        nm = sb("nm", [P, 3, 4])
        rs = sb("rs", [P, 3, 4])
        ri = sb("ri", [P, 3, 4])
        ri2 = sb("ri2", [P, 3, 2])
        ropes = sb("ropes", [P, 2, 2, 64 + ROPE])
        gq = sb("gq", [P, 2, DIFF_HD])
        gm = sb("gm", [P, 2, QK])
        subg = sb("subg", [P, 2])
        gdown = sb("gdown", [P, KD])
        lamp = sb("lamp", [P, 4, DIFF_HD])
        lamt = sb("lamt", [P, 2, DIFF_HD])
        lams = sb("lams", [P, 2])
        lame = sb("lame", [P, 2])
        neglam = sb("neglam", [P, 2])
        kpw = sb("kpw", [P, KD, ROPE])
        kpw_hi = sb("kpw_hi", [P, KD, ROPE], F32R)
        kpw_lo = sb("kpw_lo", [P, KD, ROPE], F32R)

        early = ExitStack()
        cond = sb("cond", [P, 2, D], where=early)
        ffn = ExitStack()
        wm = sb("wm", [P, 4, D], where=ffn)
        mod_prod = sb("mod_prod", [P, D], where=ffn)
        with ExitStack() as part:
            wm_first = sb("wm_first", [P, FIRST_MODS, D], where=part)
        with ExitStack() as part:
            g_hi = sb("g_hi", [P, KF, T], F32R, part)
            g_lo = sb("g_lo", [P, KF, T], F32R, part)
        ffn.close()
        with ExitStack() as part:
            v_all = sb("v_all", [P, 4, D], where=part)
            dqT = sb("dqT", [P, DIFF_HEADS, T], where=part)
            dkT = sb("dkT", [P, DIFF_HEADS, 4 * P], where=part)
            with ExitStack() as part2:
                qn = sb("qn", [P, NB, D], where=part2)
                kn = sb("kn", [P, 4, D], where=part2)
                sq3 = sb("sq3", [P, NB, ROW], where=part2)
            with ExitStack() as part2:
                e = sb("e", [P, 3, 2, ROW], where=part2)
                a2 = sb("a2", [P, ROW], where=part2)
                a = sb("a", [P, 2, ROW], where=part2)
                aT = sb("aT", [P, 2, ROW], where=part2)
                oraw = sb("oraw", [P, 2, NB, DIFF_VD], where=part2)
                onrm = sb("onrm", [P, 2, NB, DIFF_VD], where=part2)
                osq = sb("osq", [P, NB, DIFF_VD], where=part2)
                oss = sb("oss", [P, 2, NB], where=part2)
                ovar = sb("ovar", [P, 2, NB], where=part2)
                orin = sb("orin", [P, 2, NB], where=part2)
                otf = sb("otf", [P, 2, T], where=part2)
        early.close()
        with ExitStack() as part:
            mv_all = sb("mv_all", [P, 4, D], where=part)
            mqT = sb("mqT", [QK, MLA_HEADS, T], where=part)
            kpe = sb("kpe", [P, 4, ROPE], where=part)
            kpg = sb("kpg", [P, 4, ROPE], where=part)
            kps = sb("kps", [P, 4, ROPE], where=part)
            kpss = sb("kpss", [P, 4], where=part)
            cck = sb("cck", [P, 2, P], where=part)
            cck_hi = sb("cck_hi", [P, 2, P], F32R, part)
            cck_lo = sb("cck_lo", [P, 2, P], F32R, part)
            dss = sb("dss", [P, NB, 3], where=part)
            dtot = sb("dtot", [P, NB], where=part)
            dvar = sb("dvar", [P, 2, NB], where=part)
            drin = sb("drin", [P, 2, NB], where=part)
            with ExitStack() as part2:
                mqn = sb("mqn", [P, NB, MLA_HEADS * QK], where=part2)
                cn = sb("cn", [P, NB, D], where=part2)
                msq3 = sb("msq3", [P, NB, ROW], where=part2)
                ddiag = mqn[:, 0, 0:2 * T]
                kpT = mqn[0:ROPE, 2, 0:T]
                drb = mqn[:, 1, 0:2 * T].rearrange("p (r t) -> p r t", r=2)
                ckvf = sb("ckvf", [P, 2, T], where=part2)
            with ExitStack() as part2:
                mkT = sb("mkT", [P, MLA_HEADS, 4 * P], where=part2)
                msq4 = mkT[:, 12:16, :]
                with ExitStack() as part3:
                    mkn = sb("mkn", [P, 2, 4, 8, QK], where=part3)
                with ExitStack() as part3:
                    me = sb("me", [P, 3, ROW], where=part3)
                    ma = sb("ma", [P, 2, ROW], where=part3)
                    maT = sb("maT", [P, 2, ROW], where=part3)

        squares_all = wm[:].rearrange("p a b -> p (a b)")[:, 0:KD * T].rearrange("p (k t) -> p k t", k=KD)
        ps = ctx.enter_context(nc.psum_tensor("ps", [P, 8, ROW], F32))

        small_in = sem("small_in")
        cond_in = sem("cond_in")
        x_in = sem("x_in")
        params_in = sem("params_in")
        diff_in = sem("diff_in")
        mla_in = sem("mla_in")
        out_done = sem("out_done")
        y_done = sem("y_done")
        w_loaded = [sem(f"w_loaded{i}") for i in range(2)]
        w_hi_done = sem("w_hi_done")
        w_lo_done = sem("w_lo_done")
        panel_used = sem("panel_used")
        wmf_loaded = [sem(f"wmf_loaded{i}") for i in range(FIRST_MODS)]
        wm_loaded = {(ph, q): sem(f"wm_loaded_{ph[0]}{ph[1]}_{q}")
                     for ph, (_, mods) in MODS_OF.items() for q in range(mods)}
        pool_consts = sem("pool_consts")
        dve_consts = sem("dve_consts")
        cond_ready = sem("cond_ready")
        out_ready = sem("out_ready")
        first_prod = sem("first_prod")
        first_sum = sem("first_sum")
        x_squared = sem("x_squared")
        mod_step = sem("mod_step")
        res_step = sem("res_step")
        ss_ready = sem("ss_ready")
        var_ready = sem("var_ready")
        rstd_ready = sem("rstd_ready")
        diag_ready = sem("diag_ready")
        bc_ready = sem("bc_ready")
        h_tmp = sem("h_tmp")
        h_aff = sem("h_aff")
        h_hi_done = sem("h_hi_done")
        h_lo_done = sem("h_lo_done")
        gains = sem("gains")
        silu_done = sem("silu_done")
        prod_ready = sem("prod_ready")
        g_hi_done = sem("g_hi_done")
        g_ready = sem("g_ready")
        lam_step = sem("lam_step")
        lam_exp = sem("lam_exp")
        dve = sem("dve")
        proj_free = sem("proj_free")
        sq_done = sem("sq_done")
        red_done = sem("red_done")
        rms_done = sem("rms_done")
        heads_ready = sem("heads_ready")
        v_done = sem("v_done")
        tr_ready = sem("tr_ready")
        tr_done = sem("tr_done")
        k_out = sem("k_out")
        s_ready = sem("s_ready")
        nm_ready = sem("nm_ready")
        exp_done = sem("exp_done")
        a_done = sem("a_done")
        t_ready = sem("t_ready")
        at_done = sem("at_done")
        pv_ready = sem("pv_ready")
        o_done = sem("o_done")
        osq_done = sem("osq_done")
        on_done = sem("on_done")
        oT_ready = sem("oT_ready")
        oT_f = sem("oT_f")
        oT_hi = sem("oT_hi")
        oT_lo = sem("oT_lo")
        ovar_ready = sem("ovar_ready")
        orin_ready = sem("orin_ready")
        kpw_done = sem("kpw_done")
        dvar_ready = sem("dvar_ready")
        drin_ready = sem("drin_ready")
        ddiag_ready = sem("ddiag_ready")
        dbc_ready = sem("dbc_ready")
        drb_ready = sem("drb_ready")
        kpe_prod = sem("kpe_prod")
        kpT_ready = sem("kpT_ready")
        kpe_turned = sem("kpe_turned")
        mproj_free = sem("mproj_free")
        kv_keys = sem("kv_keys")
        kv_values = sem("kv_values")
        mkheads = sem("mkheads")
        cn_done = sem("cn_done")
        cT_ready = sem("cT_ready")
        cT_f = sem("cT_f")
        cT_hi = sem("cT_hi")
        cT_lo = sem("cT_lo")
        kpe_ready = sem("kpe_ready")
        cck_step = sem("cck_step")
        msq_done = sem("msq_done")
        mred_done = sem("mred_done")
        mrms_done = sem("mrms_done")
        mheads = sem("mheads")
        kbank_free = sem("kbank_free")
        mv_done = sem("mv_done")
        mtr_ready = sem("mtr_ready")
        mtr_act = sem("mtr_act")
        mtr_dve = sem("mtr_dve")
        ms_ready = sem("ms_ready")
        mnm_ready = sem("mnm_ready")
        mexp_done = sem("mexp_done")
        ma_done = sem("ma_done")
        mt_ready = sem("mt_ready")
        mat_done = sem("mat_done")
        mpv_ready = sem("mpv_ready")
        mo_hi = sem("mo_hi")
        mo_lo = sem("mo_lo")

        def src_of(name, i):
            arr = d[{"in": "w_in", "out": "w_out", "qkv": "w_qkv", "wo": "w_o", "down": "w_down",
                     "qup": "w_qup", "kvup": "w_kvup"}[name]]
            return arr[i] if name in ("in", "out", "wo") else arr

        norms = [("in", 0), ("qkv", 0), ("in", 1), ("in", 2), ("down", 0), ("in", 3)]
        residuals = [("out", 0), ("wo", 0), ("out", 1), ("out", 2), ("wo", 1), ("out", 3)]
        RES_BASE = {ph: KD * (n + 1) for n, ph in enumerate(residuals)}

        C_BANK = (0, 1, 2, 6, 7, 3, 6, 7)

        def mdst(t):
            if t < 12:
                return mqT[:, 4 * (t // 3):4 * (t // 3) + 4, (t % 3) * P:(t % 3 + 1) * P]
            g, slot = divmod(t - 12, 4)
            return mkT[0:QK, 4 * g:4 * g + 4, slot * P:(slot + 1) * P]

        def ddst(t):
            if t < 6:
                return dqT[:, 4 * (t // 3):4 * (t // 3) + 4, (t % 3) * P:(t % 3 + 1) * P]
            g, slot = divmod(t - 6, 4)
            return dkT[:, 4 * g:4 * g + 4, slot * P:(slot + 1) * P]

        PIECES = (((0, 0, (0, 1, 2)), (2, 3 * P, (3,))), ((1, 0, (0, 1, 2)),))

        def pieces(u):
            return PIECES[u % 2]

        def exps_upto(u, per):
            return per * (3 * (u // 2) + (2 if u % 2 == 0 else 3))

        def h_val(n, k):
            return H_START + KD * n + k + 1

        block = ctx.enter_context(nc.Block())

        @block.sync
        def _(sp):
            def load(name, i, slot, at, n, guarded=True):
                base, count, width = PHASE[name, i]
                if guarded:
                    sp.wait_ge(w_hi_done, n - 1)
                    sp.wait_ge(w_lo_done, n - 1)
                sp.dma_start(w_raw[:, slot, 0:width], src_of(name, i)[at]).then_inc(w_loaded[slot], 16)

            def load_mods(ph, it):
                first_mod, mods = MODS_OF.get(ph, (0, 0))
                if ph == ("in", 0) and isinstance(it, int):
                    sp.wait_ge(first_sum, KD)
                if mods:
                    sp.wait_ge(mod_step, it * (2 * mods) + 2 * first_mod)
                for q in range(mods):
                    sp.dma_start(wm[:, q, :], d["w_mod"][it * mods + (first_mod + q)]
                                 ).then_inc(wm_loaded[ph, q], 16)

            sp.dma_start(cond[:], d["cond"]).then_inc(cond_in, 16)
            sp.dma_start(x[:], d["xT"]).then_inc(x_in, 16)
            for k in range(KD):
                for q in (KD + k, k):
                    sp.dma_start(wm_first[:, q, :], d["w_mod"][q]).then_inc(wmf_loaded[q], 16)
                if k in (1, 5):
                    load("in", 0, k // 4, k // 4, k // 4, guarded=False)
            for name, i, count, width in _ORDER:
                base = PHASE[name, i][0]
                per = 4 if name == "out" else 2
                if (name, i) == ("in", 1):
                    sp.wait_ge(out_done, 16)
                for s in range(per):
                    if base > 0:
                        load(name, i, s % 2, s, base + s)
                    if s == 1:
                        load_mods((name, i), 0)
                if count > per:
                    with sp.Fori(1, count // per) as it:
                        for s in range(per):
                            load(name, i, s % 2, it * per + s, base + it * per + s)
                            if s == 1:
                                load_mods((name, i), it)
            for k in range(0, KD, 2):
                sp.wait_ge(res_step, 4 * (START + RES_BASE["out", 3] + k + 2))
                sp.dma_start(o["yT"][k:k + 2].rearrange("k p t -> p k t"), x[:, k:k + 2, :]).then_inc(y_done, 16)
            sp.wait_ge(y_done, 16 * (KD // 2))

        @block.gpsimd
        def _(pool):
            nc.gpsimd.memset(ident[:], 0.0).then_inc(pool_consts, 1)
            nc.gpsimd.memset(ones[:], 1.0).then_inc(pool_consts, 1)
            pool.wait_ge(pool_consts, 2)
            nc.gpsimd.affine_select(out=ident[:], in_=ident[:], compare_op=ALU.not_equal, fill=1.0, base=0,
                                    pattern=[[-1, P]], channel_multiplier=1).then_inc(pool_consts, 1)

            def low(n, slot, width):
                pool.wait_ge(w_hi_done, n + 1)
                nc.gpsimd.tensor_tensor(w_lo[:, slot, 0:width], w_raw[:, slot, 0:width],
                                        w_hi[:, slot, 0:width].bitcast(F32), ALU.subtract).then_inc(w_lo_done, 1)

            def first_product(k):
                pool.wait_ge(wmf_loaded[k], 16)
                if k == 0:
                    pool.wait_ge(cond_ready, 1)
                if k >= 2:
                    pool.wait_ge(first_sum, k - 1)
                nc.gpsimd.tensor_tensor(wm[:, 2 + k % 2, :], wm_first[:, k, :], cond[:, 1, :],
                                        ALU.mult).then_inc(first_prod, 1)

            def norm(n):
                pool.wait_ge(var_ready, n + 1)
                nc.gpsimd.tensor_tensor(rstd[:], var[:], nhalf[:, 0:NB], ALU.pow).then_inc(rstd_ready, 1)
                base, count, width = PHASE[norms[n]]
                if n == 0:
                    for k in range(KD + 1):
                        if k < KD:
                            first_product(k)
                        if k == 1:
                            low(0, 0, width)
                        if k > 0:
                            pool.wait_ge(h_hi_done, k)
                            nc.gpsimd.tensor_tensor(h_lo[:, k - 1, :], hf[:, (k - 1) % 4, :],
                                                    h_hi[:, k - 1, :].bitcast(F32),
                                                    ALU.subtract).then_inc(h_lo_done, 1)
                    low(1, 1, width)
                    return
                low(base + 1, 1, width)
                with pool.Fori(0, 2) as i:
                    for b in range(4):
                        pool.wait_ge(h_hi_done, i * 4 + (KD * n + b + 1))
                        nc.gpsimd.tensor_tensor(h_lo[:, i * 4 + b, :], hf[:, b, :],
                                                h_hi[:, i * 4 + b, :].bitcast(F32),
                                                ALU.subtract).then_inc(h_lo_done, 1)

            def lows(name, i):
                base, count, width = PHASE[name, i]
                with pool.Fori(1, count // 2) as it:
                    for s in range(2):
                        low(base + it * 2 + s, s, width)

            def second_low(name, i):
                base, count, width = PHASE[name, i]
                low(base + 1, 1, width)

            def next_low(name, i):
                base, count, width = PHASE[name, i]
                low(base, 0, width)

            norm(0)
            lows("in", 0)
            next_low("out", 0)
            second_low("out", 0)
            lows("out", 0)
            next_low("qkv", 0)
            norm(1)
            lows("qkv", 0)
            next_low("wo", 0)
            second_low("wo", 0)
            for h in range(DIFF_HEADS + 1):
                if h < DIFF_HEADS:
                    pool.wait_ge(ovar_ready, h + 1)
                    nc.gpsimd.tensor_tensor(orin[:, h % 2, :], ovar[:, h % 2, :], nhalf[:, 0:NB],
                                            ALU.pow).then_inc(orin_ready, 1)
                    pool.wait_ge(orin_ready, h + 1)
                    if h >= 2:
                        pool.wait_ge(oT_ready, h - 1)
                    nc.gpsimd.tensor_tensor(onrm[:, h % 2], oraw[:, h % 2],
                                            orin[:, h % 2, :].unsqueeze(2).to_broadcast([P, NB, DIFF_VD]),
                                            ALU.mult).then_inc(on_done, 1)
                if h >= 1:
                    pool.wait_ge(oT_hi, h)
                    nc.gpsimd.tensor_tensor(h_lo[:, h - 1, :], otf[:, (h - 1) % 2, :],
                                            h_hi[:, h - 1, :].bitcast(F32), ALU.subtract).then_inc(oT_lo, 1)
            lows("wo", 0)
            next_low("in", 1)
            norm(2)
            lows("in", 1)
            next_low("out", 1)
            second_low("out", 1)
            lows("out", 1)
            next_low("in", 2)
            norm(3)
            lows("in", 2)
            next_low("out", 2)
            second_low("out", 2)
            lows("out", 2)
            next_low("down", 0)
            norm(4)
            lows("down", 0)
            next_low("qup", 0)
            pool.wait_ge(dvar_ready, 1)
            nc.gpsimd.tensor_tensor(drin[:].rearrange("p a b -> p (a b)"), dvar[:].rearrange("p a b -> p (a b)"),
                                    nhalf[:, 0:2 * NB], ALU.pow).then_inc(drin_ready, 1)
            second_low("qup", 0)
            for j in range(KD):
                pool.wait_ge(cT_hi, j + 1)
                src = hf[:, j % 4, :] if j < 6 else ckvf[:, j - 6, :]
                nc.gpsimd.tensor_tensor(h_lo[:, j, :], src, h_hi[:, j, :].bitcast(F32),
                                        ALU.subtract).then_inc(cT_lo, 1)
            lows("qup", 0)
            next_low("kvup", 0)
            second_low("kvup", 0)
            next_low("wo", 1)
            second_low("wo", 1)
            lows("wo", 1)
            next_low("in", 3)
            norm(5)
            lows("in", 3)
            next_low("out", 3)
            second_low("out", 3)
            lows("out", 3)

        @block.scalar
        def _(act):
            def high(n, slot, width):
                act.wait_ge(w_loaded[slot], (n - slot) * 8 + 16)
                act.wait_ge(panel_used, n + 1)
                nc.scalar.activation(w_hi[:, slot, 0:width], w_raw[:, slot, 0:width], ACT.Copy).then_inc(w_hi_done, 1)

            def high_of(name, i, k):
                base, count, width = PHASE[name, i]
                high(base + k, k % 2, width)

            def h_high(n):
                high_of(*norms[n], 1)
                with act.Fori(0, 2) as i:
                    for b in range(4):
                        act.wait_ge(h_aff, i * 8 + (2 * KD * n + 2 * b + 2))
                        nc.scalar.activation(h_hi[:, i * 4 + b, :], hf[:, b, :], ACT.Copy).then_inc(h_hi_done, 1)

            def ffn_in(f):
                base, count, width = PHASE["in", f]

                def silu(i, b):
                    act.wait_ge(panel_used, i * 2 + (START + base + b + 1))
                    nc.scalar.activation(sg[:, b, :], ps[:, 2 * b, 0:T], ACT.Silu).then_inc(silu_done, 1)

                with act.Fori(0, KF // 2 - 1) as i:
                    for b in range(2):
                        silu(i, b)
                        high(i * 2 + (base + b + 2), b, width)
                silu(KF // 2 - 1, 0)
                high_of("out", f, 0)
                silu(KF // 2 - 1, 1)

            def ffn_out(f, after):
                base, count, width = PHASE["out", f]

                def four(i, last):
                    for s in range(4):
                        if s == 3 and last:
                            if after:
                                high_of(*after, 0)
                        else:
                            high(i * 4 + (base + s + 1), (s + 1) % 2, width)
                with act.Fori(0, KD // 2 - 1) as i:
                    four(i, False)
                four(KD // 2 - 1, True)

            def wo(l, after):
                high_of("wo", l, 2)
                high_of("wo", l, 3)
                high_of(*after, 0)

            def diff():
                U = 2 * DIFF_HEADS

                def exps(u):
                    act.wait_ge(nm_ready, u + 1)
                    for j, (qb, at, slots) in enumerate(pieces(u)):
                        cols = slice(at, at + len(slots) * P)
                        for c in range(2):
                            n = 2 * j + c
                            nc.scalar.activation(e[:, u % 3, c, cols], ps[:, 2 * (u % 3) + c, cols], ACT.Exp,
                                                 bias=nm[:, u % 3, n:n + 1], scale=DIFF_SCALE,
                                                 accum_out=rs[:, u % 3, n:n + 1]).then_inc(exp_done, 1)

                act.wait_ge(dve_consts, 1)
                high_of("qkv", 0, 2)
                for c in range(6):
                    b0 = 3 * (c % 2)
                    base = PHASE["qkv", 0][0]
                    if 2 * c + 3 < 12:
                        high_of("qkv", 0, 2 * c + 3)
                    else:
                        act.wait_ge(heads_ready, 4)
                        act.dma_start(o["new_k"], kn[:, 3, :]).then_inc(k_out, 16)
                        act.wait_ge(lam_step, 2)
                        nc.scalar.activation(lame[:], lams[:], ACT.Exp).then_inc(lam_exp, 1)
                        act.wait_ge(k_out, 16)
                        exps(0)
                    act.wait_ge(panel_used, START + base + 2 * c + 2)
                    if c < 4:
                        if c > 0:
                            act.wait_ge(red_done, c)
                        nc.scalar.activation(sq3[:], ps[:, b0:b0 + 3, :], ACT.Square).then_inc(sq_done, 1)
                        act.wait_ge(red_done, c + 1)
                        nc.scalar.activation(rms[:, 0:24], ssq[:, 0:24], ACT.Sqrt, bias=epsc[:, 0:1],
                                             scale=1.0 / DIFF_HD).then_inc(rms_done, 1)
                    else:
                        for blk in range(NB):
                            nc.scalar.activation(v_all[:, 1 + blk, (c - 4) * ROW:(c - 3) * ROW], ps[:, b0 + blk, :],
                                                 ACT.Copy).then_inc(v_done, 1)
                    if 2 * c + 4 < 12:
                        high_of("qkv", 0, 2 * c + 4)
                    elif 2 * c + 4 == 12:
                        high_of("wo", 0, 0)
                high_of("wo", 0, 1)
                act.wait_ge(v_done, 2 * NB)
                act.dma_start(o["new_v"], v_all[:, 3, :]).then_inc(out_done, 16)
                def evac_aT(u):
                    n = ROW if u % 2 == 0 else T
                    act.wait_ge(t_ready, u + 1)
                    if u >= 2:
                        act.wait_ge(pv_ready, u - 1)
                    nc.scalar.activation(aT[:, u % 2, 0:n], ps[:, 6, 0:n], ACT.Copy).then_inc(at_done, 1)

                def out_squares(u):
                    act.wait_ge(o_done, u + 1)
                    for qb, at, slots in pieces(u):
                        nc.scalar.activation(osq[:, qb, :], oraw[:, (u // 2) % 2, qb, :], ACT.Square,
                                             accum_out=oss[:, (u // 2) % 2, qb:qb + 1]).then_inc(osq_done, 1)

                def out_head(h):
                    act.wait_ge(oT_f, h + 1)
                    nc.scalar.activation(h_hi[:, h, :], otf[:, h % 2, :], ACT.Copy).then_inc(oT_hi, 1)

                exps(1)
                exps(2)
                for u in range(U + 5):
                    if u < U:
                        evac_aT(u)
                    if u + 3 < U:
                        exps(u + 3)
                    if 2 <= u <= U + 1:
                        out_squares(u - 2)
                    if u >= 6 and u % 2 == 0:
                        out_head(u // 2 - 3)

            def mla():
                base = PHASE["down", 0][0]
                high_of("down", 0, 2)
                high_of("down", 0, 3)
                act.wait_ge(panel_used, START + base + 2)
                nc.scalar.activation(cn[:, :, 0:ROW], ps[:, 0:3, :], ACT.Copy).then_inc(cn_done, 1)
                high_of("qup", 0, 0)
                act.wait_ge(panel_used, START + base + 4)
                nc.scalar.activation(cn[:, :, ROW:D], ps[:, 3:6, :], ACT.Copy).then_inc(cn_done, 1)
                high_of("qup", 0, 1)
                for r in range(2):
                    act.wait_ge(dbc_ready, r + 1)
                    nc.scalar.activation(drb[:, r, :], ps[:, 4 + r, 0:T], ACT.Copy).then_inc(drb_ready, 1)
                act.wait_ge(kpe_ready, 1)
                act.dma_start(o["new_kpe"], kpe[:, 3, :]).then_inc(out_done, 16)
                for j in range(KD):
                    act.wait_ge(cT_f, j + 1)
                    src = hf[:, j % 4, :] if j < 6 else ckvf[:, j - 6, :]
                    nc.scalar.activation(h_hi[:, j, :], src, ACT.Copy).then_inc(cT_hi, 1)
                act.dma_start(o["new_ckvT"].rearrange("k p t -> p k t"), ckvf[:, :, CTX]).then_inc(out_done, 16)
                high_of("qup", 0, 2)
                for c in range(4):
                    b0 = 3 * (c % 2)
                    if 2 * c + 3 < 8:
                        high_of("qup", 0, 2 * c + 3)
                    else:
                        high_of("kvup", 0, 2 * c + 3 - 8)
                    act.wait_ge(panel_used, START + PHASE["qup", 0][0] + 2 * c + 2)
                    act.wait_ge(mred_done, c) if c else act.wait_ge(dvar_ready, 1)
                    nc.scalar.activation(msq3[:, :, 0:T], ps[:, b0:b0 + 3, 0:T], ACT.Square).then_inc(msq_done, 1)
                    act.wait_ge(mred_done, c + 1)
                    nc.scalar.activation(rms[:, 0:12], ssq[:, 0:12], ACT.Sqrt, bias=epsc[:, 0:1],
                                         scale=1.0 / QK).then_inc(mrms_done, 1)
                    if 2 * c + 4 < 8:
                        high_of("qup", 0, 2 * c + 4)
                    elif c == 2:
                        high_of("kvup", 0, 0)
                def evac(t):
                    act.wait_ge(mtr_ready, t + 1)
                    nc.scalar.activation(mdst(t), ps[0:QK, 6 + t % 2, :].rearrange("p (h t) -> p h t", h=4),
                                         ACT.Copy).then_inc(mtr_act, 1)

                def values(half):
                    act.wait_ge(kv_values, half + 1)
                    for at, bank in ((0, 6), (2, 0)):
                        nc.scalar.activation(mv_all[:, at:at + 2, half * ROW:(half + 1) * ROW],
                                             ps[:, bank:bank + 2, :], ACT.Copy).then_inc(mv_done, 1)

                def key_squares(half):
                    act.wait_ge(kv_keys, half + 1)
                    if half:
                        act.wait_ge(mred_done, 5)
                    nc.scalar.activation(msq4, ps[:, 2:6, :], ACT.Square).then_inc(msq_done, 1)

                def key_roots(half):
                    act.wait_ge(mred_done, 5 + half)
                    nc.scalar.activation(rms[:, 0:32], ssq[:, 0:32], ACT.Sqrt, bias=epsc[:, 0:1],
                                         scale=1.0 / QK).then_inc(mrms_done, 1)

                values(0)
                key_squares(0)
                high_of("wo", 1, 0)
                key_roots(0)
                values(1)
                key_squares(1)
                evac(0)
                evac(1)
                key_roots(1)
                for t in range(2, 20):
                    evac(t)
                high_of("wo", 1, 1)
                U = 2 * MLA_HEADS

                def exps(u):
                    act.wait_ge(mnm_ready, u + 1)
                    for j, (qb, at, slots) in enumerate(pieces(u)):
                        cols = slice(at, at + len(slots) * P)
                        nc.scalar.activation(me[:, u % 3, cols], ps[:, u % 4, cols], ACT.Exp,
                                             bias=nm[:, u % 3, j:j + 1], scale=MLA_SCALE,
                                             accum_out=rs[:, u % 3, j:j + 1]).then_inc(mexp_done, 1)

                def evac_aT(u):
                    n = ROW if u % 2 == 0 else T
                    act.wait_ge(mt_ready, u + 1)
                    if u >= 2:
                        act.wait_ge(mpv_ready, u - 1)
                    nc.scalar.activation(maT[:, u % 2, 0:n], ps[:, 4 + u % 2, 0:n], ACT.Copy).then_inc(mat_done, 1)

                exps(0)
                exps(1)
                for t in range(20, 28, 2):
                    evac(t)
                for u in range(U):
                    evac_aT(u)
                    if u + 2 < U:
                        exps(u + 2)

            for dst, name in ((bmod, "b_mod"), (norm_g, "norm_g")):
                act.dma_start(dst[:], d[name]).then_inc(small_in, 16)
            for dst, name in ((ropes, "ropes"), (gq, "gq"), (gm, "gm"), (subg, "subg"), (gdown, "gdown"),
                              (lamp, "lamp"), (kpw, "kpw")):
                act.dma_start(dst[:], d[name]).then_inc(params_in, 16)
            act.wait_ge(cond_in, 16)
            nc.scalar.activation(cond[:], cond[:], ACT.Silu).then_inc(cond_ready, 1)
            act.wait_ge(x_in, 16)
            nc.scalar.activation(squares_all, x[:], ACT.Square).then_inc(x_squared, 1)
            for k in range(KD + 1):
                if k < KD:
                    act.wait_ge(first_prod, k + 1)
                    nc.scalar.activation(wm[:, 2 + k % 2, :], wm[:, 2 + k % 2, :], ACT.Copy,
                                         accum_out=modc[:, k, 1:2]).then_inc(first_sum, 1)
                if k == 0:
                    high_of("in", 0, 0)
                else:
                    act.wait_ge(h_aff, 2 * k)
                    nc.scalar.activation(h_hi[:, k - 1, :], hf[:, (k - 1) % 4, :], ACT.Copy).then_inc(h_hi_done, 1)
            high_of("in", 0, 1)
            ffn_in(0)
            ffn_out(0, ("qkv", 0))
            act.wait_ge(panel_used, START + PHASE["qkv", 0][0])
            act.wait_ge(mod_step, 2 * MODS_OF["in", 1][0])
            act.dma_start(kn[:, 0, :], d["cache_k"]).then_inc(diff_in, 16)
            act.dma_start(v_all[:, 0, :], d["cache_v"]).then_inc(diff_in, 16)
            h_high(1)
            diff()
            wo(0, ("in", 1))
            h_high(2)
            ffn_in(1)
            ffn_out(1, ("in", 2))
            h_high(3)
            ffn_in(2)
            ffn_out(2, ("down", 0))
            act.wait_ge(panel_used, START + PHASE["down", 0][0])
            act.dma_start(cck[:], d["cache_ckv"]).then_inc(mla_in, 16)
            act.dma_start(kpe[:, 0, :], d["cache_kpe"]).then_inc(mla_in, 16)
            h_high(4)
            mla()
            wo(1, ("in", 3))
            h_high(5)
            ffn_in(3)
            ffn_out(3, None)

        @block.vector
        def _(v):
            nc.vector.memset(epsc[:], EPS).then_inc(dve_consts, 1)
            nc.vector.memset(nhalf[:], -0.5).then_inc(dve_consts, 1)
            v.sem_inc(panel_used, START)
            v.sem_inc(prod_ready, START)
            v.sem_inc(h_lo_done, H_START)
            v.sem_inc(proj_free, START)
            v.sem_inc(res_step, 4 * START)
            def squares(i_dc, k, last_inc=1):
                v.wait_ge(res_step, i_dc * 4 + (4 * START + 2))
                nc.vector.tensor_tensor(square, x[:, k, :], x[:, k, :], ALU.mult).then_inc(res_step, 1)
                v.wait_ge(res_step, i_dc * 4 + (4 * START + 3))
                nc.vector.tensor_tensor(sqacc[:], sqacc[:], square, ALU.add).then_inc(res_step, 1)

            def mod_chunk(q, panel, loaded, before=None, conds=2):
                before = q if before is None else before
                v.wait_ge(*loaded)
                for s in range(conds):
                    if not (isinstance(before, int) and before == 0):
                        v.wait_ge(mod_step, before * 2 + (s - 1))
                    nc.vector.scalar_tensor_tensor(mod_prod[:] if s == 0 else panel, panel, 1.0, cond[:, s, :],
                                                   ALU.mult, ALU.mult,
                                                   accum_out=modc[:, bass.ds(q, 1), s]).then_inc(mod_step, 3 - conds)

            def mod_ring(ph, i, part, parts):
                first_mod, mods = MODS_OF.get(ph, (0, 0))
                for q in range(part * mods // parts, (part + 1) * mods // parts):
                    mod_chunk(i * mods + (first_mod + q), wm[:, q, :], (wm_loaded[ph, q], i * 16 + 16))

            def norm(n, layer, part):
                shift, scale = 72 * layer + 24 * part, 72 * layer + 24 * part + 8

                def invert():
                    v.wait_ge(ss_ready, n + 1)
                    nc.vector.tensor_scalar(var[:], ps[:, 7, 0:NB], 1.0 / D, EPS, ALU.mult,
                                            ALU.add).then_inc(var_ready, 1)
                    v.wait_ge(rstd_ready, n + 1)
                    for b in range(NB):
                        nc.vector.tensor_scalar(diag[:, b, :], ident[:], rstd[:, b:b + 1], None,
                                                ALU.mult).then_inc(diag_ready, 1)

                def one_plus_scale(ks):
                    nc.vector.scalar_tensor_tensor(gmul[:, ks], modc[:, scale + ks.start:scale + ks.stop, :], 1.0,
                                                   norm_g[:, 3 * layer + part, ks], ALU.add,
                                                   ALU.mult).then_inc(gains, 1)

                def chunk(i, b):
                    v.wait_ge(h_lo_done, i * 4 + (KD * n + b + 1))
                    nc.vector.tensor_tensor(hf[:, b, :], x[:, i * 4 + b, :], ps[:, 6, 0:T],
                                            ALU.mult).then_inc(h_tmp, 1)
                    v.wait_ge(h_tmp, i * 4 + (KD * n + b + 1))
                    for s, seg in SEGS:
                        nc.vector.tensor_scalar(hf[:, b, seg], hf[:, b, seg], gmul[:, bass.ds(i * 4 + b, 1), s],
                                                modc[:, bass.ds(i * 4 + (shift + b), 1), s], ALU.mult,
                                                ALU.add).then_inc(h_aff, 1)

                if n == 0:
                    invert()
                    v.wait_ge(cond_ready, 1)
                    v.wait_ge(small_in, 32)
                    for k in range(KD):
                        for s, q in enumerate((KD + k, k)):
                            mod_chunk(q, wm_first[:, q, :], (wmf_loaded[q], 16), before=2 * k + s, conds=2 - s)
                        v.wait_ge(mod_step, 4 * k + 4)
                        v.wait_ge(first_sum, k + 1)
                        for q in (KD + k, k):
                            nc.vector.tensor_tensor(modc[:, q, :], modc[:, q, :], bmod[:, q, :],
                                                    ALU.add).then_inc(gains, 1)
                        v.wait_ge(gains, 3 * k + 2)
                        one_plus_scale(slice(k, k + 1))
                        v.wait_ge(gains, 3 * k + 3)
                        if k == 0:
                            v.wait_ge(bc_ready, 1)
                        chunk(k // 4, k % 4)
                    return
                v.wait_ge(mod_step, 2 * (scale + 8))
                nc.vector.tensor_tensor(modc[:, shift:scale + 8, :], modc[:, shift:scale + 8, :],
                                        bmod[:, shift:scale + 8, :], ALU.add).then_inc(gains, 1)
                v.wait_ge(gains, gain_count["norm", n] - 1)
                one_plus_scale(slice(0, KD))
                invert()
                v.wait_ge(gains, gain_count["norm", n])
                v.wait_ge(bc_ready, n + 1)
                with v.Fori(0, 2) as i:
                    for b in range(4):
                        chunk(i, b)

            gain_count = {}
            for n in range(6):
                gain_count["norm", n] = 3 * KD + 5 * n
                gain_count["res", n] = 3 * KD + 5 * n + 3

            def residual(n, layer, part, factor):
                name, f = residuals[n]
                base = PHASE[name, f][0]
                gate = 72 * layer + 24 * part + 16
                final = n == 5
                v.wait_ge(mod_step, 2 * (gate + 8))
                nc.vector.tensor_tensor(modc[:, gate:gate + 8, :], modc[:, gate:gate + 8, :],
                                        bmod[:, gate:gate + 8, :], ALU.add).then_inc(gains, 1)
                v.wait_ge(gains, gain_count["res", n] - 2)
                nc.vector.tensor_scalar(gres[:], modc[:, gate:gate + 8, :], factor, None,
                                        ALU.mult).then_inc(gains, 1)
                nc.vector.memset(sqacc[:], 0.0).then_inc(gains, 1)
                v.wait_ge(gains, gain_count["res", n])
                rb = RES_BASE[name, f]

                def chunk(k, b, dc):
                    for s, seg in SEGS:
                        nc.vector.scalar_tensor_tensor(x[:, bass.ds(k, 1), seg].rearrange("p a t -> p (a t)"),
                                                       ps[:, 4 + b, seg], gres[:, bass.ds(k, 1), s],
                                                       x[:, bass.ds(k, 1), seg].rearrange("p a t -> p (a t)"),
                                                       ALU.mult, ALU.add).then_inc(res_step, 3 if final and s else 1)
                    if not final:
                        squares(dc, k)

                if name == "out":
                    with v.Fori(0, KD // 2) as i:
                        for b in range(2):
                            mod_ring((name, f), i, b, 2)
                            v.wait_ge(panel_used, i * 4 + (START + base + 2 * b + 2))
                            chunk(i * 2 + b, b, i * 2 + (rb + b))
                else:
                    with v.Fori(0, 2) as i:
                        for pn in range(2):
                            for b in range(2):
                                if pn == 1 and b == 0:
                                    v.wait_ge(out_ready, i + (2 * f + 1))
                                else:
                                    v.wait_ge(panel_used, i * 2 + (START + base + pn + 1))
                                chunk(i * 4 + 2 * pn + b, b - 2 * pn, i * 4 + (rb + 2 * pn + b))

            def ffn_in(f):
                base = PHASE["in", f][0]
                with v.Fori(0, KF // 2) as i:
                    for b in range(2):
                        m = KF * f + b + 1
                        mod_ring(("in", f), i, b, 2)
                        v.wait_ge(panel_used, i * 2 + (START + base + b + 1))
                        v.wait_ge(silu_done, i * 2 + m)
                        nc.vector.tensor_tensor(prod[:, b, :], ps[:, 2 * b + 1, 0:T], sg[:, b, :],
                                                ALU.mult).then_inc(prod_ready, 1)
                        v.wait_ge(prod_ready, i * 2 + (START + m))
                        nc.vector.tensor_copy(g_hi[:, i * 2 + b, :], prod[:, b, :]).then_inc(g_hi_done, 1)
                        v.wait_ge(g_hi_done, i * 2 + m)
                        nc.vector.tensor_tensor(g_lo[:, i * 2 + b, :], prod[:, b, :],
                                                g_hi[:, i * 2 + b, :].bitcast(F32), ALU.subtract).then_inc(g_ready, 1)

            count = [0]

            def step(ins):
                count[0] += 1
                ins.then_inc(dve, 1)
                v.wait_ge(dve, count[0])

            def rope(X, groups, half, off, blk):
                r = 4 * half
                cos = ropes[:, 0, blk, off:off + r].unsqueeze(1).to_broadcast([P, groups, r])
                sin = ropes[:, 1, blk, off:off + r].rearrange("p (c h f) -> p c h f", c=2, h=2)
                a1 = t1[:, 0:groups, 0:r]
                b1 = t2[:, 0:groups, 0:r]
                X4 = X.rearrange("p g (c h f) -> p g c h f", c=2, h=2)
                B4 = b1.rearrange("p g (c h f) -> p g c h f", c=2, h=2)
                nc.vector.tensor_tensor(a1, X, cos, ALU.mult)
                for h in range(2):
                    sh = sin[:, :, h, :].unsqueeze(1).to_broadcast([P, groups, 2, half])
                    ins = nc.vector.tensor_tensor(B4[:, :, :, h, :], X4[:, :, :, 1 - h, :], sh, ALU.mult)
                step(ins)
                step(nc.vector.tensor_tensor(X, a1, b1, ALU.add))

            def diff():
                for c in range(4):
                    b0 = 3 * (c % 2)
                    is_k = c // 2
                    v.wait_ge(sq_done, c + 1)
                    nc.vector.tensor_reduce(ssq[:, 0:24].rearrange("p (b g) -> p b g", b=NB),
                                            sq3[:].rearrange("p b (g e) -> p b g e", g=8), AX.X,
                                            ALU.add).then_inc(red_done, 1)
                    v.wait_ge(rms_done, c + 1)
                    step(nc.vector.reciprocal(rinv[:, 0:24], rms[:, 0:24]))
                    to = (kn[:, 1:4, :] if is_k else qn[:])[:, :, (c % 2) * ROW:(c % 2 + 1) * ROW]
                    for b in range(NB):
                        t8 = to[:, b, :].rearrange("p (g e) -> p g e", g=8)
                        nc.vector.tensor_tensor(t8, ps[:, b0 + b, :].rearrange("p (g e) -> p g e", g=8),
                                                rinv[:, 8 * b:8 * b + 8].unsqueeze(2).to_broadcast([P, 8, DIFF_HD]),
                                                ALU.mult).then_inc(*((proj_free, 1) if b == 2 else (dve, 1)))
                    count[0] += 2
                    v.wait_ge(proj_free, START + c + 1)
                    v.wait_ge(dve, count[0])
                    for b in range(NB):
                        t8 = to[:, b, :].rearrange("p (g e) -> p g e", g=8)
                        g8 = gq[:, is_k, :].unsqueeze(1).to_broadcast([P, 8, DIFF_HD])
                        ins = nc.vector.tensor_tensor(t8, t8, g8, ALU.mult)
                    step(ins)
                    for b in range(2):
                        rope(to[:, b, :].rearrange("p (g e) -> p g e", g=8), 8, 16, 0, b)
                    v.sem_inc(heads_ready, 1)
                for t in range(14):
                    v.wait_ge(tr_ready, t + 1)
                    nc.vector.tensor_copy(ddst(t), ps[:, 6 + t % 2, :].rearrange("p (h t) -> p h t", h=4)
                                          ).then_inc(tr_done, 1)
                v.wait_ge(lam_exp, 1)
                step(nc.vector.tensor_tensor(neglam[:, 1:2], lame[:, 1:2], lame[:, 0:1], ALU.subtract))
                step(nc.vector.tensor_scalar(neglam[:, 0:1], neglam[:, 1:2], -LAM_INIT, None, ALU.add))
                U = 2 * DIFF_HEADS

                def top(u):
                    v.wait_ge(s_ready, u + 1)
                    for j, (qb, at, slots) in enumerate(pieces(u)):
                        ins = nc.vector.tensor_reduce(mx[:, u % 3, 2 * j:2 * j + 2],
                                                      ps[:, 2 * (u % 3):2 * (u % 3) + 2, at:at + len(slots) * P],
                                                      AX.X, ALU.max)
                    n = 2 * len(pieces(u))
                    step(ins)
                    nc.vector.tensor_scalar(nm[:, u % 3, 0:n], mx[:, u % 3, 0:n], -DIFF_SCALE, None,
                                            ALU.mult).then_inc(nm_ready, 1)

                def mix(u):
                    n = len(pieces(u))
                    v.wait_ge(exp_done, exps_upto(u, 2))
                    step(nc.vector.reciprocal(ri[:, u % 3, 0:2 * n], rs[:, u % 3, 0:2 * n]))
                    step(nc.vector.tensor_scalar(ri2[:, u % 3, 0:n],
                                                 ri[:, u % 3, 0:2 * n].rearrange("p (j c) -> p j c", c=2)[:, :, 1],
                                                 neglam[:, 0:1], None, ALU.mult))
                    for j, (qb, at, slots) in enumerate(pieces(u)):
                        cols = slice(at, at + len(slots) * P)
                        ins = nc.vector.tensor_scalar(a2[:, cols], e[:, u % 3, 1, cols], ri2[:, u % 3, j:j + 1],
                                                      None, ALU.mult)
                    step(ins)
                    if u >= 2:
                        v.wait_ge(t_ready, u - 1)
                    for j, (qb, at, slots) in enumerate(pieces(u)):
                        cols = slice(at, at + len(slots) * P)
                        ins = nc.vector.scalar_tensor_tensor(a[:, u % 2, cols], e[:, u % 3, 0, cols],
                                                             ri[:, u % 3, 2 * j:2 * j + 1], a2[:, cols], ALU.mult,
                                                             ALU.add)
                    ins.then_inc(a_done, 1)

                def out_copy(u):
                    h = u // 2
                    v.wait_ge(pv_ready, u + 1)
                    if h >= 2:
                        v.wait_ge(on_done, h - 1)
                    dst, n = (oraw[:, h % 2, 0::2, :], 2) if u % 2 == 0 else (oraw[:, h % 2, 1:2, :], 1)
                    nc.vector.tensor_copy(dst, ps[:, 7, 0:n * P].rearrange("p (b t) -> p b t", b=n)
                                          ).then_inc(o_done, 1)

                top(0)
                v.wait_ge(k_out, 16)
                top(1)
                top(2)
                for u in range(U + 4):
                    if u < U:
                        mix(u)
                    if 2 <= u <= U + 1:
                        out_copy(u - 2)
                    if u >= 4 and u % 2 == 0:
                        h = u // 2 - 2
                        v.wait_ge(osq_done, 3 * h + 3)
                        nc.vector.tensor_scalar(ovar[:, h % 2, :], oss[:, h % 2, :], 1.0 / DIFF_VD, EPS, ALU.mult,
                                                ALU.add).then_inc(ovar_ready, 1)
                    if u + 3 < U:
                        top(u + 3)
                    if u >= 5 and u % 2 == 1:
                        h = (u - 5) // 2
                        v.wait_ge(oT_ready, h + 1)
                        if h >= 2:
                            v.wait_ge(oT_lo, h - 1)
                        nc.vector.tensor_scalar(otf[:, h % 2, :], ps[:, 6, 0:T], subg[:, 0:1],
                                                1.0 - LAM_INIT, ALU.mult, ALU.mult).then_inc(oT_f, 1)

            def square_latent(n):
                lo, hi = ((0, ROW), (ROW, Q_RANK), (Q_RANK, D))[n]
                if n < 2:
                    v.wait_ge(cn_done, n + 1)
                for b in range(NB):
                    src = cn[:, b, lo:hi]
                    ins = nc.vector.scalar_tensor_tensor(msq3[:, b, lo % ROW:lo % ROW + hi - lo], src, 1.0, src,
                                                         ALU.mult, ALU.mult, accum_out=dss[:, b, n:n + 1])
                step(ins)

            def mla():
                v.wait_ge(mla_in, 32)
                nc.vector.tensor_copy(cck_hi[:], cck[:]).then_inc(cck_step, 1)
                v.wait_ge(cck_step, 1)
                nc.vector.tensor_tensor(cck_lo[:], cck[:], cck_hi[:].bitcast(F32), ALU.subtract).then_inc(cck_step, 1)
                v.wait_ge(kpe_prod, 1)
                nc.vector.tensor_copy(kpT, ps[0:ROPE, 6, 0:T]).then_inc(kpT_ready, 1)
                square_latent(0)
                v.wait_ge(kpe_turned, 1)
                nc.vector.tensor_copy(kpe[:, 1:4, :], ps[:, 7, 0:NB * ROPE].rearrange("p (b r) -> p b r", b=NB)
                                      ).then_inc(kpe_ready, 1)
                v.wait_ge(kpe_ready, 1)
                square_latent(1)
                square_latent(2)
                nc.vector.tensor_scalar(dvar[:, 1, :], dss[:, :, 2], 1.0 / KV_RANK, EPS, ALU.mult, ALU.add)
                step(nc.vector.tensor_tensor(dtot[:], dss[:, :, 0], dss[:, :, 1], ALU.add))
                nc.vector.tensor_scalar(dvar[:, 0, :], dtot[:], 1.0 / Q_RANK, EPS, ALU.mult,
                                        ALU.add).then_inc(dvar_ready, 1)
                v.wait_ge(drin_ready, 1)
                for r in range(2):
                    for b in range(NB):
                        nc.vector.tensor_scalar(ddiag[:, (3 * r + b) * P:(3 * r + b + 1) * P], ident[:],
                                                drin[:, r, b:b + 1], None, ALU.mult).then_inc(ddiag_ready, 1)
                step(nc.vector.tensor_tensor(kps[:], kpe[:], kpe[:], ALU.mult))
                step(nc.vector.tensor_reduce(kpss[:], kps[:], AX.X, ALU.add))
                step(nc.vector.tensor_tensor(kpg[:], kpe[:],
                                             gm[:, 1, NOPE:QK].unsqueeze(1).to_broadcast([P, 4, ROPE]), ALU.mult))
                for b in range(2):
                    rope(kpg[:, 1 + b:2 + b, :], 1, 8, 64, b)
                for j in range(KD):
                    v.wait_ge(cT_ready, j + 1)
                    v.wait_ge(drb_ready, 1 if j < 6 else 2)
                    if 4 <= j < 6:
                        v.wait_ge(cT_lo, j - 3)
                    dst = hf[:, j % 4, :] if j < 6 else ckvf[:, j - 6, :]
                    nc.vector.scalar_tensor_tensor(dst, ps[:, C_BANK[j], 0:T], gdown[:, j:j + 1],
                                                   drb[:, 0 if j < 6 else 1, :], ALU.mult,
                                                   ALU.mult).then_inc(cT_f, 1)
                for c in range(4):
                    b0 = 3 * (c % 2)
                    v.wait_ge(msq_done, c + 1)
                    nc.vector.tensor_reduce(ssq[:, 0:12].rearrange("p (b g) -> p b g", b=NB),
                                            msq3[:, :, 0:T].rearrange("p b (g e) -> p b g e", g=4), AX.X,
                                            ALU.add).then_inc(mred_done, 1)
                    v.wait_ge(mrms_done, c + 1)
                    step(nc.vector.reciprocal(rinv[:, 0:12], rms[:, 0:12]))
                    for b in range(NB):
                        t4 = mqn[:, b, c * T:(c + 1) * T].rearrange("p (g e) -> p g e", g=4)
                        ins = nc.vector.tensor_tensor(t4, ps[:, b0 + b, 0:T].rearrange("p (g e) -> p g e", g=4),
                                                      rinv[:, 4 * b:4 * b + 4].unsqueeze(2).to_broadcast([P, 4, QK]),
                                                      ALU.mult)
                    ins.then_inc(mproj_free, 1)
                    v.wait_ge(mproj_free, c + 1)
                    for b in range(NB):
                        t4 = mqn[:, b, c * T:(c + 1) * T].rearrange("p (g e) -> p g e", g=4)
                        ins = nc.vector.tensor_tensor(t4, t4, gm[:, 0, :].unsqueeze(1).to_broadcast([P, 4, QK]),
                                                      ALU.mult)
                    step(ins)
                    for b in range(2):
                        t4 = mqn[:, b, c * T:(c + 1) * T].rearrange("p (g e) -> p g e", g=4)
                        rope(t4[:, :, NOPE:QK], 4, 8, 64, b)
                    v.sem_inc(mheads, 1)
                for half in range(2):
                    v.wait_ge(msq_done, 5 + half)
                    step(nc.vector.tensor_reduce(ssq[:, 0:32].rearrange("p (b g) -> p b g", b=4),
                                                 msq4.rearrange("p b (g e) -> p b g e", g=8), AX.X, ALU.add))
                    s4 = ssq[:, 0:32].rearrange("p (b g) -> p b g", b=4)
                    nc.vector.tensor_tensor(s4, s4, kpss[:].unsqueeze(2).to_broadcast([P, 4, 8]),
                                            ALU.add).then_inc(mred_done, 1)
                    v.wait_ge(mrms_done, 5 + half)
                    step(nc.vector.reciprocal(rinv[:, 0:32], rms[:, 0:32]))
                    if half == 0:
                        v.wait_ge(out_done, 48)
                    r4 = rinv[:, 0:32].rearrange("p (b g) -> p b g", b=4)
                    for b in range(4):
                        ins = nc.vector.tensor_tensor(mkn[:, half, b, :, 0:NOPE],
                                                      ps[:, 2 + b, :].rearrange("p (g e) -> p g e", g=8),
                                                      r4[:, b, :].unsqueeze(2).to_broadcast([P, 8, NOPE]), ALU.mult)
                    ins.then_inc(kbank_free, 1)
                    for b in range(4):
                        nc.vector.tensor_tensor(mkn[:, half, b, :, NOPE:QK],
                                                kpg[:, b, :].unsqueeze(1).to_broadcast([P, 8, ROPE]),
                                                r4[:, b, :].unsqueeze(2).to_broadcast([P, 8, ROPE]), ALU.mult)
                    v.wait_ge(kbank_free, half + 1)
                    for b in range(4):
                        ins = nc.vector.tensor_tensor(mkn[:, half, b, :, 0:NOPE], mkn[:, half, b, :, 0:NOPE],
                                                      gm[:, 1, 0:NOPE].unsqueeze(1).to_broadcast([P, 8, NOPE]),
                                                      ALU.mult)
                    step(ins)
                    v.sem_inc(mkheads, 1)
                U = 2 * MLA_HEADS

                def top(u):
                    v.wait_ge(ms_ready, u + 1)
                    for j, (qb, at, slots) in enumerate(pieces(u)):
                        ins = nc.vector.tensor_reduce(mx[:, u % 3, j:j + 1], ps[:, u % 4, at:at + len(slots) * P],
                                                      AX.X, ALU.max)
                    n = len(pieces(u))
                    step(ins)
                    nc.vector.tensor_scalar(nm[:, u % 3, 0:n], mx[:, u % 3, 0:n], -MLA_SCALE, None,
                                            ALU.mult).then_inc(mnm_ready, 1)

                top(0)
                top(1)
                for t in range(21, 28, 2):
                    v.wait_ge(mtr_ready, t + 1)
                    nc.vector.tensor_copy(mdst(t), ps[0:QK, 7, :].rearrange("p (h t) -> p h t", h=4)
                                          ).then_inc(mtr_dve, 1)

                def scale(u):
                    n = len(pieces(u))
                    v.wait_ge(mexp_done, exps_upto(u, 1))
                    step(nc.vector.reciprocal(ri[:, u % 3, 0:n], rs[:, u % 3, 0:n]))
                    if u >= 2:
                        v.wait_ge(mt_ready, u - 1)
                    for j, (qb, at, slots) in enumerate(pieces(u)):
                        cols = slice(at, at + len(slots) * P)
                        ins = nc.vector.tensor_scalar(ma[:, u % 2, cols], me[:, u % 3, cols],
                                                      ri[:, u % 3, j:j + 1], None, ALU.mult)
                    ins.then_inc(ma_done, 1)

                for u in range(U + 2):
                    if u < U:
                        scale(u)
                    if u + 2 < U:
                        top(u + 2)
                    if u >= 5 and u % 4 == 1:
                        pr = u // 4 - 1
                        bank = 6 + pr % 2
                        v.wait_ge(mpv_ready, 4 * pr + 4)
                        nc.vector.tensor_copy(h_hi[:, pr, :], ps[:, bank, 0:T]).then_inc(mo_hi, 1)
                        v.wait_ge(mo_hi, pr + 1)
                        nc.vector.tensor_tensor(h_lo[:, pr, :], ps[:, bank, 0:T],
                                                h_hi[:, pr, :].bitcast(F32), ALU.subtract).then_inc(mo_lo, 1)

            v.wait_ge(x_squared, 1)
            nc.vector.tensor_reduce(sqacc[:], squares_all.rearrange("p k t -> p t k"), AX.X,
                                    ALU.add).then_inc(res_step, 4 * KD)
            norm(0, 0, 0)
            v.wait_ge(params_in, 112)
            nc.vector.tensor_tensor(lamt[:], lamp[:, 0::2, :], lamp[:, 1::2, :], ALU.mult).then_inc(lam_step, 1)
            v.wait_ge(lam_step, 1)
            nc.vector.tensor_reduce(lams[:], lamt[:], AX.X, ALU.add).then_inc(lam_step, 1)
            nc.vector.tensor_copy(kpw_hi[:], kpw[:]).then_inc(kpw_done, 1)
            v.wait_ge(kpw_done, 1)
            nc.vector.tensor_tensor(kpw_lo[:], kpw[:], kpw_hi[:].bitcast(F32), ALU.subtract).then_inc(kpw_done, 1)
            ffn_in(0)
            residual(0, 0, 0, 0.5)
            norm(1, 0, 1)
            diff()
            residual(1, 0, 1, 1.0)
            norm(2, 0, 2)
            ffn_in(1)
            residual(2, 0, 2, 0.5)
            norm(3, 1, 0)
            ffn_in(2)
            residual(3, 1, 0, 0.5)
            norm(4, 1, 1)
            mla()
            residual(4, 1, 1, 1.0)
            norm(5, 1, 2)
            ffn_in(3)
            residual(5, 1, 2, 0.5)

        @block.tensor
        def _(pe):
            def mm3(out, l_hi, l_lo, r_hi, r_lo, first, last):
                nc.tensor.matmul(out, l_hi, r_hi, start=first, stop=False)
                nc.tensor.matmul(out, l_hi, r_lo, start=False, stop=False)
                return nc.tensor.matmul(out, l_lo, r_hi, start=False, stop=last)

            def norm(n):
                pe.wait_ge(res_step, 4 * (START + KD * (n + 1)))
                for b in range(NB):
                    mm = nc.tensor.matmul(ps[:, 7, b:b + 1], sqacc[:, b * P:(b + 1) * P], ones[:, 0:1],
                                          start=True, stop=True)
                mm.then_inc(ss_ready, 1)
                for b in range(NB):
                    pe.wait_ge(diag_ready, NB * n + b + 1)
                    mm = nc.tensor.matmul(ps[:, 6, b * P:(b + 1) * P], ones[:], diag[:, b, :], start=True,
                                          stop=True)
                mm.then_inc(bc_ready, 1)

            def w_tile(slot, t, n=P):
                return w_hi[:, slot, t * n:(t + 1) * n], w_lo[:, slot, t * n:(t + 1) * n]

            def ffn_in(f, n):
                base = PHASE["in", f][0]
                with pe.Fori(0, KF // 2) as i:
                    for b in range(2):
                        pe.wait_ge(w_lo_done, i * 2 + (base + b + 1))
                        pe.wait_ge(prod_ready, i * 2 + (KF * f + b + 1))
                        for k in range(KD):
                            if b == 0:
                                pe.wait_ge(h_lo_done, h_val(n, k))
                            for half in range(2):
                                mm = mm3(ps[:, 2 * b + half, 0:T], *w_tile(b, KD * half + k), h_hi[:, k, :],
                                         h_lo[:, k, :], k == 0, k == KD - 1)
                        mm.then_inc(panel_used, 1)

            def ffn_out(f):
                base = PHASE["out", f][0]
                rb = RES_BASE["out", f]
                kh = KF // 2
                with pe.Fori(0, KD // 2) as i:
                    for b in range(2):
                        pe.wait_ge(res_step, i * 8 + (4 * (rb + b) + 2))
                        for half in range(2):
                            pe.wait_ge(w_lo_done, i * 4 + (base + 2 * b + half + 1))
                            for k in range(kh):
                                if b == 0 and (k == 0 or half and k == kh - 1):
                                    pe.wait_ge(g_ready, KF * f + (kh if not half else KF - 1 if k == 0 else KF))
                                mm = mm3(ps[:, 4 + b, 0:T], *w_tile(half, k), g_hi[:, kh * half + k, :],
                                         g_lo[:, kh * half + k, :], half == 0 and k == 0, half == 1 and k == kh - 1)
                            mm.then_inc(panel_used, 1)

            def wo(layer, parts, before=None):
                base = PHASE["wo", layer][0]
                rb = RES_BASE["wo", layer]
                for i in range(2):
                    for pn in range(2):
                        pe.wait_ge(w_lo_done, i * 2 + (base + pn + 1))
                        pe.wait_ge(res_step, i * 16 + (4 * (rb + 2 * pn - 1) + 2))
                        if pn == 0:
                            for k in range(KD):
                                if before is not None and i == 0:
                                    before(k)
                                if i == 0:
                                    pe.wait_ge(parts, k + 1)
                                for b in range(2):
                                    mm = mm3(ps[:, 4 + b, 0:T], *w_tile(pn, KD * b + k), h_hi[:, k, :],
                                             h_lo[:, k, :], k == 0, k == KD - 1)
                            mm.then_inc(panel_used, 1)
                        else:
                            for b in range(2):
                                for k in range(KD):
                                    mm = mm3(ps[:, 2 + b, 0:T], *w_tile(pn, KD * b + k), h_hi[:, k, :],
                                             h_lo[:, k, :], k == 0, k == KD - 1)
                                mm.then_inc(out_ready if b == 0 else panel_used, 1)

            def project(s, kh, per, width, hk, banks, first, last, waits=None):
                for kk in range(per):
                    if waits is not None:
                        pe.wait_ge(waits[0], waits[1] + kh * per + kk)
                    for blk in range(NB):
                        k = hk + kh * per + kk
                        mm = mm3(ps[:, banks + blk, 0:width], h_hi[:, k, blk * P:(blk + 1) * P],
                                 h_lo[:, k, blk * P:(blk + 1) * P], *w_tile(s, kk, width),
                                 first and kk == 0, last and kk == per - 1)
                return mm

            def diff():
                base = PHASE["qkv", 0][0]

                def half(i, c, kh):
                    pe.wait_ge(w_lo_done, i * 4 + (base + 2 * c + kh + 1))
                    project(kh, kh, 4, ROW, 0, 3 * c, kh == 0, kh == 1,
                            (h_lo_done, h_val(1, 0)) if c == 0 else None).then_inc(panel_used, 1)

                def free(i, c):
                    pe.wait_ge(proj_free, i * 2 + (c + 1))

                with pe.Fori(0, 2) as i:
                    for c in range(2):
                        free(i, c)
                        half(i, c, 0)
                        half(i, c, 1)
                free(2, 0)
                half(2, 0, 0)
                half(2, 0, 1)
                for t in range(14):
                    pe.wait_ge(heads_ready, 2 if t < 6 else 4)
                    if t == 6:
                        pe.wait_ge(diff_in, 32)
                    if t >= 2:
                        pe.wait_ge(tr_done, t - 1)
                    for i in range(4):
                        if t < 6:
                            src = qn[:, t % 3, (4 * (t // 3) + i) * P:(4 * (t // 3) + i + 1) * P]
                        else:
                            g, slot = divmod(t - 6, 4)
                            src = kn[:, slot, (4 * g + i) * P:(4 * g + i + 1) * P]
                        mm = nc.tensor.transpose(ps[:, 6 + t % 2, i * P:(i + 1) * P], src, ident[:])
                    mm.then_inc(tr_ready, 1)
                U = 2 * DIFF_HEADS

                def scores(u):
                    h = u // 2
                    if u >= 3:
                        pe.wait_ge(exp_done, exps_upto(u - 3, 2))
                    for qb, at, slots in pieces(u):
                        n = len(slots) * P
                        for c in range(2):
                            r = slice(DIFF_HD * c, DIFF_HD * (c + 1))
                            mm = nc.tensor.matmul(ps[:, 2 * (u % 3) + c, at:at + n], dqT[r, h, qb * P:(qb + 1) * P],
                                                  dkT[r, h, slots[0] * P:slots[0] * P + n], start=True, stop=True)
                    mm.then_inc(s_ready, 1)

                def turn(u):
                    pe.wait_ge(a_done, u + 1)
                    if u >= 1:
                        pe.wait_ge(at_done, u)
                    for kb in range(4 if u % 2 == 0 else 3):
                        mm = nc.tensor.transpose(ps[:, 6, kb * P:(kb + 1) * P], a[:, u % 2, kb * P:(kb + 1) * P],
                                                 ident[:])
                    mm.then_inc(t_ready, 1)

                def values(u):
                    h = u // 2
                    pe.wait_ge(at_done, u + 1)
                    if u >= 1:
                        pe.wait_ge(o_done, u)
                    for j, (qb, at, slots) in enumerate(pieces(u)):
                        for kb, slot in enumerate(slots):
                            mm = nc.tensor.matmul(ps[:, 7, j * P:(j + 1) * P],
                                                  aT[:, u % 2, at + kb * P:at + (kb + 1) * P],
                                                  v_all[:, slot, h * DIFF_VD:(h + 1) * DIFF_VD], start=kb == 0,
                                                  stop=kb == len(slots) - 1)
                    mm.then_inc(pv_ready, 1)

                def out_turn(h):
                    pe.wait_ge(on_done, h + 1)
                    for b in range(NB):
                        mm = nc.tensor.transpose(ps[:, 6, b * P:(b + 1) * P], onrm[:, h % 2, b, :], ident[:])
                    mm.then_inc(oT_ready, 1)

                free(2, 1)
                half(2, 1, 0)
                pe.wait_ge(tr_done, 14)
                pe.wait_ge(v_done, NB)
                scores(0)
                half(2, 1, 1)
                pe.wait_ge(v_done, NB + 1)
                scores(1)
                pe.wait_ge(v_done, 2 * NB)
                scores(2)
                for u in range(U + 1):
                    if u + 3 < U:
                        scores(u + 3)
                    if u < U:
                        if u >= 6 and u % 2 == 0:
                            pe.wait_ge(oT_f, u // 2 - 2)
                        turn(u)
                    if 1 <= u <= U:
                        values(u - 1)
                    if u >= 5 and u % 2 == 1:
                        pe.wait_ge(at_done, u + 1)
                        out_turn((u - 5) // 2)

                def last_turns(k):
                    for at, h in ((0, DIFF_HEADS - 2), (5, DIFF_HEADS - 1)):
                        if k == at:
                            pe.wait_ge(at_done, U)
                            pe.wait_ge(oT_f, h)
                            out_turn(h)
                return last_turns

            def mla():
                base = PHASE["down", 0][0]
                for c in range(2):
                    for kh in range(2):
                        pe.wait_ge(w_lo_done, base + 2 * c + kh + 1)
                        project(kh, kh, 4, ROW, 0, 3 * c, kh == 0, kh == 1,
                                (h_lo_done, h_val(4, 0)) if c == 0 else None).then_inc(panel_used, 1)
                    if c == 0:
                        pe.wait_ge(kpw_done, 2)
                        for k in range(KD):
                            mm = mm3(ps[0:ROPE, 6, 0:T], kpw_hi[:, k, :], kpw_lo[:, k, :], h_hi[:, k, :],
                                     h_lo[:, k, :], k == 0, k == KD - 1)
                        mm.then_inc(kpe_prod, 1)
                pe.wait_ge(kpT_ready, 1)
                for blk in range(NB):
                    mm = nc.tensor.transpose(ps[:, 7, blk * ROPE:(blk + 1) * ROPE], kpT[:, blk * P:(blk + 1) * P],
                                             ident[0:ROPE, 0:ROPE])
                mm.then_inc(kpe_turned, 1)
                for j in range(KD):
                    if j == 0:
                        pe.wait_ge(cn_done, 1)
                    elif j == 4:
                        pe.wait_ge(cn_done, 2)
                        pe.wait_ge(kpe_ready, 1)
                    elif j == 6:
                        pe.wait_ge(ddiag_ready, 2 * NB)
                        for r in range(2):
                            nc.tensor.matmul(ps[:, 4 + r, 0:T], ones[:], ddiag[:, r * T:(r + 1) * T],
                                             start=True, stop=True).then_inc(dbc_ready, 1)
                    if j >= 6:
                        pe.wait_ge(cT_f, j - 2)
                    for b in range(NB):
                        mm = nc.tensor.transpose(ps[:, C_BANK[j], b * P:(b + 1) * P],
                                                 cn[:, b, j * P:(j + 1) * P], ident[:])
                    mm.then_inc(cT_ready, 1)
                base = PHASE["qup", 0][0]
                for c in range(4):
                    if c >= 2:
                        pe.wait_ge(mproj_free, c - 1)
                    else:
                        pe.wait_ge(cT_f, 3 if c == 0 else 8)
                    for kh in range(2):
                        pe.wait_ge(w_lo_done, base + 2 * c + kh + 1)
                        project(kh, kh, 3, T, 0, 3 * (c % 2), kh == 0, kh == 1,
                                (cT_lo, 1) if c == 0 else None).then_inc(panel_used, 1)
                base = PHASE["kvup", 0][0]

                def up(half, part, banks):
                    for slot in range(4):
                        for kk in range(2):
                            l_hi = cck_hi[:, kk, :] if slot == 0 else h_hi[:, 6 + kk, (slot - 1) * P:slot * P]
                            l_lo = cck_lo[:, kk, :] if slot == 0 else h_lo[:, 6 + kk, (slot - 1) * P:slot * P]
                            mm = mm3(ps[:, banks[slot], :], l_hi, l_lo, *w_tile(half, 2 * part + kk, ROW), kk == 0,
                                     kk == 1)
                    return mm

                def evacuated(t):
                    if t < 20:
                        return mtr_act, t + 1
                    return (mtr_dve, (t - 20) // 2 + 1) if t % 2 else (mtr_act, 20 + (t - 20) // 2 + 1)

                def turns(ts):
                    for t in ts:
                        if t >= 2:
                            pe.wait_ge(*evacuated(t - 2))
                        for i in range(4):
                            if t < 12:
                                h = 4 * (t // 3) + i
                                src = mqn[:, t % 3, h * QK:(h + 1) * QK]
                            else:
                                g, slot = divmod(t - 12, 4)
                                src = mkn[:, g // 2, slot, 4 * (g % 2) + i, :]
                            mm = nc.tensor.transpose(ps[0:QK, 6 + t % 2, i * P:(i + 1) * P], src, ident[:])
                        mm.then_inc(mtr_ready, 1)

                pe.wait_ge(cck_step, 2)
                pe.wait_ge(cT_f, 8)
                pe.wait_ge(cT_lo, 8)
                V_BANKS, K_BANKS = (6, 7, 0, 1), (2, 3, 4, 5)
                pe.wait_ge(w_lo_done, base + 1)
                pe.wait_ge(mproj_free, 3)
                up(0, 1, V_BANKS).then_inc(kv_values, 1)
                pe.wait_ge(mproj_free, 4)
                mm = up(0, 0, K_BANKS)
                mm.then_inc(kv_keys, 1)
                pe.wait_ge(kv_keys, 1)
                pe.sem_inc(panel_used, 1)
                pe.wait_ge(w_lo_done, base + 2)
                pe.wait_ge(mv_done, 2)
                up(1, 1, V_BANKS).then_inc(kv_values, 1)
                pe.wait_ge(kbank_free, 1)
                up(1, 0, K_BANKS).then_inc(kv_keys, 1)
                pe.wait_ge(mheads, 4)
                pe.wait_ge(mv_done, 4)
                turns(range(4))
                pe.wait_ge(kv_keys, 2)
                pe.sem_inc(panel_used, 1)
                turns(range(4, 12))
                pe.wait_ge(mkheads, 1)
                turns(range(12, 20))
                U = 2 * MLA_HEADS

                def scores(u):
                    h = u // 2
                    if u >= 4:
                        pe.wait_ge(mexp_done, exps_upto(u - 4, 1))
                    for qb, at, slots in pieces(u):
                        n = len(slots) * P
                        mm = nc.tensor.matmul(ps[:, u % 4, at:at + n], mqT[:, h, qb * P:(qb + 1) * P],
                                              mkT[0:QK, h, slots[0] * P:slots[0] * P + n], start=True, stop=True)
                    mm.then_inc(ms_ready, 1)

                def turn(u):
                    pe.wait_ge(ma_done, u + 1)
                    if u >= 2:
                        pe.wait_ge(mat_done, u - 1)
                    for kb in range(4 if u % 2 == 0 else 3):
                        mm = nc.tensor.transpose(ps[:, 4 + u % 2, kb * P:(kb + 1) * P],
                                                 ma[:, u % 2, kb * P:(kb + 1) * P], ident[:])
                    mm.then_inc(mt_ready, 1)

                def values(u):
                    h = u // 2
                    row = MLA_VD * (h % 2)
                    pe.wait_ge(mat_done, u + 1)
                    if u % 4 == 0 and u >= 8:
                        pe.wait_ge(mo_lo, u // 4 - 1)
                    for qb, at, slots in pieces(u):
                        for kb, slot in enumerate(slots):
                            mm = nc.tensor.matmul(ps[row:row + MLA_VD, 6 + (h // 2) % 2, qb * P:(qb + 1) * P],
                                                  mv_all[:, slot, h * MLA_VD:(h + 1) * MLA_VD],
                                                  maT[:, u % 2, at + kb * P:at + (kb + 1) * P], start=kb == 0,
                                                  stop=kb == len(slots) - 1)
                    mm.then_inc(mpv_ready, 1)

                pe.wait_ge(mtr_act, 20)
                scores(0)
                scores(1)
                pe.wait_ge(mkheads, 2)
                turns(range(20, 28))
                pe.wait_ge(kbank_free, 2)
                scores(2)
                pe.wait_ge(mtr_act, 24)
                pe.wait_ge(mtr_dve, 4)
                for u in range(U + 1):
                    if u + 3 < U:
                        scores(u + 3)
                    if u < U:
                        turn(u)
                    if u >= 1:
                        values(u - 1)

            pe.wait_ge(pool_consts, 3)
            norm(0)
            ffn_in(0, 0)
            ffn_out(0)
            norm(1)
            last_turns = diff()
            wo(0, oT_lo, last_turns)
            norm(2)
            ffn_in(1, 2)
            ffn_out(1)
            norm(3)
            ffn_in(2, 3)
            ffn_out(2)
            norm(4)
            mla()
            wo(1, mo_lo)
            norm(5)
            ffn_in(3, 5)
            ffn_out(3)


def rope_table():
    out = np.zeros((2, 2, P, 64 + ROPE), np.float32)
    tok = np.arange(256)
    for off, r in ((0, 64), (64, ROPE)):
        half = r // 4
        n = r // 2
        freqs = (np.float32(10000.0) ** (-np.arange(0, n, 2, dtype=np.float32) / np.float32(n))).astype(np.float32)
        for c, pos in enumerate((tok // 64, tok % 64)):
            ang = (pos.astype(np.float32)[:, None] * freqs[None, :]).astype(np.float32)
            cos, sin = np.cos(ang), np.sin(ang)
            for h in range(2):
                at = off + c * 2 * half + h * half
                out[0, :, :, at:at + half] = cos.reshape(2, P, half)
                out[1, :, :, at:at + half] = (sin if h else -sin).reshape(2, P, half)
    return np.ascontiguousarray(out.transpose(2, 0, 1, 3))


def kernel(x_prompt, x_sample, c, cache_diff_k, cache_diff_v, cache_mla_ckv, cache_mla_kpe, c_ctx,
           w_mod, b_mod, norm_g, ffn_w_in, ffn_w_out,
           diff_w_qkv, diff_q_norm, diff_k_norm, diff_lambda, diff_subln, diff_w_o,
           mla_w_down, mla_q_a_norm, mla_kv_a_norm, mla_w_q_up, mla_w_kv_up, mla_q_norm, mla_k_norm, mla_w_o):
    import concourse.bacc as bacc
    from concourse.bass_utils import run_bass_kernel_spmd

    A = np.asarray

    def every(a, *shape):
        return np.broadcast_to(A(a).reshape((1,) + shape), (P,) + shape)

    tokens = np.concatenate([A(x_sample)[0], A(x_prompt)[0]])
    kv = A(mla_w_kv_up)[0].reshape(2, P, MLA_HEADS, 2, NOPE)
    kv = kv.reshape(2, P, 2, 8, 2, NOPE).transpose(2, 1, 4, 0, 3, 5)
    both = np.stack([A(diff_w_o)[0], A(mla_w_o)[0]])
    arrays = {
        "xT": tokens.reshape(T, KD, P).transpose(2, 1, 0),
        "cond": every(np.stack([A(c_ctx), A(c)[0]]), 2, D),
        "b_mod": np.broadcast_to(A(b_mod).reshape(DEPTH * 72, P).T[:, :, None], (P, DEPTH * 72, 2)),
        "norm_g": np.broadcast_to(A(norm_g).reshape(6, KD, P).transpose(2, 0, 1)[..., None], (P, 6, KD, 2)),
        "w_mod": A(w_mod).reshape(DEPTH, D, 72, P).transpose(0, 2, 3, 1).reshape(MODS, P, D),
        "w_in": A(ffn_w_in).reshape(4, KD, P, 2, KF, P).transpose(0, 4, 2, 3, 1, 5).reshape(4, KF, P, 16 * P),
        "w_out": A(ffn_w_out).reshape(4, 2, KF // 2, P, KD, P).transpose(0, 4, 1, 3, 2, 5)
                  .reshape(4, 2 * KD, P, 11 * P),
        "w_qkv": A(diff_w_qkv)[0].reshape(2, 4, P, 6, ROW).transpose(3, 0, 2, 1, 4).reshape(12, P, 4 * ROW),
        "w_o": both.reshape(2, KD, P, 4, 2, P).transpose(0, 3, 2, 4, 1, 5).reshape(2, 4, P, 16 * P),
        "w_down": A(mla_w_down)[0, :, :D].reshape(2, 4, P, 2, ROW).transpose(3, 0, 2, 1, 4).reshape(4, P, 4 * ROW),
        "kpw": A(mla_w_down)[0, :, D:].reshape(KD, P, ROPE).transpose(1, 0, 2),
        "w_qup": A(mla_w_q_up)[0].reshape(2, 3, P, 4, T).transpose(3, 0, 2, 1, 4).reshape(8, P, 3 * T),
        "w_kvup": kv.reshape(2, P, 4 * ROW),
        "ropes": rope_table(),
        "gq": every(np.stack([A(diff_q_norm)[0], A(diff_k_norm)[0]]), 2, DIFF_HD),
        "gm": every(np.stack([A(mla_q_norm)[0], A(mla_k_norm)[0]]), 2, QK),
        "subg": np.broadcast_to(A(diff_subln)[0][:, None], (P, 2)),
        "gdown": np.concatenate([A(mla_q_a_norm)[0], A(mla_kv_a_norm)[0]]).reshape(KD, P).T,
        "lamp": every(diff_lambda, 4, DIFF_HD),
        "cache_k": A(cache_diff_k)[0, 0].reshape(P, D),
        "cache_v": A(cache_diff_v)[0, 0].reshape(P, D),
        "cache_ckv": A(cache_mla_ckv)[0, 0].reshape(P, 2, P).transpose(2, 1, 0),
        "cache_kpe": A(cache_mla_kpe)[0, 0],
    }
    arrays = {k: np.ascontiguousarray(a) for k, a in arrays.items()}
    outs = {"yT": (KD, P, T), "new_k": (P, D), "new_v": (P, D), "new_ckvT": (2, P, P), "new_kpe": (P, ROPE)}
    nc = bacc.Bacc("TRN2", target_bir_lowering=False, num_devices=1)
    d = {k: nc.dram_tensor("in_" + k, a.shape, F32, kind="ExternalInput").ap() for k, a in arrays.items()}
    o = {k: nc.dram_tensor("out_" + k, s, F32, kind="ExternalOutput").ap() for k, s in outs.items()}
    build_step(nc, d, o)
    r = run_bass_kernel_spmd(nc, [{"in_" + k: a for k, a in arrays.items()}], core_ids=[0]).results[0]
    r = {k: r["out_" + k] for k in outs}
    y = r["yT"].reshape(D, T).T
    return (y[None, 256:], y[None, :256],
            r["new_k"].reshape(1, 1, P, DIFF_HEADS, 2, DIFF_HD), r["new_v"].reshape(1, 1, P, DIFF_HEADS, DIFF_VD),
            r["new_ckvT"].reshape(KV_RANK, P).T[None, None], r["new_kpe"][None, None])
```
